# Optimizing a Trainium2 kernel written in Bass

```python
import jax, jax.numpy as jnp
from jax import lax
import numpy as np
import math

D_MODEL = 1024
BATCH = 1
SEQ = 512
DEPTH = 1

EPS = 1e-6
NEG_INF = -1e30
FORCE_SCORE = 1e4
N_BRANCH = 3

GMLP_WIDTH = 1024
GMLP_GROUPS = 4
GMLP_GROUP_DIM = GMLP_WIDTH // GMLP_GROUPS
GMLP_CHUNK = 128

NSA_HEADS = 16
NSA_KV_GROUPS = 4
NSA_HEAD_DIM = 64
NSA_HPG = NSA_HEADS // NSA_KV_GROUPS
NSA_Q_WIDTH = NSA_HEADS * NSA_HEAD_DIM
NSA_KV_WIDTH = NSA_KV_GROUPS * NSA_HEAD_DIM
CMP_BLOCK = 32
CMP_STRIDE = 16
CMP_HIDDEN = 256
SEL_BLOCK = 64
SEL_TOP_N = 16
WINDOW = 512
NSA_Q_CHUNK = 64

RNN_WIDTH = 1024
RNN_HEADS = 16
RNN_HEAD_DIM = RNN_WIDTH // RNN_HEADS
CONV_WIDTH = 4
LRU_C = 8.0

D_FF = -(-8 * D_MODEL // (3 * 256)) * 256

IN_SPLITS = (GMLP_WIDTH, GMLP_WIDTH, NSA_Q_WIDTH, 6 * NSA_KV_WIDTH, N_BRANCH * NSA_HEADS, RNN_WIDTH, RNN_WIDTH, N_BRANCH * D_MODEL)
D_IN = sum(IN_SPLITS)


def rms_norm(x, g):
    xf = x.astype(jnp.float32)
    y = xf * lax.rsqrt(jnp.mean(xf * xf, axis=-1, keepdims=True) + EPS)
    return (y * g.astype(jnp.float32)).astype(x.dtype)

def layer_norm(x, g, b):
    xf = x.astype(jnp.float32)
    mu = jnp.mean(xf, axis=-1, keepdims=True)
    var = jnp.mean(jnp.square(xf - mu), axis=-1, keepdims=True)
    y = (xf - mu) * lax.rsqrt(var + EPS) * g.astype(jnp.float32) + b.astype(jnp.float32)
    return y.astype(x.dtype)

def gmlp_mixer(u, v, ln_g, ln_b, w_s, b_s):
    B, S, _ = u.shape
    n_chunks = S // GMLP_CHUNK
    vn = layer_norm(v, ln_g, ln_b).reshape(B, n_chunks, GMLP_CHUNK, GMLP_GROUPS, GMLP_GROUP_DIM)
    causal = jnp.tril(jnp.ones((GMLP_CHUNK, GMLP_CHUNK), w_s.dtype))
    w = w_s * causal
    mixed = jnp.einsum('gts,bnsgd->bntgd', w, vn) + b_s.T[None, None, :, :, None]
    return u * mixed.reshape(B, S, GMLP_WIDTH)

def nsa_mixer(q, k_cmp, v_cmp, k_slc, v_slc, k_win, v_win, branch_gates,
              pe_k, pe_v, wk1, wk2, wv1, wv2):
    B, S, _ = q.shape
    G, HP, DH = NSA_KV_GROUPS, NSA_HPG, NSA_HEAD_DIM
    scale = DH ** -0.5
    qh = q.reshape(B, S, G, HP, DH).transpose(0, 2, 3, 1, 4)

    def kv_heads(t):
        return t.reshape(B, S, G, DH).transpose(0, 2, 1, 3)

    k_cmp, v_cmp, k_slc, v_slc, k_win, v_win = map(kv_heads, (k_cmp, v_cmp, k_slc, v_slc, k_win, v_win))
    pos = jnp.arange(S)

    n_cmp = (S - CMP_BLOCK) // CMP_STRIDE + 1
    blk_idx = jnp.arange(n_cmp)[:, None] * CMP_STRIDE + jnp.arange(CMP_BLOCK)[None, :]

    def compress(t, pe, w1, w2):
        blocks = t[:, :, blk_idx] + pe
        flat = blocks.reshape(B, G, n_cmp, CMP_BLOCK * DH)
        return jax.nn.gelu(flat @ w1) @ w2

    kc = compress(k_cmp, pe_k, wk1, wk2)
    vc = compress(v_cmp, pe_v, wv1, wv2)
    cmp_end = jnp.arange(n_cmp) * CMP_STRIDE + CMP_BLOCK - 1
    valid_c = cmp_end[None, :] <= pos[:, None]
    s_c = jnp.einsum('bghsd,bgnd->bghsn', qh, kc).astype(jnp.float32) * scale
    s_c = jnp.where(valid_c, s_c, NEG_INF)
    p_c = jax.nn.softmax(s_c, axis=-1) * jnp.any(valid_c, axis=-1)[:, None].astype(jnp.float32)
    o_cmp = jnp.einsum('bghsn,bgnd->bghsd', p_c.astype(vc.dtype), vc)

    n_sel = S // SEL_BLOCK
    c_start = np.arange(n_cmp) * CMP_STRIDE
    s_start = np.arange(n_sel) * SEL_BLOCK
    overlap = np.clip(np.minimum(c_start[:, None] + CMP_BLOCK, s_start[None, :] + SEL_BLOCK)
                      - np.maximum(c_start[:, None], s_start[None, :]), 0, None) / CMP_BLOCK
    overlap = jnp.asarray(overlap, jnp.float32)
    imp = jnp.einsum('bghsn,nj->bgsj', p_c, overlap)
    cur = (pos // SEL_BLOCK)[:, None]
    j = jnp.arange(n_sel)[None, :]
    forced = (j == 0) | (j == cur) | (j == cur - 1)
    imp = jnp.where(forced, FORCE_SCORE, jnp.where(j > cur, NEG_INF, imp))
    top_n = min(SEL_TOP_N, n_sel)
    _, sel_idx = lax.top_k(imp, top_n)

    k_sb = k_slc.reshape(B, G, n_sel, SEL_BLOCK, DH)
    v_sb = v_slc.reshape(B, G, n_sel, SEL_BLOCK, DH)
    pad = jnp.zeros((B, G, WINDOW, DH), k_win.dtype)
    k_wp = jnp.concatenate([pad, k_win], axis=2)
    v_wp = jnp.concatenate([pad, v_win], axis=2)
    gather = jax.vmap(jax.vmap(lambda blocks, ix: blocks[ix]))

    C = NSA_Q_CHUNK
    n_chunks = S // C
    q_ch = jnp.moveaxis(qh.reshape(B, G, HP, n_chunks, C, DH), 3, 0)
    idx_ch = jnp.moveaxis(sel_idx.reshape(B, G, n_chunks, C, top_n), 2, 0)

    def chunk_fn(args):
        c, qc, ic = args
        t = c * C + jnp.arange(C)
        kg = gather(k_sb, ic)
        vg = gather(v_sb, ic)
        kpos = ic[..., None] * SEL_BLOCK + jnp.arange(SEL_BLOCK)
        s = jnp.einsum('bghcd,bgckld->bghckl', qc, kg).astype(jnp.float32) * scale
        s = jnp.where((kpos <= t[:, None, None])[:, :, None], s, NEG_INF)
        p = jax.nn.softmax(s.reshape(B, G, HP, C, top_n * SEL_BLOCK), axis=-1).reshape(s.shape)
        o_s = jnp.einsum('bghckl,bgckld->bghcd', p.astype(vg.dtype), vg)
        kw = lax.dynamic_slice_in_dim(k_wp, c * C, WINDOW + C, axis=2)
        vw = lax.dynamic_slice_in_dim(v_wp, c * C, WINDOW + C, axis=2)
        wpos = c * C - WINDOW + jnp.arange(WINDOW + C)
        wmask = (wpos[None, :] >= 0) & (wpos[None, :] <= t[:, None]) & (wpos[None, :] > t[:, None] - WINDOW)
        sw = jnp.einsum('bghcd,bgkd->bghck', qc, kw).astype(jnp.float32) * scale
        sw = jnp.where(wmask, sw, NEG_INF)
        o_w = jnp.einsum('bghck,bgkd->bghcd', jax.nn.softmax(sw, axis=-1).astype(vw.dtype), vw)
        return o_s, o_w

    o_slc, o_win = lax.map(chunk_fn, (jnp.arange(n_chunks), q_ch, idx_ch))
    o_slc = jnp.moveaxis(o_slc, 0, 3).reshape(B, G, HP, S, DH)
    o_win = jnp.moveaxis(o_win, 0, 3).reshape(B, G, HP, S, DH)

    g = jax.nn.sigmoid(branch_gates).reshape(B, S, G, HP, N_BRANCH).transpose(0, 2, 3, 1, 4)
    o = g[..., 0:1] * o_cmp + g[..., 1:2] * o_slc + g[..., 2:3] * o_win
    return o.transpose(0, 3, 1, 2, 4).reshape(B, S, NSA_Q_WIDTH)

def rglru_mixer(xr, gate, conv_w, conv_b, w_a, b_a, w_x, b_x, lam):
    B, S, _ = xr.shape
    xc = lax.conv_general_dilated(xr, conv_w[:, None, :], window_strides=(1,),
                                  padding=[(CONV_WIDTH - 1, 0)],
                                  dimension_numbers=('NWC', 'WIO', 'NWC'),
                                  feature_group_count=RNN_WIDTH) + conv_b
    xh = xc.reshape(B, S, RNN_HEADS, RNN_HEAD_DIM)
    r = jax.nn.sigmoid(jnp.einsum('bshi,hio->bsho', xh, w_a).reshape(B, S, RNN_WIDTH) + b_a)
    i = jax.nn.sigmoid(jnp.einsum('bshi,hio->bsho', xh, w_x).reshape(B, S, RNN_WIDTH) + b_x)
    log_a = -LRU_C * r.astype(jnp.float32) * jax.nn.softplus(-lam.astype(jnp.float32))
    a = jnp.exp(log_a)
    b_in = jnp.sqrt(-jnp.expm1(2.0 * log_a)) * (i * xc).astype(jnp.float32)

    def combine(left, right):
        a1, b1 = left
        a2, b2 = right
        return a2 * a1, a2 * b1 + b2

    _, h = lax.associative_scan(combine, (a, b_in), axis=1)
    return h.astype(xr.dtype) * jax.nn.gelu(gate)

def hybrid_layer(x, g_pre_mix, g_post_mix, g_pre_ffn, g_post_ffn, w_in,
                 gmlp_ln_g, gmlp_ln_b, gmlp_ws, gmlp_bs,
                 nsa_pe_k, nsa_pe_v, nsa_wk1, nsa_wk2, nsa_wv1, nsa_wv2,
                 rnn_conv_w, rnn_conv_b, rnn_wa, rnn_ba, rnn_wx, rnn_bx, rnn_lam,
                 w_br_a, w_br_b, w_br_c, w_o, w_ffn_in, w_ffn_out):
    B, S, _ = x.shape
    h = rms_norm(x, g_pre_mix)
    z = h @ w_in
    split_points = [int(p) for p in np.cumsum(IN_SPLITS)[:-1]]
    u, v, q, kv, nsa_g, xr, rg, mg = jnp.split(z, split_points, axis=-1)
    k_cmp, v_cmp, k_slc, v_slc, k_win, v_win = jnp.split(kv, 6, axis=-1)

    y_a = gmlp_mixer(jax.nn.gelu(u), jax.nn.gelu(v), gmlp_ln_g, gmlp_ln_b, gmlp_ws, gmlp_bs)
    y_b = nsa_mixer(q, k_cmp, v_cmp, k_slc, v_slc, k_win, v_win, nsa_g,
                    nsa_pe_k, nsa_pe_v, nsa_wk1, nsa_wk2, nsa_wv1, nsa_wv2)
    y_c = rglru_mixer(xr, rg, rnn_conv_w, rnn_conv_b, rnn_wa, rnn_ba, rnn_wx, rnn_bx, rnn_lam)

    gates = jax.nn.sigmoid(mg).reshape(B, S, N_BRANCH, D_MODEL)
    merged = (gates[:, :, 0] * (y_a @ w_br_a)
              + gates[:, :, 1] * (y_b @ w_br_b)
              + gates[:, :, 2] * (y_c @ w_br_c))
    x = x + rms_norm(merged @ w_o, g_post_mix)

    hf = rms_norm(x, g_pre_ffn)
    f_gate, f_up = jnp.split(hf @ w_ffn_in, 2, axis=-1)
    f = (jax.nn.silu(f_gate) * f_up) @ w_ffn_out
    return x + rms_norm(f, g_post_ffn)

def first_inputs(seed: int = 0) -> dict:
    key = jax.random.key(seed)
    keys = iter(jax.random.split(key, 48))
    L = DEPTH

    def nrm(shape, scale):
        return jax.random.normal(next(keys), shape, jnp.float32) * scale

    def gain(n):
        return 1.0 + nrm((L, n), 0.05)

    u_lam = jax.random.uniform(next(keys), (L, RNN_WIDTH), jnp.float32, minval=0.9, maxval=0.999)
    a0 = u_lam ** (1.0 / LRU_C)
    rnn_lam = jnp.log(a0) - jnp.log1p(-a0)

    return {
        "x": nrm((BATCH, SEQ, D_MODEL), 1.0),
        "g_pre_mix": gain(D_MODEL),
        "g_post_mix": gain(D_MODEL),
        "g_pre_ffn": gain(D_MODEL),
        "g_post_ffn": gain(D_MODEL),
        "w_in": nrm((L, D_MODEL, D_IN), D_MODEL ** -0.5),
        "gmlp_ln_g": gain(GMLP_WIDTH),
        "gmlp_ln_b": nrm((L, GMLP_WIDTH), 0.05),
        "gmlp_ws": nrm((L, GMLP_GROUPS, GMLP_CHUNK, GMLP_CHUNK), GMLP_CHUNK ** -0.5),
        "gmlp_bs": 1.0 + nrm((L, GMLP_GROUPS, GMLP_CHUNK), 0.1),
        "nsa_pe_k": nrm((L, CMP_BLOCK, NSA_HEAD_DIM), 0.1),
        "nsa_pe_v": nrm((L, CMP_BLOCK, NSA_HEAD_DIM), 0.1),
        "nsa_wk1": nrm((L, CMP_BLOCK * NSA_HEAD_DIM, CMP_HIDDEN), (CMP_BLOCK * NSA_HEAD_DIM) ** -0.5),
        "nsa_wk2": nrm((L, CMP_HIDDEN, NSA_HEAD_DIM), CMP_HIDDEN ** -0.5),
        "nsa_wv1": nrm((L, CMP_BLOCK * NSA_HEAD_DIM, CMP_HIDDEN), (CMP_BLOCK * NSA_HEAD_DIM) ** -0.5),
        "nsa_wv2": nrm((L, CMP_HIDDEN, NSA_HEAD_DIM), CMP_HIDDEN ** -0.5),
        "rnn_conv_w": nrm((L, CONV_WIDTH, RNN_WIDTH), CONV_WIDTH ** -0.5),
        "rnn_conv_b": nrm((L, RNN_WIDTH), 0.05),
        "rnn_wa": nrm((L, RNN_HEADS, RNN_HEAD_DIM, RNN_HEAD_DIM), RNN_HEAD_DIM ** -0.5),
        "rnn_ba": nrm((L, RNN_WIDTH), 0.1),
        "rnn_wx": nrm((L, RNN_HEADS, RNN_HEAD_DIM, RNN_HEAD_DIM), RNN_HEAD_DIM ** -0.5),
        "rnn_bx": nrm((L, RNN_WIDTH), 0.1),
        "rnn_lam": rnn_lam,
        "w_br_a": nrm((L, GMLP_WIDTH, D_MODEL), GMLP_WIDTH ** -0.5),
        "w_br_b": nrm((L, NSA_Q_WIDTH, D_MODEL), NSA_Q_WIDTH ** -0.5),
        "w_br_c": nrm((L, RNN_WIDTH, D_MODEL), RNN_WIDTH ** -0.5),
        "w_o": nrm((L, D_MODEL, D_MODEL), D_MODEL ** -0.5),
        "w_ffn_in": nrm((L, D_MODEL, 2 * D_FF), D_MODEL ** -0.5),
        "w_ffn_out": nrm((L, D_FF, D_MODEL), D_FF ** -0.5),
    }

def first_block(x, g_pre_mix, g_post_mix, g_pre_ffn, g_post_ffn, w_in,
              gmlp_ln_g, gmlp_ln_b, gmlp_ws, gmlp_bs,
              nsa_pe_k, nsa_pe_v, nsa_wk1, nsa_wk2, nsa_wv1, nsa_wv2,
              rnn_conv_w, rnn_conv_b, rnn_wa, rnn_ba, rnn_wx, rnn_bx, rnn_lam,
              w_br_a, w_br_b, w_br_c, w_o, w_ffn_in, w_ffn_out):
    for l in range(DEPTH):
        x = hybrid_layer(x, g_pre_mix[l], g_post_mix[l], g_pre_ffn[l], g_post_ffn[l], w_in[l],
                         gmlp_ln_g[l], gmlp_ln_b[l], gmlp_ws[l], gmlp_bs[l],
                         nsa_pe_k[l], nsa_pe_v[l], nsa_wk1[l], nsa_wk2[l], nsa_wv1[l], nsa_wv2[l],
                         rnn_conv_w[l], rnn_conv_b[l], rnn_wa[l], rnn_ba[l], rnn_wx[l], rnn_bx[l], rnn_lam[l],
                         w_br_a[l], w_br_b[l], w_br_c[l], w_o[l], w_ffn_in[l], w_ffn_out[l])
    return x


DEPTH_2 = 2

HEAD_DIM = 64
N_HEADS_A = 8
N_HEADS_B = 8
N_KV_HEADS_B = 2
DILATED_BRANCHES = ((128, 1), (512, 4), (2048, 16))
WINDOW_B = 128
REL_BUCKETS = 32
REL_MAX_DIST = 1024
N_REL_HEADS = N_HEADS_A + N_HEADS_B
D_ATTN_IN = (3 * N_HEADS_A + N_HEADS_B + 2 * N_KV_HEADS_B) * HEAD_DIM
D_ATTN_OUT = (N_HEADS_A + N_HEADS_B) * HEAD_DIM
RWKV_HEAD = 64
RWKV_HEADS = D_MODEL // RWKV_HEAD
DECAY_LORA = 64
AAA_LORA = 64
GATE_LORA = 128
D_FF_2 = 4 * D_MODEL
N_ATTN_LAYERS = (DEPTH_2 + 1) // 2
N_RWKV_LAYERS = DEPTH_2 // 2
NORM_EPS = 1e-6
GN_EPS = 64e-5
NEG_INF_2 = -1e30


F32 = jnp.float32

def rms_norm_2(x, g):
    x32 = x.astype(F32)
    y = x32 * lax.rsqrt(jnp.mean(x32 * x32, axis=-1, keepdims=True) + NORM_EPS)
    return (y * g.astype(F32)).astype(x.dtype)

def t5_bucket(rel):
    nb = REL_BUCKETS // 2
    max_exact = nb // 2
    bucket = jnp.where(rel > 0, nb, 0)
    n = jnp.abs(rel)
    nf = jnp.maximum(n, 1).astype(F32)
    large = max_exact + (jnp.log(nf / max_exact) / math.log(REL_MAX_DIST / max_exact)
                         * (nb - max_exact)).astype(jnp.int32)
    large = jnp.minimum(large, nb - 1)
    return bucket + jnp.where(n < max_exact, n, large)

def band_rel_bias(table_h, block, dilation):
    i = jnp.arange(block)[:, None]
    j = jnp.arange(3 * block)[None, :]
    bucket = t5_bucket((j - block - i) * dilation)
    return jnp.transpose(table_h[bucket], (2, 0, 1))

def banded_attention(q, k, v, bias, radius, block, sink=None):
    nB, H, G, L, hd = q.shape
    nb = -(-L // block)
    pad = nb * block - L
    qb = jnp.pad(q, [(0, 0)] * 3 + [(0, pad), (0, 0)]).reshape(nB, H, G, nb, block, hd)

    def windows(t):
        tb = jnp.pad(t, [(0, 0)] * 3 + [(block, block + pad), (0, 0)]).reshape(nB, H, G, nb + 2, block, hd)
        return jnp.concatenate([tb[:, :, :, :-2], tb[:, :, :, 1:-1], tb[:, :, :, 2:]], axis=-2)

    kb, vb = windows(k), windows(v)
    valid = jnp.pad(jnp.ones((L,), bool), (block, block + pad)).reshape(nb + 2, block)
    valid = jnp.concatenate([valid[:-2], valid[1:-1], valid[2:]], axis=-1)
    rel = jnp.arange(3 * block)[None, :] - block - jnp.arange(block)[:, None]
    mask = (jnp.abs(rel) <= radius)[None] & valid[:, None, :]
    s = jnp.einsum('bhgnqd,bhgnkd->bhgnqk', qb, kb).astype(F32) * (hd ** -0.5)
    s = s + bias.astype(F32)[None, :, None, None]
    s = jnp.where(mask, s, NEG_INF_2)
    m = jnp.max(s, axis=-1)
    if sink is not None:
        sink_b = sink.astype(F32)[None, :, None, None, None]
        m = jnp.maximum(m, sink_b)
    p = jnp.exp(s - m[..., None])
    denom = jnp.sum(p, axis=-1)
    if sink is not None:
        denom = denom + jnp.exp(sink_b - m)
    o = jnp.einsum('bhgnqk,bhgnkd->bhgnqd', p, vb.astype(F32)) / denom[..., None]
    lse = m + jnp.log(denom)
    o = o.reshape(nB, H, G, nb * block, hd)[..., :L, :]
    lse = lse.reshape(nB, H, G, nb * block)[..., :L]
    return o, lse

def dilated_attention(q, k, v, table_a):
    nB, H, S, hd = q.shape
    outs, lses = [], []
    for window, dil in DILATED_BRANCHES:
        radius = window // 2 // dil

        def split(t):
            return t.reshape(nB, H, S // dil, dil, hd).transpose(0, 1, 3, 2, 4)

        bias = band_rel_bias(table_a, radius, dil)
        o, lse = banded_attention(split(q), split(k), split(v), bias, radius, radius)
        outs.append(o.transpose(0, 1, 3, 2, 4).reshape(nB, H, S, hd))
        lses.append(lse.transpose(0, 1, 3, 2).reshape(nB, H, S))
    wts = jax.nn.softmax(jnp.stack(lses), axis=0)
    return jnp.einsum('rbhs,rbhsd->bhsd', wts, jnp.stack(outs))

def window_gqa(q, k, v, sink, table_b):
    rep = N_HEADS_B // N_KV_HEADS_B
    k = jnp.repeat(k, rep, axis=1)
    v = jnp.repeat(v, rep, axis=1)
    bias = band_rel_bias(table_b, WINDOW_B, 1)
    o, _ = banded_attention(q[:, :, None], k[:, :, None], v[:, :, None], bias, WINDOW_B, WINDOW_B, sink)
    return o[:, :, 0]

def attention_mixer(h, w_in, sink, w_out, rel_table):
    nB, S, _ = h.shape
    proj = h @ w_in
    sizes = [N_HEADS_A * HEAD_DIM] * 3 + [N_HEADS_B * HEAD_DIM, N_KV_HEADS_B * HEAD_DIM, N_KV_HEADS_B * HEAD_DIM]
    cuts = [int(c) for c in np.cumsum(sizes)[:-1]]
    qa, ka, va, qb, kb, vb = jnp.split(proj, cuts, axis=-1)

    def heads(t):
        return t.reshape(nB, S, -1, HEAD_DIM).transpose(0, 2, 1, 3)

    oa = dilated_attention(heads(qa), heads(ka), heads(va), rel_table[:, :N_HEADS_A])
    ob = window_gqa(heads(qb), heads(kb), heads(vb), sink, rel_table[:, N_HEADS_A:])
    o = jnp.concatenate([oa, ob], axis=1).astype(h.dtype)
    o = o.transpose(0, 2, 1, 3).reshape(nB, S, D_ATTN_OUT)
    return o @ w_out

def rwkv7_scan(r, w, k, v, kk, a):
    def step(state, inp):
        r_t, w_t, k_t, v_t, kk_t, a_t = inp
        sa = jnp.einsum('bhvk,bhk->bhv', state, -kk_t)
        state = (state * w_t[:, :, None, :] + sa[..., None] * (kk_t * a_t)[:, :, None, :]
                 + v_t[..., None] * k_t[:, :, None, :])
        return state, jnp.einsum('bhvk,bhk->bhv', state, r_t)

    nB, S, H, N = r.shape
    xs = tuple(jnp.moveaxis(t, 1, 0) for t in (r, w, k, v, kk, a))
    _, out = lax.scan(step, jnp.zeros((nB, H, N, N), F32), xs)
    return jnp.moveaxis(out, 0, 1)

def group_norm(o, gn_w, gn_b):
    mu = jnp.mean(o, axis=-1, keepdims=True)
    var = jnp.mean(jnp.square(o - mu), axis=-1, keepdims=True)
    y = (o - mu) * lax.rsqrt(var + GN_EPS)
    nB, S, H, N = o.shape
    return y.reshape(nB, S, H * N) * gn_w.astype(F32) + gn_b.astype(F32)

def rwkv7_mixer(h, mu_prev, mu_next, w_r, w_k, w_v, w_o, k_k, k_a, r_k, gn_w, gn_b,
                w0, w1, w2, a0, a1, a2, g1, g2):
    nB, S, D = h.shape
    H, N = RWKV_HEADS, RWKV_HEAD
    dx_p = jnp.pad(h, ((0, 0), (1, 0), (0, 0)))[:, :-1] - h
    dx_n = jnp.pad(h, ((0, 0), (0, 1), (0, 0)))[:, 1:] - h

    def mix(c):
        return h + dx_p * mu_prev[c] + dx_n * mu_next[c]

    def heads(t):
        return t.astype(F32).reshape(nB, S, H, N)

    xw, xa, xg = mix(1), mix(4), mix(5)
    r = mix(0) @ w_r
    k = mix(2) @ w_k
    v = mix(3) @ w_v
    kk = heads(k * k_k)
    kk = kk / jnp.maximum(jnp.sqrt(jnp.sum(kk * kk, axis=-1, keepdims=True)), 1e-12)
    rh, vh = heads(r), heads(v)
    dir_out = []
    for d in range(2):
        w_log = -jax.nn.softplus(-(w0[d] + jnp.tanh(xw @ w1[d]) @ w2[d])) - 0.5
        decay = jnp.exp(-jnp.exp(w_log.astype(F32)))
        a = jax.nn.sigmoid(a0[d] + (xa @ a1[d]) @ a2[d])
        g = jax.nn.sigmoid(xg @ g1[d]) @ g2[d]
        kd = heads(k * (1 + (a - 1) * k_a))
        ins = [rh, heads(decay), kd, vh, kk, heads(a)]
        if d == 1:
            ins = [jnp.flip(t, axis=1) for t in ins]
        o = rwkv7_scan(*ins)
        if d == 1:
            o = jnp.flip(o, axis=1)
        bonus = jnp.sum(rh * kd * r_k.astype(F32), axis=-1, keepdims=True) * vh
        dir_out.append((group_norm(o, gn_w, gn_b) + bonus.reshape(nB, S, D)) * g.astype(F32))
    y = dir_out[0] + dir_out[1]
    return y.astype(h.dtype) @ w_o

def second_inputs(seed: int = 0) -> dict:
    key = jax.random.key(seed)
    ks = iter(jax.random.split(key, 40))

    def nrm(shape, scale):
        return scale * jax.random.normal(next(ks), shape, F32)

    NA, NR, D = N_ATTN_LAYERS, N_RWKV_LAYERS, D_MODEL
    return {
        'x': nrm((BATCH, SEQ, D), 1.0),
        'rel_table': nrm((REL_BUCKETS, N_REL_HEADS), 0.5),
        'norm_g': 1.0 + nrm((DEPTH_2, 4, D), 0.05),
        'attn_w_in': nrm((NA, D, D_ATTN_IN), D ** -0.5),
        'attn_sink': nrm((NA, N_HEADS_B), 0.5),
        'attn_w_out': nrm((NA, D_ATTN_OUT, D), D_ATTN_OUT ** -0.5),
        'rk_mu_prev': jax.random.uniform(next(ks), (NR, 6, D), F32, 0.0, 0.5),
        'rk_mu_next': jax.random.uniform(next(ks), (NR, 6, D), F32, 0.0, 0.5),
        'rk_w_r': nrm((NR, D, D), D ** -0.5),
        'rk_w_k': nrm((NR, D, D), D ** -0.5),
        'rk_w_v': nrm((NR, D, D), D ** -0.5),
        'rk_w_o': nrm((NR, D, D), D ** -0.5),
        'rk_k_k': 0.85 + nrm((NR, D), 0.05),
        'rk_k_a': 1.0 + nrm((NR, D), 0.05),
        'rk_r_k': nrm((NR, RWKV_HEADS, RWKV_HEAD), 0.1),
        'rk_gn_w': 1.0 + nrm((NR, D), 0.05),
        'rk_gn_b': nrm((NR, D), 0.02),
        'rk_w0': -2.0 + nrm((NR, 2, D), 1.0),
        'rk_w1': nrm((NR, 2, D, DECAY_LORA), D ** -0.5),
        'rk_w2': nrm((NR, 2, DECAY_LORA, D), 0.1 * DECAY_LORA ** -0.5),
        'rk_a0': nrm((NR, 2, D), 0.5),
        'rk_a1': nrm((NR, 2, D, AAA_LORA), D ** -0.5),
        'rk_a2': nrm((NR, 2, AAA_LORA, D), 0.5 * AAA_LORA ** -0.5),
        'rk_g1': nrm((NR, 2, D, GATE_LORA), D ** -0.5),
        'rk_g2': nrm((NR, 2, GATE_LORA, D), GATE_LORA ** -0.5),
        'mlp_w1': nrm((DEPTH_2, D, D_FF_2), D ** -0.5),
        'mlp_w2': nrm((DEPTH_2, D_FF_2, D), D_FF_2 ** -0.5),
    }

def second_block(x, rel_table, norm_g, attn_w_in, attn_sink, attn_w_out,
              rk_mu_prev, rk_mu_next, rk_w_r, rk_w_k, rk_w_v, rk_w_o, rk_k_k, rk_k_a, rk_r_k,
              rk_gn_w, rk_gn_b, rk_w0, rk_w1, rk_w2, rk_a0, rk_a1, rk_a2, rk_g1, rk_g2,
              mlp_w1, mlp_w2):
    h = x
    for layer in range(DEPTH_2):
        g = norm_g[layer]
        i = layer // 2
        u = rms_norm_2(h, g[0])
        if layer % 2 == 0:
            u = attention_mixer(u, attn_w_in[i], attn_sink[i], attn_w_out[i], rel_table)
        else:
            u = rwkv7_mixer(u, rk_mu_prev[i], rk_mu_next[i], rk_w_r[i], rk_w_k[i], rk_w_v[i], rk_w_o[i],
                            rk_k_k[i], rk_k_a[i], rk_r_k[i], rk_gn_w[i], rk_gn_b[i],
                            rk_w0[i], rk_w1[i], rk_w2[i], rk_a0[i], rk_a1[i], rk_a2[i], rk_g1[i], rk_g2[i])
        h = h + rms_norm_2(u, g[1])
        u = rms_norm_2(h, g[2])
        u = jnp.square(jax.nn.relu(u @ mlp_w1[layer])) @ mlp_w2[layer]
        h = h + rms_norm_2(u, g[3])
    return h


def setup_inputs(seed=0):
    out = dict(first_inputs(seed))
    for name, value in second_inputs(seed + 1).items():
        if name != "x":
            out[name + "_2"] = value
    return out


def reference(
    x, g_pre_mix, g_post_mix, g_pre_ffn, g_post_ffn, w_in, gmlp_ln_g, gmlp_ln_b, gmlp_ws,
    gmlp_bs, nsa_pe_k, nsa_pe_v, nsa_wk1, nsa_wk2, nsa_wv1, nsa_wv2, rnn_conv_w, rnn_conv_b,
    rnn_wa, rnn_ba, rnn_wx, rnn_bx, rnn_lam, w_br_a, w_br_b, w_br_c, w_o, w_ffn_in, w_ffn_out,
    rel_table_2, norm_g_2, attn_w_in_2, attn_sink_2, attn_w_out_2, rk_mu_prev_2, rk_mu_next_2,
    rk_w_r_2, rk_w_k_2, rk_w_v_2, rk_w_o_2, rk_k_k_2, rk_k_a_2, rk_r_k_2, rk_gn_w_2, rk_gn_b_2,
    rk_w0_2, rk_w1_2, rk_w2_2, rk_a0_2, rk_a1_2, rk_a2_2, rk_g1_2, rk_g2_2, mlp_w1_2, mlp_w2_2,
):
    x = first_block(
        x, g_pre_mix, g_post_mix, g_pre_ffn, g_post_ffn, w_in, gmlp_ln_g, gmlp_ln_b, gmlp_ws,
        gmlp_bs, nsa_pe_k, nsa_pe_v, nsa_wk1, nsa_wk2, nsa_wv1, nsa_wv2, rnn_conv_w, rnn_conv_b,
        rnn_wa, rnn_ba, rnn_wx, rnn_bx, rnn_lam, w_br_a, w_br_b, w_br_c, w_o, w_ffn_in,
        w_ffn_out,
    )
    return second_block(
        x, rel_table_2, norm_g_2, attn_w_in_2, attn_sink_2, attn_w_out_2, rk_mu_prev_2,
        rk_mu_next_2, rk_w_r_2, rk_w_k_2, rk_w_v_2, rk_w_o_2, rk_k_k_2, rk_k_a_2, rk_r_k_2,
        rk_gn_w_2, rk_gn_b_2, rk_w0_2, rk_w1_2, rk_w2_2, rk_a0_2, rk_a1_2, rk_a2_2, rk_g1_2,
        rk_g2_2, mlp_w1_2, mlp_w2_2,
    )


_drawn_inputs = setup_inputs


def setup_inputs(seed=0):
    import zlib

    import numpy as np

    out = dict(_drawn_inputs(seed))
    spreads = {}
    factors = {'gmlp_ln_b': 2.707,
     'nsa_pe_k': 8.0,
     'rnn_ba': 4.947,
     'rnn_bx': 3.595,
     'attn_sink_2': 8.0,
     'rk_gn_w_2': 2.744,
     'rk_gn_b_2': 6.57,
     'rk_w1_2': 6.127,
     'rk_w2_2': 5.954}
    for name, (base, spread) in spreads.items():
        noise = np.random.default_rng([zlib.crc32(name.encode()), seed]).standard_normal(out[name].shape)
        drawn = base * np.exp(spread * noise) if base else spread * noise
        out[name] = __import__('jax').numpy.asarray(drawn.astype(out[name].dtype))
    for name, factor in factors.items():
        out[name] = (out[name] * factor).astype(out[name].dtype)
    return out
```

```python
import math
from contextlib import ExitStack

import numpy as np

import concourse.bass as bass
from concourse import mybir

F32 = mybir.dt.float32
ALU = mybir.AluOpType
ACT = mybir.ActivationFunctionType
AX = mybir.AxisListType
P = 128
S = 512
D = 1024
NB = D // P
QT = S // P
PIECE = 2048
RING = 4
NEG = -1e30
EPS = 1e-6
GN_EPS = 64e-5
DFF = 2816
NFF = DFF // P
MLP = 4096
NMLP = MLP // P
NH = 16
NCMP = 31
CH = 64
NCH = S // CH
LEVELS = (2, 4, 8, 16, 32)
DECAY = math.exp(-0.5)
ROT = 6

STREAM = [("w_v", 8192), ("w_u", 8192), ("w_q", 8192), ("w_kv", 8192), ("w_vt", 4096),
          ("wk1", 4096), ("wv1", 4096), ("w_xr", 8192), ("w_rg", 8192)]
STREAM += [(f"w_mb{nb}", 6 * 1024) for nb in range(NB)]
STREAM += [("w_o", 8192), ("w_fi", 2 * NFF * 1024), ("w_fo", NFF * 1024)]
STREAM += [("w_a2", 14 * 1024), ("w_va", 4096), ("w_ao", 8192), ("w_m10", NMLP * 1024), ("w_m20", NMLP * 1024)]
STREAM += [("w_rw", 1024), ("w_ra", 1024), ("w_rg1", 2048), ("w_rr", 8192), ("w_rk", 8192), ("w_rv", 8192),
           ("w_ro", 8192), ("w_m11", NMLP * 1024), ("w_m21", NMLP * 1024)]

VECS = [("g_pre_mix", 8), ("g_post_mix", 8), ("g_pre_ffn", 8), ("g_post_ffn", 8), ("conv_w", 32), ("conv_b", 8),
        ("rnn_ba", 8), ("rnn_bx", 8), ("rnn_lam", 8), ("pe_k", 16), ("pe_v", 16), ("norm_g", 64),
        ("mu_prev", 48), ("mu_next", 48), ("k_k", 8), ("k_a", 8), ("r_k", 8), ("gn_w", 8), ("gn_b", 8),
        ("w0", 16), ("a0", 16)]
NVEC = sum(n for _, n in VECS)


class Engine:

    def __init__(self, sem):
        self.sem, self.count, self.queue, self.met = sem, 0, [], {}

    def wait(self, *tokens):
        for t in tokens:
            if t is None:
                continue
            if isinstance(t, list):
                self.wait(*t)
            elif self.met.get(id(t[0]), 0) < t[1]:
                self.met[id(t[0])] = t[1]
                self.queue.append(lambda e, t=t: e.wait_ge(t[0], t[1]))

    def do(self, fn, *tokens):
        self.wait(*tokens)
        self.count += 1
        self.queue.append(lambda e: fn(e).then_inc(self.sem, 1))
        return (self.sem, self.count)

    def quiet(self, fn, *tokens):
        self.wait(*tokens)
        self.queue.append(fn)

    def dma(self, out, in_, sem, value, *tokens):
        self.wait(*tokens)
        self.queue.append(lambda e: e.dma_start(out, in_).then_inc(sem, 16))
        return (sem, value)

    def now(self):
        return (self.sem, self.count)


class Core:
    pass


def program(nc, I, out):
    with ExitStack() as ctx:
        names = iter(range(10 ** 6))

        def semaphore(name):
            return ctx.enter_context(nc.semaphore(f"{name}{next(names)}"))

        arena = ctx.enter_context(nc.sbuf_tensor("arena", [P, 51600], F32))
        psum = [ctx.enter_context(nc.psum_tensor(f"bank{i}", [P, 512], F32)) for i in range(8)]
        pe, act, dve, pool, sp = (Engine(semaphore(n)) for n in ("pe", "act", "dve", "pool", "sp"))
        top = [0]

        def alloc(n):
            a = arena[:, top[0]:top[0] + n]
            top[0] += n
            assert top[0] <= 51600, top[0]
            return a

        def alloc3(a, b):
            return alloc(a * b).rearrange("p (a b) -> p a b", b=b)

        def barrier():
            tokens = [e.now() for e in (pe, act, dve, pool)]
            for e in (pe, act, dve, pool):
                e.wait(tokens)

        def load(pairs, *tokens):
            s = semaphore("ld")
            for dst, src in pairs:
                pool.dma(dst, src, s, 0, *tokens)
            return (s, 16 * len(pairs))

        ring_t = alloc(RING * PIECE)
        slots = [ring_t[:, i * PIECE:(i + 1) * PIECE] for i in range(RING)]
        slot_sem = [semaphore("w") for _ in range(RING)]
        pieces = []
        for name, total in STREAM:
            for a in range(0, total, PIECE):
                pieces.append((name, a, min(PIECE, total - a)))
        state = {"issued": 0, "at": 0, "off": 0, "freed": 0}

        def issue(token):
            i = state["issued"]
            if i >= len(pieces):
                return
            name, a, n = pieces[i]
            sp.dma(slots[i % RING][:, 0:n], I[name][:, a:a + n], slot_sem[i % RING], 0, token)
            state["issued"] += 1

        def take(name, n):
            i = state["at"]
            assert pieces[i][0] == name and state["off"] + n <= pieces[i][2], (name, pieces[i])
            assert i < state["issued"], "the ring is too small"
            ap = slots[i % RING][:, state["off"]:state["off"] + n]
            token = (slot_sem[i % RING], 16 * (i // RING + 1))
            state["off"] += n
            if state["off"] == pieces[i][2]:
                state["at"] += 1
                state["off"] = 0
            return ap, token

        def release(token):
            while state["freed"] < state["at"]:
                issue(token)
                state["freed"] += 1

        for _ in range(RING):
            issue(None)

        bank_free = [None] * 8
        turn = [0]

        def bank():
            i = turn[0] % ROT
            turn[0] += 1
            return i, psum[i], bank_free[i]

        def mm(out_, lhsT, rhs, start, stop_, last, *tokens):
            if last:
                return pe.do(lambda e: e.matmul(out_, lhsT, rhs, start=start, stop=stop_, skip_group_check=True), *tokens)
            return pe.quiet(lambda e: e.matmul(out_, lhsT, rhs, start=start, stop=stop_, skip_group_check=True), *tokens)

        def tr(out_, in_, ident_, last, *tokens):
            if last:
                return pe.do(lambda e: e.transpose(out_, in_, ident_), *tokens)
            return pe.quiet(lambda e: e.transpose(out_, in_, ident_), *tokens)

        def gemm(name, nblocks, kt, rhs, rhs_token, evac):
            for nb in range(nblocks):
                i, ps, free = bank()
                for k in range(kt):
                    w, wt = take(name, P)
                    t = mm(ps[:, :], w, rhs(k), k == 0, k == kt - 1, k == kt - 1, free, wt, rhs_token)
                release(t)
                bank_free[i] = evac(nb, ps, t)

        vec_t = alloc(NVEC)
        vec, at = {}, 0
        for name, n in VECS:
            vec[name] = vec_t[:, at:at + n]
            at += n
        ident = alloc(P)
        tri = alloc(P)
        ones = alloc(P)
        bd = alloc(P)
        bdm = alloc(P)
        eps = alloc(4)
        c_tok = load([(vec_t, I["vecs"][:, :]), (ident, I["ident"][:, :]), (tri, I["tri"][:, :]), (bd, I["bd"][:, :])])
        k1 = pool.do(lambda e: e.memset(ones, 1.0 / D))
        k2 = pool.do(lambda e: e.memset(eps[:, 0:1], EPS))
        k2 = pool.do(lambda e: e.memset(eps[:, 1:2], GN_EPS))
        k3 = dve.do(lambda e: e.tensor_scalar(bdm, bd, 1.0 / CH, None, ALU.mult), c_tok)
        xT = alloc3(NB, S)
        x_tok = load([(xT, I["xT"].rearrange("(k p) t -> p k t", p=P))])
        base = top[0]
        for e in (pe, act, dve, pool):
            e.wait(c_tok, k1, k2, k3, x_tok)

        def rstd_of(src, dst, *tokens):
            mark = top[0]
            sq = [alloc(S) for _ in range(2)]
            used = [None, None]
            i, ps, free = bank()
            for k in range(NB):
                q = sq[k % 2]
                t = act.do(lambda e, q=q, k=k: e.activation(q, src[:, k, :], ACT.Square), used[k % 2], *tokens)
                used[k % 2] = m = mm(ps[:, :], ones, q, k == 0, k == NB - 1, True, free, t)
            a = act.do(lambda e: e.activation(dst, ps[:, :], ACT.Sqrt, bias=eps[:, 0:1]), m)
            bank_free[i] = a
            top[0] = mark
            return dve.do(lambda e: e.reciprocal(dst, dst), a)

        def normed(src, gain, dst, r, tok):
            for k in range(NB):
                t = dve.do(lambda e, k=k: e.scalar_tensor_tensor(dst[:, k, :], src[:, k, :], gain[:, k:k + 1], r,
                                                                 ALU.mult, ALU.mult), tok)
            return t

        def add_normed(src, gain, r, tok):
            for k in range(NB):
                t = dve.do(lambda e, k=k: e.scalar_tensor_tensor(src[:, k, :], src[:, k, :], gain[:, k:k + 1], r,
                                                                 ALU.mult, ALU.mult), tok)
                t = pool.do(lambda e, k=k: e.tensor_tensor(xT[:, k, :], xT[:, k, :], src[:, k, :], ALU.add), t)
            return t

        def copy(eng, dst, src, *tokens):
            if eng is act:
                return act.do(lambda e: e.activation(dst, src, ACT.Copy), *tokens)
            return eng.do(lambda e: e.tensor_copy(dst, src), *tokens)

        def turns(nb):
            return act if nb % 2 else dve

        def emit():
            with nc.Block() as block:
                for e, reg in ((sp, block.sync), (pool, block.gpsimd), (act, block.scalar),
                               (pe, block.tensor), (dve, block.vector)):
                    def body(eng, e=e):
                        for fn in e.queue:
                            fn(eng)
                    reg(body)

        T = Core()
        T.pe = pe
        T.act = act
        T.dve = dve
        T.pool = pool
        T.sp = sp
        T.vec = vec
        T.I = I
        T.alloc = alloc
        T.alloc3 = alloc3
        T.bank = bank
        T.mm = mm
        T.tr = tr
        T.gemm = gemm
        T.take = take
        T.release = release
        T.copy = copy
        T.psum = psum
        T.bank_free = bank_free
        T.xT = xT
        T.ident = ident
        T.top = top
        T.rstd_of = rstd_of
        T.normed = normed
        T.add_normed = add_normed
        T.load = load
        T.barrier = barrier
        T.state = state
        T.eps = eps
        T.tri = tri
        T.turns = turns
        T.base = base
        T.semaphore = semaphore
        T.bd = bd
        T.bdm = bdm
        T.ones = ones
        layer1(T)
        attention2(T)
        rwkv(T)
        t = [pe.now(), act.now(), dve.now(), pool.now()]
        s = semaphore("out")
        sp.dma(out.rearrange("(k p) t -> p k t", p=P), xT, s, 16, t)
        sp.wait((s, 16))
        assert state["at"] == len(pieces)
        emit()


def layer1(g):
    pe, act, dve, pool, vec, I = g.pe, g.act, g.dve, g.pool, g.vec, g.I
    alloc, alloc3, bank, mm, tr, gemm, take, release = g.alloc, g.alloc3, g.bank, g.mm, g.tr, g.gemm, g.take, g.release
    copy, psum, bank_free, xT, ident, top = g.copy, g.psum, g.bank_free, g.xT, g.ident, g.top

    yA, yB, yC = alloc3(NB, S), alloc3(NB, S), alloc3(NB, S)
    hT = alloc3(NB, S)
    r = alloc(S)
    work = top[0]
    t = g.rstd_of(xT, r)
    h_tok = g.normed(xT, vec["g_pre_mix"], hT, r, t)

    V = alloc3(QT, D)
    lng, lnb = alloc(D), alloc(D)
    wsT = alloc3(4, P)
    bsB = alloc3(4, P)
    sums = alloc(QT * 2)
    st = alloc(QT * 4).rearrange("p (a b) -> p a b", b=4)
    sqs = yA[:, 0:2, :].rearrange("p a b -> p (a b)")
    l_tok = g.load([(lng, I["ln_g"][0, :].partition_broadcast(P)), (lnb, I["ln_b"][0, :].partition_broadcast(P)),
                    (wsT, I["wsT"].rearrange("p (a b) -> p a b", b=P)), (bsB, I["bs"][0, :].partition_broadcast(P).rearrange("p (a b) -> p a b", b=P))])
    w_tok = pool.do(lambda e: e.affine_select(out=wsT, in_=wsT, compare_op=ALU.is_ge, fill=0.0, base=0,
                                              pattern=[[0, 4], [1, P]], channel_multiplier=-1), l_tok)
    for half in range(2):
        ws = [take("w_v", 512) for _ in range(NB)]
        for qt in range(QT):
            i, ps, free = bank()
            for k in range(NB):
                t = mm(ps[:, :], hT[:, k, qt * P:(qt + 1) * P], ws[k][0], k == 0, k == NB - 1, k == NB - 1,
                       free, ws[k][1], h_tok)
            bank_free[i] = act.do(lambda e, ps=ps, qt=qt, half=half: e.activation(
                V[:, qt, half * 512:half * 512 + 512], ps[:, :], ACT.Gelu_apprx_tanh,
                accum_out=sums[:, 2 * qt + half:2 * qt + half + 1]), t)
        release(t)
    v_tok = act.now()

    def ln(qt):
        a = dve.do(lambda e: e.tensor_tensor(st[:, qt, 0:1], sums[:, 2 * qt:2 * qt + 1], sums[:, 2 * qt + 1:2 * qt + 2], ALU.add), v_tok)
        a = dve.do(lambda e: e.tensor_scalar(st[:, qt, 0:1], st[:, qt, 0:1], 1.0 / D, None, ALU.mult), a)
        a = dve.do(lambda e: e.tensor_scalar(V[:, qt, :], V[:, qt, :], st[:, qt, 0:1], None, ALU.subtract), a)
        b = act.do(lambda e: e.activation(sqs, V[:, qt, :], ACT.Square, accum_out=st[:, qt, 1:2]), a)
        b = act.do(lambda e: e.activation(st[:, qt, 2:3], st[:, qt, 1:2], ACT.Sqrt, scale=1.0 / D, bias=g.eps[:, 0:1]), b)
        b = dve.do(lambda e: e.reciprocal(st[:, qt, 3:4], st[:, qt, 2:3]), b)
        b = dve.do(lambda e: e.scalar_tensor_tensor(V[:, qt, :], V[:, qt, :], st[:, qt, 3:4], lng, ALU.mult, ALU.mult), b, l_tok)
        return dve.do(lambda e: e.tensor_tensor(V[:, qt, :], V[:, qt, :], lnb, ALU.add), b)

    ln_tok = [ln(qt) for qt in range(QT)]
    uT = alloc3(NB, S)
    gemm("w_u", NB, NB, lambda k: hT[:, k, :], h_tok,
         lambda nb, ps, t: act.do(lambda e: e.activation(uT[:, nb, :], ps[:, :], ACT.Gelu_apprx_tanh), t))
    u_tok = act.now()
    for fb in range(NB):
        i, ps, free = bank()
        for n in range(QT):
            t = mm(ps[:, n * P:(n + 1) * P], V[:, n, fb * P:(fb + 1) * P], wsT[:, fb // 2, :], True, True, n == QT - 1,
                   free, ln_tok, w_tok)
        a = dve.do(lambda e, fb=fb, ps=ps: e.tensor_tensor(
            yA[:, fb, :].rearrange("p (n t) -> p n t", t=P), ps[:, :].rearrange("p (n t) -> p n t", t=P),
            bsB[:, fb // 2, :].unsqueeze(1).broadcast_to((P, QT, P)), ALU.add), t, u_tok)
        bank_free[i] = a
        dve.do(lambda e, fb=fb: e.tensor_tensor(yA[:, fb, :], yA[:, fb, :], uT[:, fb, :], ALU.mult), a)
    g.barrier()

    top[0] = work
    qT = alloc3(NB, S)
    ks, kw = alloc3(4, S), alloc3(4, S)
    kc2, vc2 = yC[:, 0:4, :], yC[:, 4:8, :]
    VV = alloc3(QT, S)
    gat = alloc3(QT, 48)
    gw = alloc(NB * 48)
    gw_tok = g.load([(gw, I["w_gate"][:, :])])
    gemm("w_q", NB, NB, lambda k: hT[:, k, :], h_tok,
         lambda nb, ps, t: (act.do(lambda e: e.activation(qT[:, nb, :], ps[:, :], ACT.Copy, scale=0.125), t) if nb % 2 else
                            dve.do(lambda e: e.tensor_scalar(qT[:, nb, :], ps[:, :], 0.125, None, ALU.mult), t)))

    def kv_evac(nb, ps, t):
        eng = act if nb % 2 else dve
        what, half = nb // 2, nb % 2
        for gi in range(2):
            grp = 2 * half + gi
            src = ps[64 * gi:64 * gi + 64, :]
            if what < 2:
                dst = (kc2, vc2)[what]
                t2 = copy(eng, dst[0:64, grp, :], src, t)
                t2 = copy(eng, dst[64:128, grp, 0:S - 1], src[:, 1:S], t)
            else:
                dst = (ks, kw)[what - 2]
                t2 = copy(eng, dst[0:64, grp, :], src, t)
                t2 = copy(eng, dst[64:128, grp, :], src, t)
        return t2

    gemm("w_kv", 8, NB, lambda k: hT[:, k, :], h_tok, kv_evac)
    ws = [take("w_vt", 512) for _ in range(NB)]
    for qt in range(QT):
        i, ps, free = bank()
        for k in range(NB):
            t = mm(ps[:, :], hT[:, k, qt * P:(qt + 1) * P], ws[k][0], k == 0, k == NB - 1, k == NB - 1, free, ws[k][1])
        bank_free[i] = copy(g.turns(qt), VV[:, qt, :], ps[:, :], t)
    release(t)
    i, ps, free = bank()
    for qt in range(QT):
        for k in range(NB):
            t = mm(ps[:, qt * 48:qt * 48 + 48], hT[:, k, qt * P:(qt + 1) * P], gw[:, k * 48:k * 48 + 48], k == 0,
                   k == NB - 1, k == NB - 1, free, gw_tok)
    bank_free[i] = act.do(lambda e, ps=ps: e.activation(gat, ps[:, 0:192].rearrange("p (a b) -> p a b", b=48), ACT.Sigmoid), t)
    kv_tok = [act.now(), dve.now()]

    hid = alloc3(4, P)
    peb = alloc(4)
    kc = alloc(4 * NCMP)
    vcS = alloc3(4, 64)
    w2 = alloc(4 * 64).rearrange("p (a b c) -> p a b c", a=2, b=2)
    w2_tok = g.load([(w2, I["w_cmp2"].rearrange("p (a b c) -> p a b c", a=2, b=2))])
    for kind in range(2):
        src = (kc2, vc2)[kind]
        for hb in range(2):
            us = [take(("wk1", "wv1")[kind], P) for _ in range(16)]
            i, ps, free = bank()
            for j in range(16):
                mm(ps[:, 0:124].rearrange("p (a b) -> p a b", b=NCMP), us[j][0], src[:, :, 2 * j:2 * j + 481:16], j == 0,
                   j == 15, False, free, us[j][1], kv_tok)
            pv = vec[("pe_k", "pe_v")[kind]]
            for j in range(16):
                t = mm(ps[:, 128:129], us[j][0], pv[:, j:j + 1], j == 0, j == 15, j == 15)
            release(t)
            c = 2 * kind + hb
            a = act.do(lambda e, ps=ps, c=c: e.activation(peb[:, c:c + 1], ps[:, 128:129], ACT.Copy), t)
            bank_free[i] = act.do(lambda e, ps=ps, c=c: e.activation(hid[:, c, 0:124], ps[:, 0:124], ACT.Gelu_apprx_tanh,
                                                                     bias=peb[:, c:c + 1]), a)
    h2 = act.now()
    i, ps, free = bank()
    for hb in range(2):
        t = mm(ps[0:64, 0:124], w2[:, 0, hb, :], hid[:, hb, 0:124], hb == 0, hb == 1, hb == 1, free, h2, w2_tok)
    copy(dve, kc[0:64, :], ps[0:64, 0:124], t)
    bank_free[i] = copy(dve, kc[64:128, :], ps[0:64, 0:124], t)
    i, ps, free = bank()
    for grp in range(4):
        for hb in range(2):
            t = mm(ps[0:NCMP, grp * 64:grp * 64 + 64], hid[:, 2 + hb, grp * NCMP:(grp + 1) * NCMP], w2[:, 1, hb, :],
                   hb == 0, hb == 1, hb == 1, free)
    bank_free[i] = kc_tok = copy(dve, vcS[0:NCMP, :, :], ps[0:NCMP, 0:256].rearrange("p (a b) -> p a b", b=64), t)

    cneg = alloc(QT * NCMP).rearrange("p (a b) -> p a b", b=NCMP)
    rv = alloc(1)
    Pc = yC[:, 0:4, :].rearrange("p a b -> p (a b)")[:, 0:QT * 16 * NCMP].rearrange("p (q h n) -> p q h n", q=QT, n=NCMP)
    sm = alloc(3 * 8).rearrange("p (a b) -> p a b", b=8)
    cn_tok = g.load([(cneg, I["cneg"].rearrange("p (a b) -> p a b", b=NCMP)), (rv, I["rowvalid"][:, :])])
    g.barrier()
    gv = gat.rearrange("p q (h c) -> p q h c", c=3)
    for qt in range(QT):
        for par in range(2):
            i, ps, free = bank()
            for hh in range(8):
                h = 2 * hh + par
                b0 = 64 * par
                t = mm(ps[:, hh * NCMP:(hh + 1) * NCMP], qT[b0:b0 + 64, hh, qt * P:(qt + 1) * P],
                       kc[b0:b0 + 64, (h // 4) * NCMP:(h // 4 + 1) * NCMP], True, True, hh == 7, free, kc_tok)
            pc = Pc[:, qt, par::2, :]
            a = dve.do(lambda e, ps=ps, qt=qt, pc=pc: e.tensor_tensor(
                pc, ps[:, 0:8 * NCMP].rearrange("p (a b) -> p a b", b=NCMP),
                cneg[:, qt, :].unsqueeze(1).broadcast_to((P, 8, NCMP)), ALU.add), t, cn_tok)
            bank_free[i] = a
            a = dve.do(lambda e, pc=pc: e.tensor_reduce(sm[:, 0, :], pc, AX.X, ALU.max), a)
            a = dve.do(lambda e, pc=pc: e.tensor_tensor(pc, pc, sm[:, 0, :].unsqueeze(2).broadcast_to((P, 8, NCMP)), ALU.subtract), a)
            b = act.do(lambda e, pc=pc: e.activation(pc, pc, ACT.Exp), a)
            a = dve.do(lambda e, pc=pc: e.tensor_reduce(sm[:, 1, :], pc, AX.X, ALU.add), b)
            a = dve.do(lambda e: e.reciprocal(sm[:, 2, :], sm[:, 1, :]), a)
            a = dve.do(lambda e, qt=qt, par=par: e.tensor_tensor(sm[:, 2, :], sm[:, 2, :], gv[:, qt, par::2, 0], ALU.mult), a)
            if qt == 0:
                a = dve.do(lambda e: e.tensor_scalar(sm[:, 2, :], sm[:, 2, :], rv, None, ALU.mult), a)
            pc_tok = dve.do(lambda e, pc=pc: e.tensor_tensor(pc, pc, sm[:, 2, :].unsqueeze(2).broadcast_to((P, 8, NCMP)), ALU.mult), a)

    Pb = [alloc3(QT, S) for _ in range(2)]
    Pb_free = [None, None]
    PT = [alloc(S) for _ in range(3)]
    PT_free = [None] * 3
    nm = alloc3(2, 4 * QT)
    n_pt = [0]

    def scores(h, br, buf):
        grp, b0 = h // 4, 64 * (h % 2)
        K = (ks, kw)[br]
        done = None
        for qt in range(QT):
            n = (qt + 1) * P
            i, ps, free = bank()
            t = mm(ps[:, 0:n], qT[b0:b0 + 64, h // 2, qt * P:(qt + 1) * P], K[b0:b0 + 64, grp, 0:n], True, True, True, free)
            a = dve.do(lambda e, ps=ps, qt=qt: e.tensor_tensor(ps[:, qt * P:(qt + 1) * P], ps[:, qt * P:(qt + 1) * P],
                                                               g.tri, ALU.add), t)
            m = nm[:, buf, 4 * qt:4 * qt + 4]
            a = dve.do(lambda e, ps=ps, n=n, m=m: e.tensor_reduce(m[:, 0:1], ps[:, 0:n], AX.X, ALU.max, negate=True), a, Pb_free[buf])
            b = act.do(lambda e, ps=ps, n=n, m=m, qt=qt: e.activation(Pb[buf][:, qt, 0:n], ps[:, 0:n], ACT.Exp, bias=m[:, 0:1],
                                                                      accum_out=m[:, 1:2]), a)
            bank_free[i] = b
            a = dve.do(lambda e, m=m: e.reciprocal(m[:, 2:3], m[:, 1:2]), b)
            a = dve.do(lambda e, m=m, qt=qt, h=h: e.tensor_tensor(m[:, 3:4], m[:, 2:3], gv[:, qt, h, 1 + br:2 + br], ALU.mult), a)
            done = dve.do(lambda e, m=m, n=n, qt=qt: e.tensor_scalar(Pb[buf][:, qt, 0:n], Pb[buf][:, qt, 0:n], m[:, 3:4], None, ALU.mult), a)
        return done

    def values(h, br, buf, tok, o):
        grp, b0 = h // 4, 64 * (h % 2)
        for kt in range(QT):
            i, ps, free = bank()
            for qt in range(kt, QT):
                t = tr(ps[:, qt * P:(qt + 1) * P], Pb[buf][:, qt, kt * P:(kt + 1) * P], ident, qt == QT - 1, free, tok)
            if kt == QT - 1:
                Pb_free[buf] = t
            j = n_pt[0] % 3
            n_pt[0] += 1
            bank_free[i] = c = copy(act if kt == 1 else dve, PT[j][:, kt * P:S], ps[:, kt * P:S], t, PT_free[j])
            PT_free[j] = last = mm(o[b0:b0 + 64, kt * P:S], VV[:, kt, br * 256 + grp * 64:br * 256 + grp * 64 + 64],
                                   PT[j][:, kt * P:S], False, kt == QT - 1 and br == 1, True, c)
        return last

    def compressed(h, o, free_o):
        b0 = 64 * (h % 2)
        i, ps, free = bank()
        for qt in range(QT):
            t = tr(ps[0:NCMP, qt * P:(qt + 1) * P], Pc[:, qt, h, :], ident, qt == QT - 1, free, pc_tok)
        j = n_pt[0] % 3
        n_pt[0] += 1
        bank_free[i] = c = copy(dve, PT[j][0:NCMP, :], ps[0:NCMP, :], t, PT_free[j])
        PT_free[j] = mm(o[b0:b0 + 64, :], vcS[0:NCMP, h // 4, :], PT[j][0:NCMP, :], True, False, True, c, free_o)

    jobs = [(h, br) for h in range(NH) for br in range(2)]
    ready = scores(*jobs[0], 0)
    o_free = [None, None]
    for n, (h, br) in enumerate(jobs):
        nxt = scores(*jobs[n + 1], (n + 1) % 2) if n + 1 < len(jobs) else None
        ob = (h // 2) % 2
        o = psum[6 + ob]
        if br == 0:
            compressed(h, o, o_free[ob] if h % 2 == 0 else None)
        last = values(h, br, n % 2, ready, o)
        if h % 2 == 1 and br == 1:
            o_free[ob] = copy(act, yB[:, h // 2, :], o[:, :], last)
        ready = nxt
    g.barrier()

    top[0] = work
    xc, rr, ii, gl = (alloc3(NB, S) for _ in range(4))
    bda, bdx = alloc3(NB, P), alloc3(NB, P)
    xs = [alloc(S + 3) for _ in range(2)]
    xs_free = [None, None]
    c8 = alloc(NB)
    z = pool.do(lambda e: e.memset(bda, 0.0))
    z = pool.do(lambda e: e.memset(bdx, 0.0), z)
    for q in xs:
        z = pool.do(lambda e, q=q: e.memset(q[:, 0:3], 0.0))
    pairs = []
    for dst, name in ((bda, "rnn_wa"), (bdx, "rnn_wx")):
        for par in range(2):
            pairs.append((dst[64 * par:64 * par + 64, :, 64 * par:64 * par + 64],
                          I[name][par::2, :, :].rearrange("h i o -> i h o")))
    bd_tok = g.load(pairs, z)
    sp_t = alloc3(6, NB)
    ab, ee, zz, z2, ac, mx = (sp_t[:, j, :] for j in range(6))
    lam = vec["rnn_lam"]
    a = dve.do(lambda e: e.tensor_scalar(ab, lam, -1.0, None, ALU.mult))
    a = dve.do(lambda e: e.tensor_tensor(ab, ab, lam, ALU.min), a)
    m0 = dve.do(lambda e: e.tensor_scalar(mx, lam, -1.0, 0.0, ALU.mult, ALU.max), a)
    b = act.do(lambda e: e.activation(ee, ab, ACT.Exp), a)
    a = dve.do(lambda e: e.tensor_scalar(zz, ee, 2.0, None, ALU.add), b)
    a = dve.do(lambda e: e.reciprocal(zz, zz), a)
    a = dve.do(lambda e: e.tensor_tensor(zz, zz, ee, ALU.mult), a)
    a = dve.do(lambda e: e.tensor_tensor(z2, zz, zz, ALU.mult), a)
    a = dve.do(lambda e: e.tensor_scalar(ac, z2, 1.0 / 15, 1.0 / 13, ALU.mult, ALU.add), a)
    for n in (11, 9, 7, 5, 3, 1):
        a = dve.do(lambda e: e.tensor_tensor(ac, ac, z2, ALU.mult), a)
        a = dve.do(lambda e, n=n: e.tensor_scalar(ac, ac, 1.0 / n, None, ALU.add), a)
    a = dve.do(lambda e: e.tensor_tensor(ac, ac, zz, ALU.mult), a)
    a = dve.do(lambda e: e.scalar_tensor_tensor(ac, ac, 2.0, mx, ALU.mult, ALU.add), a, m0)
    c8_tok = dve.do(lambda e: e.tensor_scalar(c8, ac, -8.0, None, ALU.mult), a)

    cw, cb = vec["conv_w"], vec["conv_b"]
    xc_tok = [None] * NB

    def conv(nb, ps, t):
        q = xs[nb % 2]
        a = act.do(lambda e: e.activation(q[:, 3:S + 3], ps[:, :], ACT.Copy), t, xs_free[nb % 2], z)
        b = dve.do(lambda e: e.tensor_scalar(xc[:, nb, :], q[:, 3:S + 3], cw[:, 24 + nb:25 + nb], cb[:, nb:nb + 1], ALU.mult, ALU.add), a)
        for j in (2, 1, 0):
            b = dve.do(lambda e, j=j: e.scalar_tensor_tensor(xc[:, nb, :], q[:, j:j + S], cw[:, 8 * j + nb:8 * j + nb + 1], xc[:, nb, :],
                                                             ALU.mult, ALU.add), b)
        xs_free[nb % 2] = xc_tok[nb] = b
        return a

    gemm("w_xr", NB, NB, lambda k: hT[:, k, :], h_tok, conv)
    gemm("w_rg", NB, NB, lambda k: hT[:, k, :], h_tok,
         lambda nb, ps, t: act.do(lambda e: e.activation(gl[:, nb, :], ps[:, :], ACT.Gelu_apprx_tanh), t))
    for nb in range(NB):
        for w, dst, bias in ((bda, rr, "rnn_ba"), (bdx, ii, "rnn_bx")):
            i, ps, free = bank()
            t = mm(ps[:, :], w[:, nb, :], xc[:, nb, :], True, True, True, free, bd_tok, xc_tok[nb])
            bank_free[i] = act.do(lambda e, ps=ps, dst=dst, bias=bias, nb=nb: e.activation(
                dst[:, nb, :], ps[:, :], ACT.Sigmoid, bias=vec[bias][:, nb:nb + 1]), t)
    tk = [None] * NB
    ta = [None] * NB
    for nb in range(NB):
        a = dve.do(lambda e, nb=nb: e.tensor_tensor(xc[:, nb, :], xc[:, nb, :], ii[:, nb, :], ALU.mult), act.now() if nb == 0 else None)
        b = act.do(lambda e, nb=nb: e.activation(ii[:, nb, :], rr[:, nb, :], ACT.Tanh, scale=c8[:, nb:nb + 1]), a, c8_tok)
        b = ta[nb] = act.do(lambda e, nb=nb: e.activation(rr[:, nb, :], rr[:, nb, :], ACT.Exp, scale=c8[:, nb:nb + 1]), b)
        yc = yC[:, nb, :]
        a = dve.do(lambda e, nb=nb, yc=yc: e.tensor_tensor(yc, rr[:, nb, :], rr[:, nb, :], ALU.mult), b)
        tk[nb] = dve.do(lambda e, nb=nb, yc=yc: e.scalar_tensor_tensor(ii[:, nb, :], yc, 1.0, ii[:, nb, :], ALU.add, ALU.mult), a)
    for nb in range(NB):
        b = act.do(lambda e, nb=nb: e.activation(ii[:, nb, :], ii[:, nb, :], ACT.Sqrt, scale=-1.0), tk[nb])
        a = dve.do(lambda e, nb=nb: e.tensor_tensor(xc[:, nb, :], xc[:, nb, :], ii[:, nb, :], ALU.mult), b)
        a = dve.do(lambda e, nb=nb: e.tensor_tensor_scan(yC[:, nb, :], rr[:, nb, :], xc[:, nb, :], 0.0, ALU.mult, ALU.add), a)
        dve.do(lambda e, nb=nb: e.tensor_tensor(yC[:, nb, :], yC[:, nb, :], gl[:, nb, :], ALU.mult), a)
    g.barrier()

    top[0] = work
    mg, mo = alloc3(NB, S), alloc3(NB, S)
    gt = [alloc(S) for _ in range(3)]
    gt_free = [None] * 3
    tt = alloc(S)
    n = 0
    for nb in range(NB):
        for c in range(3):
            i, ps, free = bank()
            for k in range(NB):
                w, wt = take(f"w_mb{nb}", P)
                t = mm(ps[:, :], w, hT[:, k, :], k == 0, k == NB - 1, k == NB - 1, free, wt)
            release(t)
            q = gt[n % 3]
            bank_free[i] = s = act.do(lambda e, ps=ps, q=q: e.activation(q, ps[:, :], ACT.Sigmoid), t, gt_free[n % 3])
            i, ps, free = bank()
            for k in range(NB):
                w, wt = take(f"w_mb{nb}", P)
                t = mm(ps[:, :], w, (yA, yB, yC)[c][:, k, :], k == 0, k == NB - 1, k == NB - 1, free, wt)
            release(t)
            if c == 0:
                a = dve.do(lambda e, ps=ps, q=q, nb=nb: e.tensor_tensor(mg[:, nb, :], ps[:, :], q, ALU.mult), t, s)
                bank_free[i] = a
            else:
                b = dve.do(lambda e, ps=ps, q=q: e.tensor_tensor(tt, ps[:, :], q, ALU.mult), t, s, a)
                bank_free[i] = b
                a = dve.do(lambda e, nb=nb: e.tensor_tensor(mg[:, nb, :], mg[:, nb, :], tt, ALU.add), b)
            gt_free[n % 3] = a
            n += 1
    m_tok = dve.now()
    gemm("w_o", NB, NB, lambda k: mg[:, k, :], m_tok, lambda nb, ps, t: copy(g.turns(nb), mo[:, nb, :], ps[:, :], t))
    t = g.rstd_of(mo, r, act.now(), dve.now())
    x_tok = g.add_normed(mo, vec["g_post_mix"], r, t)
    g.barrier()

    top[0] = g.base
    hf, fo = alloc3(NB, S), alloc3(NB, S)
    pr = alloc3(NFF, S)
    r = alloc(S)
    sg = [alloc(S) for _ in range(2)]
    sg_free = [None, None]
    t = g.rstd_of(xT, r)
    h_tok = g.normed(xT, vec["g_pre_ffn"], hf, r, t)
    for nb in range(NFF):
        two = []
        for _ in range(2):
            i, ps, free = bank()
            for k in range(NB):
                w, wt = take("w_fi", P)
                t = mm(ps[:, :], w, hf[:, k, :], k == 0, k == NB - 1, k == NB - 1, free, wt, h_tok)
            release(t)
            two.append((i, ps, t))
        q = sg[nb % 2]
        bank_free[two[0][0]] = s = act.do(lambda e, ps=two[0][1], q=q: e.activation(q, ps[:, :], ACT.Silu), two[0][2], sg_free[nb % 2])
        bank_free[two[1][0]] = sg_free[nb % 2] = dve.do(
            lambda e, ps=two[1][1], q=q, nb=nb: e.tensor_tensor(pr[:, nb, :], ps[:, :], q, ALU.mult), two[1][2], s)
    f_tok = dve.now()
    gemm("w_fo", NB, NFF, lambda k: pr[:, k, :], f_tok, lambda nb, ps, t: copy(g.turns(nb), fo[:, nb, :], ps[:, :], t))
    t = g.rstd_of(fo, r, act.now(), dve.now())
    g.add_normed(fo, vec["g_post_ffn"], r, t)
    g.barrier()


def mlp(g, layer):
    act, dve, pool = g.act, g.dve, g.pool
    g.top[0] = g.base
    hf = g.alloc3(NB, S)
    hid = g.alloc3(NMLP, S)
    r = g.alloc(S)
    t = g.rstd_of(g.xT, r)
    gain = g.vec["norm_g"]
    h_tok = g.normed(g.xT, gain[:, 32 * layer + 16:32 * layer + 24], hf, r, t)
    relu = [g.alloc(S) for _ in range(2)]
    relu_free = [None, None]

    def evac(nb, ps, t):
        q = relu[nb % 2]
        a = act.do(lambda e: e.activation(q, ps[:, :], ACT.Relu), t, relu_free[nb % 2])
        relu_free[nb % 2] = dve.do(lambda e: e.tensor_tensor(hid[:, nb, :], q, q, ALU.mult), a)
        return a

    g.gemm(f"w_m1{layer}", NMLP, NB, lambda k: hf[:, k, :], h_tok, evac)
    m_tok = dve.now()
    pe_tok = g.pe.now()
    fo = hf
    g.gemm(f"w_m2{layer}", NB, NMLP, lambda k: hid[:, k, :], m_tok,
           lambda nb, ps, t: g.copy(g.turns(nb), fo[:, nb, :], ps[:, :], t, pe_tok))
    t = g.rstd_of(fo, r, act.now(), dve.now())
    g.add_normed(fo, gain[:, 32 * layer + 24:32 * layer + 32], r, t)


def attention2(g):
    pe, act, dve, pool, vec, I = g.pe, g.act, g.dve, g.pool, g.vec, g.I
    alloc, alloc3, bank, mm, tr, gemm, take, release = g.alloc, g.alloc3, g.bank, g.mm, g.tr, g.gemm, g.take, g.release
    copy, psum, bank_free, xT, ident, top = g.copy, g.psum, g.bank_free, g.xT, g.ident, g.top
    top[0] = g.base
    hT = alloc3(NB, S)
    r = alloc(S)
    oT = alloc3(NB, S)
    qT, kT = alloc3(NB, S), alloc3(4, S)
    kb = alloc3(2, S)
    VA = alloc3(QT, S)
    VB = alloc3(QT, P)
    sink = alloc(8)
    mark = top[0]
    oh, tab = alloc(1024), alloc(16)
    bv = alloc(1024)
    ld = g.load([(oh[0:32, :], I["onehot"][:, :]), (tab[0:32, :], I["rel_table"][:, :]),
                 (sink, I["sink"][0, :].partition_broadcast(P))])
    for half in range(2):
        i, ps, free = bank()
        t = mm(ps[0:16, :], tab[0:32, :], oh[0:32, half * 512:half * 512 + 512], True, True, True, free, ld)
        bank_free[i] = b_tok = copy(dve, bv[0:16, half * 512:half * 512 + 512], ps[0:16, :], t)
    s_b = g.semaphore("bv")
    pool.dma(I["scratch"][:, :], bv[0:16, :], s_b, 16, b_tok)
    bv_tok = (s_b, 16)

    t = g.rstd_of(xT, r)
    h_tok = g.normed(xT, vec["norm_g"][:, 0:8], hT, r, t)

    def evac(nb, ps, t):
        eng = act if nb % 2 else dve
        if nb < 8:
            return (act.do(lambda e: e.activation(qT[:, nb, :], ps[:, :], ACT.Copy, scale=0.125), t) if nb % 2 else
                    dve.do(lambda e: e.tensor_scalar(qT[:, nb, :], ps[:, :], 0.125, None, ALU.mult), t))
        if nb < 12:
            return copy(eng, kT[:, nb - 8, :], ps[:, :], t)
        for gi in range(2):
            for c in range(2):
                t2 = copy(eng, kb[64 * c:64 * c + 64, gi, :], ps[64 * gi:64 * gi + 64, :], t)
        return t2

    gemm("w_a2", 13, NB, lambda k: hT[:, k, :], h_tok, evac)
    vbw = [take("w_a2", P) for _ in range(NB)]
    i, ps, free = bank()
    for qt in range(QT):
        for k in range(NB):
            t = mm(ps[:, qt * P:(qt + 1) * P], hT[:, k, qt * P:(qt + 1) * P], vbw[k][0], k == 0, k == NB - 1,
                   k == NB - 1, free, vbw[k][1])
    release(t)
    bank_free[i] = copy(dve, VB, ps[:, :].rearrange("p (a b) -> p a b", b=P), t)
    ws = [take("w_va", 512) for _ in range(NB)]
    for qt in range(QT):
        i, ps, free = bank()
        for k in range(NB):
            t = mm(ps[:, :], hT[:, k, qt * P:(qt + 1) * P], ws[k][0], k == 0, k == NB - 1, k == NB - 1, free, ws[k][1])
        bank_free[i] = copy(g.turns(qt), VA[:, qt, :], ps[:, :], t)
    release(t)
    g.barrier()
    top[0] = mark

    BT = [alloc(896) for _ in range(2)]
    BT_free = [None, None]
    bt_sem = [g.semaphore("bt") for _ in range(2)]
    mA, mB = alloc(896), alloc(896)
    mk = g.load([(mA, I["maskA"][:, :]), (mB, I["maskB"][:, :])], bv_tok)
    Pb = [alloc3(QT, S) for _ in range(2)]
    Pb_free = [None, None]
    PT = [alloc(S) for _ in range(3)]
    PT_free = [None] * 3
    nm = alloc3(2, 8 * QT)
    n_pt = [0]

    def keys(h, qt):
        return (0, S) if h < 8 else (max(0, (qt - 1) * P), min(S, (qt + 2) * P))

    def bias(h):
        b = BT[h % 2]
        sc = I["scratch"]
        src = bass.AP(tensor=sc.tensor, offset=sc.offset + h * 1024, ap=[[1, P], [1, 896]])
        pool.dma(b, src, bt_sem[h % 2], 0, BT_free[h % 2], bv_tok)
        return pool.do(lambda e: e.tensor_tensor(b, b, mA if h < 8 else mB, ALU.add), (bt_sem[h % 2], 16 * (h // 2 + 1)), mk)

    bias_tok = [None] * 18
    bias_tok[0] = bias(0)

    def scores(h, buf):
        b0 = 64 * (h % 2)
        K = kT[b0:b0 + 64, h // 2, :] if h < 8 else kb[b0:b0 + 64, (h - 8) // 4, :]
        done = None
        for qt in range(QT):
            a0, a1 = keys(h, qt)
            n = a1 - a0
            i, ps, free = bank()
            t = mm(ps[:, 0:n], qT[b0:b0 + 64, h // 2, qt * P:(qt + 1) * P], K[:, a0:a1], True, True, True, free)
            off = 384 - qt * P + a0
            pb = Pb[buf][:, qt, a0:a1]
            a = dve.do(lambda e, ps=ps, n=n, off=off, pb=pb: e.tensor_tensor(pb, ps[:, 0:n], BT[h % 2][:, 896 - off - n:896 - off][:, ::-1], ALU.add),
                       t, bias_tok[h], Pb_free[buf])
            bank_free[i] = a
            if qt == QT - 1:
                BT_free[h % 2] = a
            m = nm[:, buf, 8 * qt:8 * qt + 8]
            a = dve.do(lambda e, pb=pb, m=m: e.tensor_reduce(m[:, 0:1], pb, AX.X, ALU.max), a)
            if h >= 8:
                a = dve.do(lambda e, m=m, h=h: e.tensor_tensor(m[:, 0:1], m[:, 0:1], sink[:, h - 8:h - 7], ALU.max), a, ld)
            a = dve.do(lambda e, m=m: e.tensor_scalar(m[:, 1:2], m[:, 0:1], -1.0, None, ALU.mult), a)
            b = act.do(lambda e, pb=pb, m=m: e.activation(pb, pb, ACT.Exp, bias=m[:, 1:2], accum_out=m[:, 2:3]), a)
            if h >= 8:
                b = act.do(lambda e, m=m, h=h: e.activation(m[:, 3:4], sink[:, h - 8:h - 7], ACT.Exp, bias=m[:, 1:2]), b)
                a = dve.do(lambda e, m=m: e.tensor_tensor(m[:, 2:3], m[:, 2:3], m[:, 3:4], ALU.add), b)
            else:
                a = b
            a = dve.do(lambda e, m=m: e.reciprocal(m[:, 4:5], m[:, 2:3]), a)
            done = dve.do(lambda e, m=m, pb=pb: e.tensor_scalar(pb, pb, m[:, 4:5], None, ALU.mult), a)
        return done

    def values(h, buf, tok, o, free_o):
        b0 = 64 * (h % 2)
        for n, kt in enumerate(range(QT)):
            qs = [qt for qt in range(QT) if keys(h, qt)[0] <= kt * P < keys(h, qt)[1]]
            a0, a1 = qs[0] * P, (qs[-1] + 1) * P
            i, ps, free = bank()
            for qt in qs:
                t = tr(ps[:, qt * P:(qt + 1) * P], Pb[buf][:, qt, kt * P:(kt + 1) * P], ident, qt == qs[-1], free, tok)
            if kt == QT - 1:
                Pb_free[buf] = t
            j = n_pt[0] % 3
            n_pt[0] += 1
            bank_free[i] = c = copy(act, PT[j][:, a0:a1], ps[:, a0:a1], t, PT_free[j])
            V = VA[:, kt, h * 64:h * 64 + 64] if h < 8 else VB[:, kt, (h - 8) // 4 * 64:(h - 8) // 4 * 64 + 64]
            PT_free[j] = last = mm(o[b0:b0 + 64, a0:a1], V, PT[j][:, a0:a1], n == 0, n == QT - 1, True, c,
                                   free_o if n == 0 else None)
        return last

    ready = scores(0, 0)
    o_free = [None, None]
    for h in range(NH):
        if h + 1 < NH:
            bias_tok[h + 1] = bias(h + 1)
            nxt = scores(h + 1, (h + 1) % 2)
        o = psum[6 + (h // 2) % 2]
        last = values(h, h % 2, ready, o, o_free[(h // 2) % 2] if h % 2 == 0 else None)
        if h % 2 == 1:
            o_free[(h // 2) % 2] = o_tok = copy(act, oT[:, h // 2, :], o[:, :], last)
        ready = nxt
    u = hT
    gemm("w_ao", NB, NB, lambda k: oT[:, k, :], o_tok, lambda nb, ps, t: copy(g.turns(nb), u[:, nb, :], ps[:, :], t))
    t = g.rstd_of(u, r, act.now(), dve.now())
    g.add_normed(u, vec["norm_g"][:, 8:16], r, t)
    g.barrier()
    mlp(g, 0)
    g.barrier()


def rwkv(g):
    pe, act, dve, pool, vec, I = g.pe, g.act, g.dve, g.pool, g.vec, g.I
    alloc, alloc3, bank, mm, tr, gemm = g.alloc, g.alloc3, g.bank, g.mm, g.tr, g.gemm
    copy, psum, bank_free, xT, ident, top = g.copy, g.psum, g.bank_free, g.xT, g.ident, g.top
    top[0] = g.base
    rT, kT, vT = alloc3(NB, S), alloc3(NB, S), alloc3(NB, S)
    tw, ta, tg = alloc(S), alloc(S), alloc3(2, S)
    yT = alloc3(NB, S)
    mark = top[0]
    hT, dp, dn = yT, alloc3(NB, S), alloc3(NB, S)
    r = alloc(S)
    mix = alloc3(NB, S)
    t = g.rstd_of(xT, r)
    h_tok = g.normed(xT, vec["norm_g"][:, 32:40], hT, r, t)
    a = pool.do(lambda e: e.tensor_tensor(dp[:, :, 1:S], hT[:, :, 0:S - 1], hT[:, :, 1:S], ALU.subtract), h_tok)
    a = pool.do(lambda e: e.tensor_scalar(dp[:, :, 0:1], hT[:, :, 0:1], -1.0, None, ALU.mult), h_tok)
    b = dve.do(lambda e: e.tensor_tensor(dn[:, :, 0:S - 1], hT[:, :, 1:S], hT[:, :, 0:S - 1], ALU.subtract), h_tok)
    b = dve.do(lambda e: e.tensor_scalar(dn[:, :, S - 1:S], hT[:, :, S - 1:S], -1.0, None, ALU.mult), h_tok)
    d_tok = [a, b]
    mp, mn = vec["mu_prev"], vec["mu_next"]

    def mixed(c, free):
        for k in range(NB):
            m = 8 * c + k
            a = dve.do(lambda e, k=k, m=m: e.scalar_tensor_tensor(mix[:, k, :], dp[:, k, :], mp[:, m:m + 1], hT[:, k, :],
                                                                  ALU.mult, ALU.add), d_tok, free)
            a = dve.do(lambda e, k=k, m=m: e.scalar_tensor_tensor(mix[:, k, :], dn[:, k, :], mn[:, m:m + 1], mix[:, k, :],
                                                                  ALU.mult, ALU.add), a)
        return a

    rhs = lambda k: mix[:, k, :]
    m = mixed(1, None)
    gemm("w_rw", 1, NB, rhs, m, lambda nb, ps, t: act.do(lambda e: e.activation(tw, ps[:, :], ACT.Tanh), t))
    m = mixed(4, pe.now())
    gemm("w_ra", 1, NB, rhs, m, lambda nb, ps, t: copy(act, ta, ps[:, :], t))
    m = mixed(5, pe.now())
    gemm("w_rg1", 2, NB, rhs, m, lambda nb, ps, t: act.do(lambda e: e.activation(tg[:, nb, :], ps[:, :], ACT.Sigmoid), t))
    for c, name, dst in ((0, "w_rr", rT), (2, "w_rk", kT), (3, "w_rv", vT)):
        m = mixed(c, pe.now())
        gemm(name, NB, NB, rhs, m, lambda nb, ps, t: copy(act, dst[:, nb, :], ps[:, :], t))
    g.barrier()
    top[0] = mark

    lm = alloc(2 * 6 * 64).rearrange("p (d l a) -> p d l a", d=2, l=6)
    mM = alloc3(2, P)
    rm = alloc(S)
    w2 = alloc(4 * P).rearrange("p (a b) -> p a b", a=4)
    omka = alloc(NB)
    ld = g.load([(lm[0:64], I["levels"].rearrange("p (d l a) -> p d l a", d=2, l=6)),
                 (mM, I["maskM"].rearrange("p (a b) -> p a b", b=P)), (rm, I["starts"][0, :].partition_broadcast(P))])
    kk, sg, cs, aa, kd, e1, e2, t1, t2 = (alloc(S) for _ in range(9))
    AR, BK, BKs = (alloc(2 * S).rearrange("p (c a t) -> p c a t", a=2, t=CH) for _ in range(3))
    wc = alloc(NCH)
    M = alloc3(16, P)
    XT, X, Y, LM, G1, BKn = (alloc3(16, CH) for _ in range(6))
    SAV = alloc3(NCH, P)
    U = alloc(P)
    Sb = alloc(P)
    oS, bon = aa, cs
    vec_k = vec["k_a"]
    z1 = pool.do(lambda e: e.memset(Sb, 0.0))
    z2 = dve.do(lambda e: e.tensor_scalar(omka, vec_k, -1.0, 1.0, ALU.mult, ALU.add))
    w2_sem = g.semaphore("w2")
    g.barrier()
    for e in (pe, act, dve, pool):
        e.wait(ld)

    def chunks(ap):
        return ap.rearrange("p (c t) -> p c t", t=CH)

    def norm_rows(b):
        a = dve.do(lambda e: e.tensor_scalar(kk, kT[:, b, :], vec["k_k"][:, b:b + 1], None, ALU.mult))
        s = act.do(lambda e: e.activation(t1, kk, ACT.Square), a)
        i, ps, free = bank()
        t = mm(ps[:, :], g.bd, t1, True, True, True, free, s)
        bank_free[i] = s = act.do(lambda e, ps=ps: e.activation(t2, ps[:, :], ACT.Sqrt), t)
        a = dve.do(lambda e: e.tensor_scalar(t2, t2, 1e-12, None, ALU.max), s)
        a = dve.do(lambda e: e.reciprocal(t2, t2), a)
        return dve.do(lambda e: e.tensor_tensor(kk, kk, t2, ALU.mult), a)

    def scan(b, d, kk_tok, w2_tok):
        sa_used = None
        i, ps, free = bank()
        t = mm(ps[:, :], w2[64 * d:64 * d + 64, 0, :], tw[64 * d:64 * d + 64, :], True, True, True, free, w2_tok)
        bank_free[i] = s1 = act.do(lambda e, ps=ps: e.activation(sg, ps[:, :], ACT.Sigmoid, bias=vec["w0"][:, 8 * d + b:8 * d + b + 1]), t)
        i, ps, free = bank()
        t = mm(ps[:, :], w2[64 * d:64 * d + 64, 1, :], ta[64 * d:64 * d + 64, :], True, True, True, free)
        bank_free[i] = s2 = act.do(lambda e, ps=ps: e.activation(aa, ps[:, :], ACT.Sigmoid, bias=vec["a0"][:, 8 * d + b:8 * d + b + 1]), t)
        st = -1 if d else 1
        a = dve.do(lambda e: e.tensor_tensor_scan(cs[:, ::st], rm, sg[:, ::st], 0.0, ALU.mult, ALU.add), s1)
        last = chunks(cs)[:, :, 0:1] if d else chunks(cs)[:, :, CH - 1:CH]
        s3 = act.do(lambda e: e.activation(e1, cs, ACT.Exp, scale=-DECAY), a)
        s4 = act.do(lambda e: e.activation(e2, cs, ACT.Exp, scale=DECAY), a)
        s5 = act.do(lambda e: e.activation(wc.unsqueeze(2), last, ACT.Exp, scale=-DECAY), a)
        a = dve.do(lambda e: e.tensor_tensor(sg, cs, sg, ALU.subtract), s5)
        s6 = act.do(lambda e: e.activation(sg, sg, ACT.Exp, scale=-DECAY), a)
        a = dve.do(lambda e: e.tensor_scalar(kd, aa, vec_k[:, b:b + 1], omka[:, b:b + 1], ALU.mult, ALU.add), s2)
        kd_tok = dve.do(lambda e: e.tensor_tensor(kd, kd, kT[:, b, :], ALU.mult), a)
        a = dve.do(lambda e: e.tensor_tensor(AR[:, :, 1, :], chunks(rT[:, b, :]), chunks(e1), ALU.mult), s3)
        a = dve.do(lambda e: e.scalar_tensor_tensor(AR[:, :, 0, :], chunks(kk), -1.0, chunks(sg), ALU.mult, ALU.mult), s6, kk_tok)
        a = dve.do(lambda e: e.tensor_tensor(t1, kk, aa, ALU.mult), s2, kk_tok)
        a = dve.do(lambda e: e.tensor_tensor(BK[:, :, 0, :], chunks(t1), chunks(e2), ALU.mult), a, s4)
        a = dve.do(lambda e: e.tensor_tensor(BK[:, :, 1, :], chunks(kd), chunks(e2), ALU.mult), kd_tok)
        bk = a
        bks = pool.do(lambda e: e.tensor_tensor(BKs.rearrange("p c a t -> p c (a t)"), BK.rearrange("p c a t -> p c (a t)"),
                                                wc.unsqueeze(2).broadcast_to((P, NCH, P)), ALU.mult), bk, s5)
        for q in range(2):
            i, ps, free = bank()
            for c in range(4):
                ch = 4 * q + c
                t = tr(ps[0:CH, c * P:(c + 1) * P], vT[:, b, ch * CH:(ch + 1) * CH], ident, c == 3, free)
            bank_free[i] = v_tok = copy(act, SAV[64:128, 4 * q:4 * q + 4, :], ps[0:CH, :].rearrange("p (a b) -> p a b", b=P), t)
        for hh in range(2):
            h0 = 64 * hh
            for q in range(2):
                i, ps, free = bank()
                for c in range(4):
                    ch = 4 * q + c
                    t = mm(ps[:, c * P:(c + 1) * P], BK[h0:h0 + 64, ch, :, :], AR[h0:h0 + 64, ch, :, :], True, True,
                           c == 3, free, bk)
                u = 8 * hh + 4 * q
                bank_free[i] = m_tok = dve.do(lambda e, ps=ps, u=u: e.tensor_tensor(
                    M[:, u:u + 4, :], ps[:, :].rearrange("p (a b) -> p a b", b=P),
                    mM[:, d, :].unsqueeze(1).broadcast_to((P, 4, P)), ALU.mult), t)
        LT = M[0:64, :, 0:CH]
        x_tok = {}

        def masked(level, free):
            return pool.do(lambda e: e.tensor_tensor(LM[0:64], LT, lm[0:64, d, level, :].unsqueeze(1).broadcast_to((64, 16, CH)),
                                                     ALU.mult), m_tok, free)

        a = masked(0, None)
        a = xt = pool.do(lambda e: e.tensor_tensor(XT[0:64], LM[0:64], ident[0:64, 0:64].unsqueeze(1).broadcast_to((64, 16, CH)),
                                                   ALU.add), a)
        for level in range(1, 6):
            lt = masked(level, [pe.now(), xt])
            xs = []
            for q in range(2):
                i, ps, free = bank()
                for c in range(8):
                    t = tr(ps[0:64, c * CH:(c + 1) * CH], XT[0:64, 8 * q + c, :], ident[0:64, 0:64], c == 7, free, xt)
                bank_free[i] = c_tok = copy(act, X[0:64, 8 * q:8 * q + 8, :], ps[0:64, :].rearrange("p (a b) -> p a b", b=CH), t)
                xs.append(c_tok)
            ys = []
            for q in range(2):
                i, ps, free = bank()
                for c in range(8):
                    u = 8 * q + c
                    t = mm(ps[0:64, c * CH:(c + 1) * CH], LM[0:64, u, :], X[0:64, u, :], True, True, c == 7, free, lt, xs[q])
                bank_free[i] = c_tok = copy(act, Y[0:64, 8 * q:8 * q + 8, :], ps[0:64, :].rearrange("p (a b) -> p a b", b=CH), t)
                ys.append(c_tok)
            for q in range(2):
                i, ps, free = bank()
                for c in range(8):
                    u = 8 * q + c
                    t = mm(ps[0:64, c * CH:(c + 1) * CH], Y[0:64, u, :], XT[0:64, u, :], True, True, c == 7, free, ys[q])
                bank_free[i] = xt = dve.do(lambda e, ps=ps, q=q: e.tensor_tensor(
                    XT[0:64, 8 * q:8 * q + 8, :], XT[0:64, 8 * q:8 * q + 8, :],
                    ps[0:64, :].rearrange("p (a b) -> p a b", b=CH), ALU.add), t, xt)
        for hh in range(2):
            h0 = 64 * hh
            i, ps, free = bank()
            for ch in range(NCH):
                t = mm(ps[0:64, ch * CH:(ch + 1) * CH], M[64:128, 8 * hh + ch, 0:CH], SAV[64:128, ch, h0:h0 + 64], True, True,
                       ch == NCH - 1, free, v_tok, m_tok)
            bank_free[i] = g1 = copy(dve, G1[0:64, 8 * hh:8 * hh + 8, :], ps[0:64, :].rearrange("p (a b) -> p a b", b=CH), t)
            i, ps, free = bank()
            for ch in range(NCH):
                t = tr(ps[:, ch * CH:(ch + 1) * CH], BKs[h0:h0 + 64, ch, :, :], ident[h0:h0 + 64, h0:h0 + 64], ch == NCH - 1, free, bks)
            bank_free[i] = bn = copy(act, BKn[:, 8 * hh:8 * hh + 8, :], ps[:, :].rearrange("p (a b) -> p a b", b=CH), t)
        O = psum[6]
        o_free = bank_free[6]
        sb = [z1, dve.now(), act.now()]
        G1c = G1.rearrange("p (h c) v -> p h c v", h=2)
        first = True
        for ch in (range(NCH - 1, -1, -1) if d else range(NCH)):
            if first:
                a = dve.do(lambda e, ch=ch: e.tensor_copy(U[0:64].rearrange("p (h v) -> p h v", h=2), G1c[0:64, :, ch, :]), g1, pe.now())
            else:
                i, ps, free = bank()
                t = mm(ps[0:64, 0:P], AR[:, ch, 0, :], Sb, True, True, True, free, sb)
                bank_free[i] = a = dve.do(lambda e, ps=ps, ch=ch: e.tensor_tensor(
                    U[0:64].rearrange("p (h v) -> p h v", h=2), ps[0:64, 0:P].rearrange("p (h v) -> p h v", h=2),
                    G1c[0:64, :, ch, :], ALU.add), t, g1, sa_used)
            i, ps, free = bank()
            for hh in range(2):
                sa_used = t = mm(ps[0:64, 64 * hh:64 * hh + 64], XT[0:64, 8 * hh + ch, :], U[0:64, 64 * hh:64 * hh + 64],
                                 True, True, hh == 1, free, a, xt)
            sa_used = pe.now()
            bank_free[i] = sv = copy(dve, SAV[0:64, ch, :], ps[0:64, 0:P], t)
            o_cols = slice(ch * CH, (ch + 1) * CH)
            if not first:
                mm(O[:, o_cols], Sb, AR[:, ch, 1, :], True, False, False, sb)
            for hh in range(2):
                h0 = 64 * hh
                o_last = mm(O[h0:h0 + 64, o_cols], SAV[:, ch, h0:h0 + 64], M[:, 8 * hh + ch, CH:P], first, True, hh == 1, o_free, sv, v_tok)
            i, ps, free = bank()
            for hh in range(2):
                h0 = 64 * hh
                t = mm(ps[h0:h0 + 64, 0:64], BKn[:, 8 * hh + ch, :], SAV[:, ch, h0:h0 + 64], True, True, hh == 1, free, bn)
            sb = []
            for hh in range(2):
                h0 = 64 * hh
                blk = Sb[h0:h0 + 64, h0:h0 + 64]
                if first:
                    a = dve.do(lambda e, ps=ps, h0=h0, blk=blk: e.tensor_copy(blk, ps[h0:h0 + 64, 0:64]), t)
                else:
                    a = dve.do(lambda e, ps=ps, h0=h0, blk=blk, ch=ch: e.scalar_tensor_tensor(
                        blk, blk, wc[h0:h0 + 64, ch:ch + 1], ps[h0:h0 + 64, 0:64], ALU.mult, ALU.add), t, o_last)
                sb.append(a)
            bank_free[i] = a
            first = False
        a = copy(dve, oS, O[:, :], o_last)
        bank_free[6] = a
        i, ps, free = bank()
        t = mm(ps[:, :], g.bdm, oS, True, True, True, free, a)
        bank_free[i] = a = dve.do(lambda e, ps=ps: e.tensor_tensor(oS, oS, ps[:, :], ALU.subtract), t)
        s = act.do(lambda e: e.activation(t1, oS, ACT.Square), a)
        i, ps, free = bank()
        t = mm(ps[:, :], g.bdm, t1, True, True, True, free, s)
        bank_free[i] = s = act.do(lambda e, ps=ps: e.activation(t2, ps[:, :], ACT.Sqrt, bias=g.eps[:, 1:2]), t)
        a = dve.do(lambda e: e.reciprocal(t2, t2), s)
        a = dve.do(lambda e: e.tensor_tensor(oS, oS, t2, ALU.mult), a)
        a = dve.do(lambda e: e.tensor_scalar(oS, oS, vec["gn_w"][:, b:b + 1], vec["gn_b"][:, b:b + 1], ALU.mult, ALU.add), a)
        c = dve.do(lambda e: e.scalar_tensor_tensor(e1, rT[:, b, :], vec["r_k"][:, b:b + 1], kd, ALU.mult, ALU.mult), a)
        i, ps, free = bank()
        t = mm(ps[:, :], g.bd, e1, True, True, True, free, c)
        bank_free[i] = c = dve.do(lambda e, ps=ps: e.tensor_tensor(bon, vT[:, b, :], ps[:, :], ALU.mult), t)
        a = dve.do(lambda e: e.tensor_tensor(oS, oS, bon, ALU.add), c)
        i, ps, free = bank()
        t = mm(ps[:, :], w2[:, 2 + d, :], tg[:, d, :], True, True, True, free)
        if d == 0:
            bank_free[i] = a = dve.do(lambda e, ps=ps: e.tensor_tensor(yT[:, b, :], oS, ps[:, :], ALU.mult), a, t)
        else:
            bank_free[i] = a = dve.do(lambda e, ps=ps: e.tensor_tensor(oS, oS, ps[:, :], ALU.mult), a, t)
            a = dve.do(lambda e: e.tensor_tensor(yT[:, b, :], yT[:, b, :], oS, ALU.add), a)
        g.barrier()

    for b in range(NB):
        w2_tok = pool.dma(w2, I["rk2"].rearrange("p (a n) -> p a n", a=4)[:, :, b * P:(b + 1) * P], w2_sem, 16 * (b + 1))
        kk_tok = norm_rows(b)
        for d in range(2):
            scan(b, d, kk_tok, w2_tok)
    g.barrier()
    top[0] = mark
    u, r = kT, alloc(S)
    gemm("w_ro", NB, NB, lambda k: yT[:, k, :], dve.now(), lambda nb, ps, t: copy(g.turns(nb), u[:, nb, :], ps[:, :], t))
    t = g.rstd_of(u, r, act.now(), dve.now())
    g.add_normed(u, vec["norm_g"][:, 40:48], r, t)
    g.barrier()
    mlp(g, 1)


def _fm(w):
    k, n = w.shape
    return np.ascontiguousarray(w.reshape(k // P, P, n // P, P).transpose(1, 2, 0, 3).reshape(P, -1))


def _tm(w):
    k, n = w.shape
    return np.ascontiguousarray(w.reshape(k // P, P, n // 512, 512).transpose(1, 2, 0, 3).reshape(P, -1))


def _vec(v):
    return v.reshape(-1, P).T


def _bucket(rel):
    nb, me = 16, 8
    n = np.abs(rel)
    large = me + (np.log(np.maximum(n, 1) / me) / math.log(1024 / me) * (nb - me)).astype(np.int64)
    return np.where(rel > 0, nb, 0) + np.where(n < me, n, np.minimum(large, nb - 1))


def _constants():
    c = {}
    f = np.float32
    c["ident"] = np.eye(P, dtype=f)
    i = np.arange(P)
    c["tri"] = np.where(i[None, :] <= i[:, None], 0.0, NEG).astype(f)
    c["bd"] = np.kron(np.eye(2), np.ones((64, 64))).astype(f)
    pos = np.arange(S).reshape(QT, P).T[:, :, None]
    end = np.arange(NCMP)[None, None, :] * 16 + 31
    c["cneg"] = np.where(end <= pos, 0.0, NEG).astype(f).reshape(P, -1)
    c["rowvalid"] = (i[:, None] >= 31).astype(f)
    rel = 511 - np.arange(1024)
    c["onehot"] = (_bucket(rel)[None, :] == np.arange(32)[:, None]).astype(f)
    d = 511 - np.arange(896)[None, :] - i[:, None]
    a = np.abs(d)
    count = (a <= 64).astype(int) + ((d % 4 == 0) & (a <= 256)) + (d % 16 == 0)
    c["maskA"] = np.where(count > 0, np.log(np.maximum(count, 1)), NEG).astype(f)
    c["maskB"] = np.where(a <= 128, 0.0, NEG).astype(f)
    s, t = np.arange(CH)[:, None], np.arange(CH)[None, :]
    lv = [(s // n + 1 == t // n) & (s // (2 * n) == t // (2 * n)) for n in (1,) + LEVELS]
    c["levels"] = np.stack([np.stack(lv, 1), np.stack([m.T for m in lv], 1)], 1).astype(f).reshape(CH, -1)
    fw = np.tile(np.concatenate([s < t, s <= t], 1), (2, 1))
    bw = np.tile(np.concatenate([s > t, s >= t], 1), (2, 1))
    c["maskM"] = np.concatenate([fw, bw], 1).astype(f)
    c["starts"] = (np.arange(S) % CH > 0).astype(f).reshape(1, -1)
    return c


def _layout(x):
    a = {n: np.asarray(v) for n, v in x.items()}
    o = _constants()
    o["xT"] = np.ascontiguousarray(a["x"][0].T)
    w = a["w_in"][0]
    cut = np.cumsum([0, 1024, 1024, 1024, 1536, 48, 1024, 1024, 3072])
    u, v, q, kv, gates, xr, rg, mg = (w[:, cut[j]:cut[j + 1]] for j in range(8))
    o["w_v"], o["w_u"], o["w_q"] = _tm(v), _fm(u), _fm(q)
    o["w_kv"] = _fm(np.concatenate([kv[:, 0:768], kv[:, 1024:1280]], 1))
    o["w_vt"] = _tm(np.concatenate([kv[:, 768:1024], kv[:, 1280:1536]], 1))
    o["w_gate"] = np.ascontiguousarray(gates.reshape(NB, P, 48).transpose(1, 0, 2).reshape(P, -1))
    o["wk1"], o["wv1"] = _fm(a["nsa_wk1"][0]), _fm(a["nsa_wv1"][0])
    o["w_cmp2"] = np.ascontiguousarray(np.concatenate(
        [a[n][0].reshape(2, P, 64).transpose(1, 0, 2).reshape(P, -1) for n in ("nsa_wk2", "nsa_wv2")], 1))
    o["w_xr"], o["w_rg"] = _fm(xr), _fm(rg)
    br = [a[n][0] for n in ("w_br_a", "w_br_b", "w_br_c")]
    for nb in range(NB):
        parts = []
        for c in range(3):
            parts.append(_fm(mg[:, c * D + nb * P:c * D + (nb + 1) * P]))
            parts.append(_fm(br[c][:, nb * P:(nb + 1) * P]))
        o[f"w_mb{nb}"] = np.ascontiguousarray(np.concatenate(parts, 1))
    o["w_o"] = _fm(a["w_o"][0])
    fi = a["w_ffn_in"][0]
    o["w_fi"] = _fm(np.stack([fi[:, :DFF].reshape(D, NFF, P), fi[:, DFF:].reshape(D, NFF, P)], 2).reshape(D, -1))
    o["w_fo"] = _fm(a["w_ffn_out"][0])
    w = a["attn_w_in_2"][0]
    o["w_a2"] = _fm(np.concatenate([w[:, 0:512], w[:, 1536:2048], w[:, 512:1024], w[:, 2048:2176], w[:, 2176:2304]], 1))
    o["w_va"] = _tm(w[:, 1024:1536])
    o["w_ao"] = _fm(a["attn_w_out_2"][0])
    for layer in range(2):
        o[f"w_m1{layer}"] = _fm(a["mlp_w1_2"][layer])
        o[f"w_m2{layer}"] = _fm(a["mlp_w2_2"][layer])
    o["rel_table"] = a["rel_table_2"]
    o["sink"] = a["attn_sink_2"].reshape(1, 8)
    o["w_rw"] = _fm(np.concatenate(list(a["rk_w1_2"][0]), 1))
    o["w_ra"] = _fm(np.concatenate(list(a["rk_a1_2"][0]), 1))
    o["w_rg1"] = _fm(np.concatenate(list(a["rk_g1_2"][0]), 1))
    for n, s in (("w_rr", "rk_w_r_2"), ("w_rk", "rk_w_k_2"), ("w_rv", "rk_w_v_2"), ("w_ro", "rk_w_o_2")):
        o[n] = _fm(a[s][0])
    o["rk2"] = np.ascontiguousarray(np.concatenate(
        [a["rk_w2_2"][0].reshape(P, D), a["rk_a2_2"][0].reshape(P, D), a["rk_g2_2"][0, 0], a["rk_g2_2"][0, 1]], 1))
    o["ln_g"], o["ln_b"] = a["gmlp_ln_g"], a["gmlp_ln_b"]
    o["wsT"] = np.ascontiguousarray(a["gmlp_ws"][0].transpose(2, 0, 1).reshape(P, -1))
    o["bs"] = a["gmlp_bs"].reshape(1, -1)
    o["rnn_wa"], o["rnn_wx"] = a["rnn_wa"][0], a["rnn_wx"][0]
    src = {"g_pre_mix": "g_pre_mix", "g_post_mix": "g_post_mix", "g_pre_ffn": "g_pre_ffn", "g_post_ffn": "g_post_ffn",
           "conv_w": "rnn_conv_w", "conv_b": "rnn_conv_b", "rnn_ba": "rnn_ba", "rnn_bx": "rnn_bx",
           "rnn_lam": "rnn_lam", "pe_k": "nsa_pe_k", "pe_v": "nsa_pe_v", "norm_g": "norm_g_2",
           "mu_prev": "rk_mu_prev_2", "mu_next": "rk_mu_next_2", "k_k": "rk_k_k_2", "k_a": "rk_k_a_2",
           "r_k": "rk_r_k_2", "gn_w": "rk_gn_w_2", "gn_b": "rk_gn_b_2", "w0": "rk_w0_2", "a0": "rk_a0_2"}
    o["vecs"] = np.ascontiguousarray(np.concatenate([_vec(a[src[n]]) for n, _ in VECS], 1))
    return o


def kernel(**inputs):
    import concourse.bacc as bacc
    from concourse.bass_utils import run_bass_kernel_spmd

    nc = bacc.Bacc("TRN2", target_bir_lowering=False, num_devices=1)
    arrays = _layout(inputs)
    I = {n: nc.dram_tensor(f"in_{n}", a.shape, mybir.dt.from_np(a.dtype), kind="ExternalInput").ap()
         for n, a in arrays.items()}
    I["scratch"] = nc.dram_tensor("scratch", (16, 1024), F32, kind="Internal").ap()
    out = nc.dram_tensor("out_0", (D, S), F32, kind="ExternalOutput").ap()
    program(nc, I, out)
    r = run_bass_kernel_spmd(nc, [{f"in_{n}": a for n, a in arrays.items()}], core_ids=[0])
    return np.ascontiguousarray(r.results[0]["out_0"].T)[None]
```

```python
import math
from contextlib import ExitStack

import numpy as np

import concourse.bass as bass
from concourse import mybir

F32 = mybir.dt.float32
ALU = mybir.AluOpType
ACT = mybir.ActivationFunctionType
AX = mybir.AxisListType
P = 128
S = 512
D = 1024
NB = D // P
QT = S // P
PIECE = 2048
RING = 4
NEG = -1e30
EPS = 1e-6
GN_EPS = 64e-5
DFF = 2816
NFF = DFF // P
MLP = 4096
NMLP = MLP // P
NH = 16
NCMP = 31
CH = 64
NCH = S // CH
LEVELS = (2, 4, 8, 16, 32)
DECAY = math.exp(-0.5)
ROT = 6
NPT = 5

STREAM = [("w_v", 8192), ("w_u", 8192), ("w_q", 8192), ("w_kv", 8192), ("w_vt", 4096),
          ("wk1", 4096), ("wv1", 4096), ("w_xr", 8192), ("w_rg", 8192)]
STREAM += [(f"w_mb{nb}", 6 * 1024) for nb in range(NB)]
STREAM += [("w_o", 8192), ("w_fi", 2 * NFF * 1024), ("w_fo", NFF * 1024)]
STREAM += [("w_a2", 14 * 1024), ("w_va", 4096), ("w_ao", 8192), ("w_m10", NMLP * 1024), ("w_m20", NMLP * 1024)]
STREAM += [("w_rw", 1024), ("w_ra", 1024), ("w_rg1", 2048), ("w_rr", 8192), ("w_rk", 8192), ("w_rv", 8192),
           ("w_ro", 8192), ("w_m11", NMLP * 1024), ("w_m21", NMLP * 1024)]

VECS = [("g_pre_mix", 8), ("g_post_mix", 8), ("g_pre_ffn", 8), ("g_post_ffn", 8), ("conv_w", 32), ("conv_b", 8),
        ("rnn_ba", 8), ("rnn_bx", 8), ("rnn_lam", 8), ("pe_k", 16), ("pe_v", 16), ("norm_g", 64),
        ("mu_prev", 48), ("mu_next", 48), ("k_k", 8), ("k_a", 8), ("r_k", 8), ("gn_w", 8), ("gn_b", 8),
        ("w0", 16), ("a0", 16)]
NVEC = sum(n for _, n in VECS)


class Engine:

    def __init__(self, sem):
        self.sem, self.count, self.queue, self.met = sem, 0, [], {}

    def wait(self, *tokens):
        for t in tokens:
            if t is None:
                continue
            if isinstance(t, list):
                self.wait(*t)
            elif self.met.get(id(t[0]), 0) < t[1]:
                self.met[id(t[0])] = t[1]
                self.queue.append(lambda e, t=t: e.wait_ge(t[0], t[1]))

    def do(self, fn, *tokens):
        self.wait(*tokens)
        self.count += 1
        self.queue.append(lambda e: fn(e).then_inc(self.sem, 1))
        return (self.sem, self.count)

    def quiet(self, fn, *tokens):
        self.wait(*tokens)
        self.queue.append(fn)

    def dma(self, out, in_, sem, value, *tokens):
        self.wait(*tokens)
        self.queue.append(lambda e: e.dma_start(out, in_).then_inc(sem, 16))
        return (sem, value)

    def now(self):
        return (self.sem, self.count)


class Core:
    pass


def program(nc, I, out):
    with ExitStack() as ctx:
        names = iter(range(10 ** 6))

        def semaphore(name):
            return ctx.enter_context(nc.semaphore(f"{name}{next(names)}"))

        arena = ctx.enter_context(nc.sbuf_tensor("arena", [P, 53200], F32))
        psum = [ctx.enter_context(nc.psum_tensor(f"bank{i}", [P, 512], F32)) for i in range(8)]
        pe, act, dve, pool, sp = (Engine(semaphore(n)) for n in ("pe", "act", "dve", "pool", "sp"))
        top = [0]

        def alloc(n):
            a = arena[:, top[0]:top[0] + n]
            top[0] += n
            assert top[0] <= 53200, top[0]
            return a

        def alloc3(a, b):
            return alloc(a * b).rearrange("p (a b) -> p a b", b=b)

        def barrier():
            tokens = [e.now() for e in (pe, act, dve, pool)]
            for e in (pe, act, dve, pool):
                e.wait(tokens)

        def load(pairs, *tokens):
            s = semaphore("ld")
            for dst, src in pairs:
                pool.dma(dst, src, s, 0, *tokens)
            return (s, 16 * len(pairs))

        ring_t = alloc(RING * PIECE)
        slots = [ring_t[:, i * PIECE:(i + 1) * PIECE] for i in range(RING)]
        slot_sem = [semaphore("w") for _ in range(RING)]
        pieces = []
        for name, total in STREAM:
            for a in range(0, total, PIECE):
                pieces.append((name, a, min(PIECE, total - a)))
        state = {"issued": 0, "at": 0, "off": 0, "freed": 0, "hold": False}

        def issue(token):
            i = state["issued"]
            if i >= len(pieces):
                return
            name, a, n = pieces[i]
            sp.dma(slots[i % RING][:, 0:n], I[name][:, a:a + n], slot_sem[i % RING], 0, token)
            state["issued"] += 1

        def take(name, n):
            i = state["at"]
            assert pieces[i][0] == name and state["off"] + n <= pieces[i][2], (name, pieces[i])
            assert i < state["issued"], "the ring is too small"
            ap = slots[i % RING][:, state["off"]:state["off"] + n]
            token = (slot_sem[i % RING], 16 * (i // RING + 1))
            state["off"] += n
            if state["off"] == pieces[i][2]:
                state["at"] += 1
                state["off"] = 0
            return ap, token

        def release(token):
            while state["freed"] < state["at"] and not state["hold"]:
                issue(token)
                state["freed"] += 1

        def resume():
            state["hold"] = False
            release([e.now() for e in (pe, act, dve, pool)])

        for _ in range(RING):
            issue(None)

        bank_free = [None] * 8
        turn = [0]

        def bank():
            i = turn[0] % ROT
            turn[0] += 1
            return i, psum[i], bank_free[i]

        def mm(out_, lhsT, rhs, start, stop_, last, *tokens):
            if last:
                return pe.do(lambda e: e.matmul(out_, lhsT, rhs, start=start, stop=stop_, skip_group_check=True), *tokens)
            return pe.quiet(lambda e: e.matmul(out_, lhsT, rhs, start=start, stop=stop_, skip_group_check=True), *tokens)

        def tr(out_, in_, ident_, last, *tokens):
            if last:
                return pe.do(lambda e: e.transpose(out_, in_, ident_), *tokens)
            return pe.quiet(lambda e: e.transpose(out_, in_, ident_), *tokens)

        def gemm(name, nblocks, kt, rhs, rhs_token, evac):
            for nb in range(nblocks):
                i, ps, free = bank()
                for k in range(kt):
                    w, wt = take(name, P)
                    t = mm(ps[:, :], w, rhs(k), k == 0, k == kt - 1, k == kt - 1, free, wt, rhs_token)
                release(t)
                bank_free[i] = evac(nb, ps, t)

        vec_t = alloc(NVEC)
        vec, at = {}, 0
        for name, n in VECS:
            vec[name] = vec_t[:, at:at + n]
            at += n
        ident = alloc(P)
        tri = alloc(P)
        ones = alloc(P)
        bd = alloc(P)
        bdm = alloc(P)
        eps = alloc(4)
        c_tok = load([(vec_t, I["vecs"][:, :]), (ident, I["ident"][:, :]), (tri, I["tri"][:, :]), (bd, I["bd"][:, :])])
        k1 = pool.do(lambda e: e.memset(ones, 1.0 / D))
        k2 = pool.do(lambda e: e.memset(eps[:, 0:1], EPS))
        k2 = pool.do(lambda e: e.memset(eps[:, 1:2], GN_EPS))
        k3 = dve.do(lambda e: e.tensor_scalar(bdm, bd, 1.0 / CH, None, ALU.mult), c_tok)
        xT = alloc3(NB, S)
        x_tok = load([(xT, I["xT"].rearrange("(k p) t -> p k t", p=P))])
        base = top[0]
        for e in (pe, act, dve, pool):
            e.wait(c_tok, k1, k2, k3, x_tok)

        def rstd_of(src, dst, *tokens):
            mark = top[0]
            sq = [alloc(S) for _ in range(2)]
            used = [None, None]
            i, ps, free = bank()
            for k in range(NB):
                q = sq[k % 2]
                t = act.do(lambda e, q=q, k=k: e.activation(q, src[:, k, :], ACT.Square), used[k % 2], *tokens)
                used[k % 2] = m = mm(ps[:, :], ones, q, k == 0, k == NB - 1, True, free, t)
            a = act.do(lambda e: e.activation(dst, ps[:, :], ACT.Sqrt, bias=eps[:, 0:1]), m)
            bank_free[i] = a
            top[0] = mark
            return dve.do(lambda e: e.reciprocal(dst, dst), a)

        def normed(src, gain, dst, r, tok):
            for k in range(NB):
                t = dve.do(lambda e, k=k: e.scalar_tensor_tensor(dst[:, k, :], src[:, k, :], gain[:, k:k + 1], r,
                                                                 ALU.mult, ALU.mult), tok)
            return t

        def add_normed(src, gain, r, tok):
            for k in range(NB):
                t = dve.do(lambda e, k=k: e.scalar_tensor_tensor(src[:, k, :], src[:, k, :], gain[:, k:k + 1], r,
                                                                 ALU.mult, ALU.mult), tok)
                t = pool.do(lambda e, k=k: e.tensor_tensor(xT[:, k, :], xT[:, k, :], src[:, k, :], ALU.add), t)
            return t

        def copy(eng, dst, src, *tokens):
            if eng is act:
                return act.do(lambda e: e.activation(dst, src, ACT.Copy), *tokens)
            return eng.do(lambda e: e.tensor_copy(dst, src), *tokens)

        def turns(nb):
            return act if nb % 2 else dve

        def emit():
            with nc.Block() as block:
                for e, reg in ((sp, block.sync), (pool, block.gpsimd), (act, block.scalar),
                               (pe, block.tensor), (dve, block.vector)):
                    def body(eng, e=e):
                        for fn in e.queue:
                            fn(eng)
                    reg(body)

        T = Core()
        T.pe = pe
        T.act = act
        T.dve = dve
        T.pool = pool
        T.sp = sp
        T.vec = vec
        T.I = I
        T.alloc = alloc
        T.alloc3 = alloc3
        T.bank = bank
        T.mm = mm
        T.tr = tr
        T.gemm = gemm
        T.take = take
        T.release = release
        T.resume = resume
        T.ring_t = ring_t
        T.copy = copy
        T.psum = psum
        T.bank_free = bank_free
        T.xT = xT
        T.ident = ident
        T.top = top
        T.rstd_of = rstd_of
        T.normed = normed
        T.add_normed = add_normed
        T.load = load
        T.barrier = barrier
        T.state = state
        T.eps = eps
        T.tri = tri
        T.turns = turns
        T.base = base
        T.semaphore = semaphore
        T.bd = bd
        T.bdm = bdm
        T.ones = ones
        layer1(T)
        attention2(T)
        rwkv(T)
        t = [pe.now(), act.now(), dve.now(), pool.now()]
        s = semaphore("out")
        sp.dma(out.rearrange("(k p) t -> p k t", p=P), xT, s, 16, t)
        sp.wait((s, 16))
        assert state["at"] == len(pieces)
        emit()


def layer1(g):
    pe, act, dve, pool, vec, I = g.pe, g.act, g.dve, g.pool, g.vec, g.I
    alloc, alloc3, bank, mm, tr, gemm, take, release = g.alloc, g.alloc3, g.bank, g.mm, g.tr, g.gemm, g.take, g.release
    copy, psum, bank_free, xT, ident, top = g.copy, g.psum, g.bank_free, g.xT, g.ident, g.top

    yA, yB, yC = alloc3(NB, S), alloc3(NB, S), alloc3(NB, S)
    hT = alloc3(NB, S)
    r = alloc(S)
    work = top[0]
    t = g.rstd_of(xT, r)
    h_tok = g.normed(xT, vec["g_pre_mix"], hT, r, t)

    V = alloc3(QT, D)
    lng, lnb = alloc(D), alloc(D)
    wsT = alloc3(4, P)
    bsB = alloc3(4, P)
    sums = alloc(QT * 2)
    st = alloc(QT * 4).rearrange("p (a b) -> p a b", b=4)
    sqs = yA[:, 0:2, :].rearrange("p a b -> p (a b)")
    l_tok = g.load([(lng, I["ln_g"][0, :].partition_broadcast(P)), (lnb, I["ln_b"][0, :].partition_broadcast(P)),
                    (wsT, I["wsT"].rearrange("p (a b) -> p a b", b=P)), (bsB, I["bs"][0, :].partition_broadcast(P).rearrange("p (a b) -> p a b", b=P))])
    w_tok = pool.do(lambda e: e.affine_select(out=wsT, in_=wsT, compare_op=ALU.is_ge, fill=0.0, base=0,
                                              pattern=[[0, 4], [1, P]], channel_multiplier=-1), l_tok)
    for half in range(2):
        ws = [take("w_v", 512) for _ in range(NB)]
        for qt in range(QT):
            i, ps, free = bank()
            for k in range(NB):
                t = mm(ps[:, :], hT[:, k, qt * P:(qt + 1) * P], ws[k][0], k == 0, k == NB - 1, k == NB - 1,
                       free, ws[k][1], h_tok)
            bank_free[i] = act.do(lambda e, ps=ps, qt=qt, half=half: e.activation(
                V[:, qt, half * 512:half * 512 + 512], ps[:, :], ACT.Gelu_apprx_tanh,
                accum_out=sums[:, 2 * qt + half:2 * qt + half + 1]), t)
        release(t)
    v_tok = act.now()

    def ln(qt):
        a = dve.do(lambda e: e.tensor_tensor(st[:, qt, 0:1], sums[:, 2 * qt:2 * qt + 1], sums[:, 2 * qt + 1:2 * qt + 2], ALU.add), v_tok)
        a = dve.do(lambda e: e.tensor_scalar(st[:, qt, 0:1], st[:, qt, 0:1], 1.0 / D, None, ALU.mult), a)
        a = dve.do(lambda e: e.tensor_scalar(V[:, qt, :], V[:, qt, :], st[:, qt, 0:1], None, ALU.subtract), a)
        b = act.do(lambda e: e.activation(sqs, V[:, qt, :], ACT.Square, accum_out=st[:, qt, 1:2]), a)
        b = act.do(lambda e: e.activation(st[:, qt, 2:3], st[:, qt, 1:2], ACT.Sqrt, scale=1.0 / D, bias=g.eps[:, 0:1]), b)
        b = dve.do(lambda e: e.reciprocal(st[:, qt, 3:4], st[:, qt, 2:3]), b)
        b = dve.do(lambda e: e.scalar_tensor_tensor(V[:, qt, :], V[:, qt, :], st[:, qt, 3:4], lng, ALU.mult, ALU.mult), b, l_tok)
        return dve.do(lambda e: e.tensor_tensor(V[:, qt, :], V[:, qt, :], lnb, ALU.add), b)

    ln_tok = [ln(qt) for qt in range(QT)]
    uT = alloc3(NB, S)
    gemm("w_u", NB, NB, lambda k: hT[:, k, :], h_tok,
         lambda nb, ps, t: act.do(lambda e: e.activation(uT[:, nb, :], ps[:, :], ACT.Gelu_apprx_tanh), t))
    u_tok = act.now()
    for fb in range(NB):
        i, ps, free = bank()
        for n in range(QT):
            t = mm(ps[:, n * P:(n + 1) * P], V[:, n, fb * P:(fb + 1) * P], wsT[:, fb // 2, :], True, True, n == QT - 1,
                   free, ln_tok, w_tok)
        a = dve.do(lambda e, fb=fb, ps=ps: e.tensor_tensor(
            yA[:, fb, :].rearrange("p (n t) -> p n t", t=P), ps[:, :].rearrange("p (n t) -> p n t", t=P),
            bsB[:, fb // 2, :].unsqueeze(1).broadcast_to((P, QT, P)), ALU.add), t, u_tok)
        bank_free[i] = a
        dve.do(lambda e, fb=fb: e.tensor_tensor(yA[:, fb, :], yA[:, fb, :], uT[:, fb, :], ALU.mult), a)
    g.barrier()

    top[0] = work
    qT = alloc3(NB, S)
    ks, kw = (alloc(8 * S).rearrange("p (h g s) -> p h g s", h=2, g=4) for _ in range(2))
    for q in (ks, kw):
        z_tok = pool.do(lambda e, q=q: e.memset(q[0:64, 1], 0.0))
        z_tok = pool.do(lambda e, q=q: e.memset(q[64:128, 0], 0.0))
    kc2, vc2 = yC[:, 0:4, :], yC[:, 4:8, :]
    VV = alloc3(QT, S)
    gat = alloc3(QT, 48)
    gw = alloc(NB * 48)
    gw_tok = g.load([(gw, I["w_gate"][:, :])])
    gemm("w_q", NB, NB, lambda k: hT[:, k, :], h_tok,
         lambda nb, ps, t: (act.do(lambda e: e.activation(qT[:, nb, :], ps[:, :], ACT.Copy, scale=0.125), t) if nb % 2 else
                            dve.do(lambda e: e.tensor_scalar(qT[:, nb, :], ps[:, :], 0.125, None, ALU.mult), t)))

    def kv_evac(nb, ps, t):
        eng = act if nb % 2 else dve
        what, half = nb // 2, nb % 2
        for gi in range(2):
            grp = 2 * half + gi
            src = ps[64 * gi:64 * gi + 64, :]
            if what < 2:
                dst = (kc2, vc2)[what]
                t2 = copy(eng, dst[0:64, grp, :], src, t)
                t2 = copy(eng, dst[64:128, grp, 0:S - 1], src[:, 1:S], t)
            else:
                dst = (ks, kw)[what - 2]
                t2 = copy(eng, dst[0:64, 0, grp, :], src, t)
                t2 = copy(eng, dst[64:128, 1, grp, :], src, t)
        return t2

    gemm("w_kv", 8, NB, lambda k: hT[:, k, :], h_tok, kv_evac)
    ws = [take("w_vt", 512) for _ in range(NB)]
    for qt in range(QT):
        i, ps, free = bank()
        for k in range(NB):
            t = mm(ps[:, :], hT[:, k, qt * P:(qt + 1) * P], ws[k][0], k == 0, k == NB - 1, k == NB - 1, free, ws[k][1])
        bank_free[i] = copy(g.turns(qt), VV[:, qt, :], ps[:, :], t)
    release(t)
    i, ps, free = bank()
    for qt in range(QT):
        for k in range(NB):
            t = mm(ps[:, qt * 48:qt * 48 + 48], hT[:, k, qt * P:(qt + 1) * P], gw[:, k * 48:k * 48 + 48], k == 0,
                   k == NB - 1, k == NB - 1, free, gw_tok)
    bank_free[i] = act.do(lambda e, ps=ps: e.activation(gat, ps[:, 0:192].rearrange("p (a b) -> p a b", b=48), ACT.Sigmoid), t)
    kv_tok = [act.now(), dve.now()]

    hid = alloc3(4, P)
    peb = alloc(4)
    kc = alloc(4 * NCMP)
    vcS = alloc3(4, 64)
    w2 = alloc(4 * 64).rearrange("p (a b c) -> p a b c", a=2, b=2)
    w2_tok = g.load([(w2, I["w_cmp2"].rearrange("p (a b c) -> p a b c", a=2, b=2))])
    for kind in range(2):
        src = (kc2, vc2)[kind]
        for hb in range(2):
            us = [take(("wk1", "wv1")[kind], P) for _ in range(16)]
            i, ps, free = bank()
            for j in range(16):
                mm(ps[:, 0:124].rearrange("p (a b) -> p a b", b=NCMP), us[j][0], src[:, :, 2 * j:2 * j + 481:16], j == 0,
                   j == 15, False, free, us[j][1], kv_tok)
            pv = vec[("pe_k", "pe_v")[kind]]
            for j in range(16):
                t = mm(ps[:, 128:129], us[j][0], pv[:, j:j + 1], j == 0, j == 15, j == 15)
            release(t)
            c = 2 * kind + hb
            a = act.do(lambda e, ps=ps, c=c: e.activation(peb[:, c:c + 1], ps[:, 128:129], ACT.Copy), t)
            bank_free[i] = act.do(lambda e, ps=ps, c=c: e.activation(hid[:, c, 0:124], ps[:, 0:124], ACT.Gelu_apprx_tanh,
                                                                     bias=peb[:, c:c + 1]), a)
    h2 = act.now()
    i, ps, free = bank()
    for hb in range(2):
        t = mm(ps[0:64, 0:124], w2[:, 0, hb, :], hid[:, hb, 0:124], hb == 0, hb == 1, hb == 1, free, h2, w2_tok)
    copy(dve, kc[0:64, :], ps[0:64, 0:124], t)
    bank_free[i] = copy(dve, kc[64:128, :], ps[0:64, 0:124], t)
    i, ps, free = bank()
    for grp in range(4):
        for hb in range(2):
            t = mm(ps[0:NCMP, grp * 64:grp * 64 + 64], hid[:, 2 + hb, grp * NCMP:(grp + 1) * NCMP], w2[:, 1, hb, :],
                   hb == 0, hb == 1, hb == 1, free)
    bank_free[i] = kc_tok = copy(dve, vcS[0:NCMP, :, :], ps[0:NCMP, 0:256].rearrange("p (a b) -> p a b", b=64), t)

    cneg = alloc(QT * NCMP).rearrange("p (a b) -> p a b", b=NCMP)
    rv = alloc(1)
    Pc = yC[:, 0:4, :].rearrange("p a b -> p (a b)")[:, 0:QT * 16 * NCMP].rearrange("p (q h n) -> p q h n", q=QT, n=NCMP)
    sm = alloc(3 * 8).rearrange("p (a b) -> p a b", b=8)
    cn_tok = g.load([(cneg, I["cneg"].rearrange("p (a b) -> p a b", b=NCMP)), (rv, I["rowvalid"][:, :])])
    g.barrier()
    gv = gat.rearrange("p q (h c) -> p q h c", c=3)
    for qt in range(QT):
        for par in range(2):
            i, ps, free = bank()
            for hh in range(8):
                h = 2 * hh + par
                b0 = 64 * par
                t = mm(ps[:, hh * NCMP:(hh + 1) * NCMP], qT[b0:b0 + 64, hh, qt * P:(qt + 1) * P],
                       kc[b0:b0 + 64, (h // 4) * NCMP:(h // 4 + 1) * NCMP], True, True, hh == 7, free, kc_tok)
            pc = Pc[:, qt, par::2, :]
            a = dve.do(lambda e, ps=ps, qt=qt, pc=pc: e.tensor_tensor(
                pc, ps[:, 0:8 * NCMP].rearrange("p (a b) -> p a b", b=NCMP),
                cneg[:, qt, :].unsqueeze(1).broadcast_to((P, 8, NCMP)), ALU.add), t, cn_tok)
            bank_free[i] = a
            a = dve.do(lambda e, pc=pc: e.tensor_reduce(sm[:, 0, :], pc, AX.X, ALU.max), a)
            a = dve.do(lambda e, pc=pc: e.tensor_tensor(pc, pc, sm[:, 0, :].unsqueeze(2).broadcast_to((P, 8, NCMP)), ALU.subtract), a)
            b = act.do(lambda e, pc=pc: e.activation(pc, pc, ACT.Exp), a)
            a = dve.do(lambda e, pc=pc: e.tensor_reduce(sm[:, 1, :], pc, AX.X, ALU.add), b)
            a = dve.do(lambda e: e.reciprocal(sm[:, 2, :], sm[:, 1, :]), a)
            a = dve.do(lambda e, qt=qt, par=par: e.tensor_tensor(sm[:, 2, :], sm[:, 2, :], gv[:, qt, par::2, 0], ALU.mult), a)
            if qt == 0:
                a = dve.do(lambda e: e.tensor_scalar(sm[:, 2, :], sm[:, 2, :], rv, None, ALU.mult), a)
            pc_tok = dve.do(lambda e, pc=pc: e.tensor_tensor(pc, pc, sm[:, 2, :].unsqueeze(2).broadcast_to((P, 8, NCMP)), ALU.mult), a)

    Pb = [alloc3(QT, S) for _ in range(2)]
    Pb_free = [None, None]
    PT = [alloc(S) for _ in range(NPT)]
    PT_free = [None] * NPT
    nm = alloc3(2, 4 * QT)
    n_pt = [0]

    def scores(h, br, buf):
        K = (ks, kw)[br][:, h % 2, h // 4, :]
        tiles = []
        for qt in range(QT):
            n = (qt + 1) * P
            i, ps, free = bank()
            t = mm(ps[:, 0:n], qT[:, h // 2, qt * P:(qt + 1) * P], K[:, 0:n], True, True, True, free)
            tiles.append((qt, n, i, ps, t, nm[:, buf, 4 * qt:4 * qt + 4]))
        maxima = []
        for qt, n, i, ps, t, m in tiles:
            dve.do(lambda e, ps=ps, qt=qt: e.tensor_tensor(ps[:, qt * P:(qt + 1) * P], ps[:, qt * P:(qt + 1) * P],
                                                           g.tri, ALU.add), t)
            dve.wait(dve.now(), Pb_free[buf])
            maxima.append(dve.do(lambda e, ps=ps, n=n, m=m: e.tensor_reduce(m[:, 0:1], ps[:, 0:n], AX.X, ALU.max, negate=True)))
        done = []
        for (qt, n, i, ps, t, m), a in zip(tiles, maxima):
            bank_free[i] = b = act.do(lambda e, ps=ps, n=n, m=m, qt=qt: e.activation(
                Pb[buf][:, qt, 0:n], ps[:, 0:n], ACT.Exp, bias=m[:, 0:1], accum_out=m[:, 1:2]), a)
            done.append(b)
        return done

    def weights(h, br, buf, done):
        m = nm[:, buf, :].rearrange("p (q c) -> p q c", c=4)
        a = dve.do(lambda e: e.reciprocal(m[:, :, 2:3], m[:, :, 1:2]), done)
        a = dve.do(lambda e: e.tensor_tensor(m[:, :, 3:4], m[:, :, 2:3], gv[:, :, h, 1 + br:2 + br], ALU.mult), a)
        out = []
        for qt in range(QT):
            n = (qt + 1) * P
            out.append(dve.do(lambda e, n=n, qt=qt: e.tensor_scalar(Pb[buf][:, qt, 0:n], Pb[buf][:, qt, 0:n], m[:, qt, 3:4], None,
                                                                    ALU.mult), a))
        return out

    def values(h, br, buf, tok, o):
        grp, b0 = h // 4, 64 * (h % 2)
        tiles = []
        for kt in range(QT):
            i, ps, free = bank()
            for qt in range(kt, QT):
                t = tr(ps[:, qt * P:(qt + 1) * P], Pb[buf][:, qt, kt * P:(kt + 1) * P], ident, qt == QT - 1, free, tok)
            j = n_pt[0] % NPT
            n_pt[0] += 1
            bank_free[i] = c = copy(act if kt % 2 else dve, PT[j][:, kt * P:S], ps[:, kt * P:S], t, PT_free[j])
            tiles.append((kt, j, c))
        Pb_free[buf] = t
        for kt, j, c in tiles:
            PT_free[j] = last = mm(o[b0:b0 + 64, kt * P:S], VV[:, kt, br * 256 + grp * 64:br * 256 + grp * 64 + 64],
                                   PT[j][:, kt * P:S], False, kt == QT - 1 and br == 1, True, c)
        return last

    def compressed(h, o, free_o):
        b0 = 64 * (h % 2)
        i, ps, free = bank()
        for qt in range(QT):
            t = tr(ps[0:NCMP, qt * P:(qt + 1) * P], Pc[:, qt, h, :], ident, qt == QT - 1, free, pc_tok)
        j = n_pt[0] % NPT
        n_pt[0] += 1
        bank_free[i] = c = copy(dve, PT[j][0:NCMP, :], ps[0:NCMP, :], t, PT_free[j])
        PT_free[j] = mm(o[b0:b0 + 64, :], vcS[0:NCMP, h // 4, :], PT[j][0:NCMP, :], True, False, True, c, free_o)

    jobs = [(h, br) for h in range(NH) for br in range(2)]
    ready = weights(*jobs[0], 0, scores(*jobs[0], 0))
    o_free = [None, None]
    for n, (h, br) in enumerate(jobs):
        more = n + 1 < len(jobs)
        nxt = scores(*jobs[n + 1], (n + 1) % 2) if more else None
        ob = (h // 2) % 2
        o = psum[6 + ob]
        if br == 0:
            compressed(h, o, o_free[ob] if h % 2 == 0 else None)
        last = values(h, br, n % 2, ready, o)
        if h % 2 == 1 and br == 1:
            o_free[ob] = copy(act, yB[:, h // 2, :], o[:, :], last)
        ready = weights(*jobs[n + 1], (n + 1) % 2, nxt) if more else None
    g.barrier()

    top[0] = work
    xc, rr, ii, gl = (alloc3(NB, S) for _ in range(4))
    bda, bdx = alloc3(NB, P), alloc3(NB, P)
    xs = [alloc(S + 3) for _ in range(2)]
    xs_free = [None, None]
    c8 = alloc(NB)
    z = pool.do(lambda e: e.memset(bda, 0.0))
    z = pool.do(lambda e: e.memset(bdx, 0.0), z)
    for q in xs:
        z = pool.do(lambda e, q=q: e.memset(q[:, 0:3], 0.0))
    pairs = []
    for dst, name in ((bda, "rnn_wa"), (bdx, "rnn_wx")):
        for par in range(2):
            pairs.append((dst[64 * par:64 * par + 64, :, 64 * par:64 * par + 64],
                          I[name][par::2, :, :].rearrange("h i o -> i h o")))
    bd_tok = g.load(pairs, z)
    sp_t = alloc3(6, NB)
    ab, ee, zz, z2, ac, mx = (sp_t[:, j, :] for j in range(6))
    lam = vec["rnn_lam"]
    a = dve.do(lambda e: e.tensor_scalar(ab, lam, -1.0, None, ALU.mult))
    a = dve.do(lambda e: e.tensor_tensor(ab, ab, lam, ALU.min), a)
    m0 = dve.do(lambda e: e.tensor_scalar(mx, lam, -1.0, 0.0, ALU.mult, ALU.max), a)
    b = act.do(lambda e: e.activation(ee, ab, ACT.Exp), a)
    a = dve.do(lambda e: e.tensor_scalar(zz, ee, 2.0, None, ALU.add), b)
    a = dve.do(lambda e: e.reciprocal(zz, zz), a)
    a = dve.do(lambda e: e.tensor_tensor(zz, zz, ee, ALU.mult), a)
    a = dve.do(lambda e: e.tensor_tensor(z2, zz, zz, ALU.mult), a)
    a = dve.do(lambda e: e.tensor_scalar(ac, z2, 1.0 / 15, 1.0 / 13, ALU.mult, ALU.add), a)
    for n in (11, 9, 7, 5, 3, 1):
        a = dve.do(lambda e: e.tensor_tensor(ac, ac, z2, ALU.mult), a)
        a = dve.do(lambda e, n=n: e.tensor_scalar(ac, ac, 1.0 / n, None, ALU.add), a)
    a = dve.do(lambda e: e.tensor_tensor(ac, ac, zz, ALU.mult), a)
    a = dve.do(lambda e: e.scalar_tensor_tensor(ac, ac, 2.0, mx, ALU.mult, ALU.add), a, m0)
    c8_tok = dve.do(lambda e: e.tensor_scalar(c8, ac, -8.0, None, ALU.mult), a)

    cw, cb = vec["conv_w"], vec["conv_b"]
    xc_tok = [None] * NB

    def conv(nb, ps, t):
        q = xs[nb % 2]
        a = act.do(lambda e: e.activation(q[:, 3:S + 3], ps[:, :], ACT.Copy), t, xs_free[nb % 2], z)
        b = dve.do(lambda e: e.tensor_scalar(xc[:, nb, :], q[:, 3:S + 3], cw[:, 24 + nb:25 + nb], cb[:, nb:nb + 1], ALU.mult, ALU.add), a)
        for j in (2, 1, 0):
            b = dve.do(lambda e, j=j: e.scalar_tensor_tensor(xc[:, nb, :], q[:, j:j + S], cw[:, 8 * j + nb:8 * j + nb + 1], xc[:, nb, :],
                                                             ALU.mult, ALU.add), b)
        xs_free[nb % 2] = xc_tok[nb] = b
        return a

    gemm("w_xr", NB, NB, lambda k: hT[:, k, :], h_tok, conv)
    gemm("w_rg", NB, NB, lambda k: hT[:, k, :], h_tok,
         lambda nb, ps, t: act.do(lambda e: e.activation(gl[:, nb, :], ps[:, :], ACT.Gelu_apprx_tanh), t))
    for nb in range(NB):
        for w, dst, bias in ((bda, rr, "rnn_ba"), (bdx, ii, "rnn_bx")):
            i, ps, free = bank()
            t = mm(ps[:, :], w[:, nb, :], xc[:, nb, :], True, True, True, free, bd_tok, xc_tok[nb])
            bank_free[i] = act.do(lambda e, ps=ps, dst=dst, bias=bias, nb=nb: e.activation(
                dst[:, nb, :], ps[:, :], ACT.Sigmoid, bias=vec[bias][:, nb:nb + 1]), t)
    tk = [None] * NB
    ta = [None] * NB
    for nb in range(NB):
        a = dve.do(lambda e, nb=nb: e.tensor_tensor(xc[:, nb, :], xc[:, nb, :], ii[:, nb, :], ALU.mult), act.now() if nb == 0 else None)
        b = act.do(lambda e, nb=nb: e.activation(ii[:, nb, :], rr[:, nb, :], ACT.Tanh, scale=c8[:, nb:nb + 1]), a, c8_tok)
        b = ta[nb] = act.do(lambda e, nb=nb: e.activation(rr[:, nb, :], rr[:, nb, :], ACT.Exp, scale=c8[:, nb:nb + 1]), b)
        yc = yC[:, nb, :]
        a = dve.do(lambda e, nb=nb, yc=yc: e.tensor_tensor(yc, rr[:, nb, :], rr[:, nb, :], ALU.mult), b)
        tk[nb] = dve.do(lambda e, nb=nb, yc=yc: e.scalar_tensor_tensor(ii[:, nb, :], yc, 1.0, ii[:, nb, :], ALU.add, ALU.mult), a)
    for nb in range(NB):
        b = act.do(lambda e, nb=nb: e.activation(ii[:, nb, :], ii[:, nb, :], ACT.Sqrt, scale=-1.0), tk[nb])
        a = dve.do(lambda e, nb=nb: e.tensor_tensor(xc[:, nb, :], xc[:, nb, :], ii[:, nb, :], ALU.mult), b)
        a = dve.do(lambda e, nb=nb: e.tensor_tensor_scan(yC[:, nb, :], rr[:, nb, :], xc[:, nb, :], 0.0, ALU.mult, ALU.add), a)
        dve.do(lambda e, nb=nb: e.tensor_tensor(yC[:, nb, :], yC[:, nb, :], gl[:, nb, :], ALU.mult), a)
    g.barrier()

    top[0] = work
    mg, mo = alloc3(NB, S), alloc3(NB, S)
    gt = [alloc(S) for _ in range(3)]
    gt_free = [None] * 3
    tt = alloc(S)
    n = 0
    for nb in range(NB):
        for c in range(3):
            i, ps, free = bank()
            for k in range(NB):
                w, wt = take(f"w_mb{nb}", P)
                t = mm(ps[:, :], w, hT[:, k, :], k == 0, k == NB - 1, k == NB - 1, free, wt)
            release(t)
            q = gt[n % 3]
            bank_free[i] = s = act.do(lambda e, ps=ps, q=q: e.activation(q, ps[:, :], ACT.Sigmoid), t, gt_free[n % 3])
            i, ps, free = bank()
            for k in range(NB):
                w, wt = take(f"w_mb{nb}", P)
                t = mm(ps[:, :], w, (yA, yB, yC)[c][:, k, :], k == 0, k == NB - 1, k == NB - 1, free, wt)
            release(t)
            if c == 0:
                a = dve.do(lambda e, ps=ps, q=q, nb=nb: e.tensor_tensor(mg[:, nb, :], ps[:, :], q, ALU.mult), t, s)
                bank_free[i] = a
            else:
                b = dve.do(lambda e, ps=ps, q=q: e.tensor_tensor(tt, ps[:, :], q, ALU.mult), t, s, a)
                bank_free[i] = b
                a = dve.do(lambda e, nb=nb: e.tensor_tensor(mg[:, nb, :], mg[:, nb, :], tt, ALU.add), b)
            gt_free[n % 3] = a
            n += 1
    m_tok = dve.now()
    gemm("w_o", NB, NB, lambda k: mg[:, k, :], m_tok, lambda nb, ps, t: copy(g.turns(nb), mo[:, nb, :], ps[:, :], t))
    t = g.rstd_of(mo, r, act.now(), dve.now())
    x_tok = g.add_normed(mo, vec["g_post_mix"], r, t)
    g.barrier()

    top[0] = g.base
    hf, fo = alloc3(NB, S), alloc3(NB, S)
    pr = alloc3(NFF, S)
    r = alloc(S)
    sg = [alloc(S) for _ in range(2)]
    sg_free = [None, None]
    t = g.rstd_of(xT, r)
    h_tok = g.normed(xT, vec["g_pre_ffn"], hf, r, t)
    for nb in range(NFF):
        two = []
        for _ in range(2):
            i, ps, free = bank()
            for k in range(NB):
                w, wt = take("w_fi", P)
                t = mm(ps[:, :], w, hf[:, k, :], k == 0, k == NB - 1, k == NB - 1, free, wt, h_tok)
            release(t)
            two.append((i, ps, t))
        q = sg[nb % 2]
        bank_free[two[0][0]] = s = act.do(lambda e, ps=two[0][1], q=q: e.activation(q, ps[:, :], ACT.Silu), two[0][2], sg_free[nb % 2])
        bank_free[two[1][0]] = sg_free[nb % 2] = dve.do(
            lambda e, ps=two[1][1], q=q, nb=nb: e.tensor_tensor(pr[:, nb, :], ps[:, :], q, ALU.mult), two[1][2], s)
    f_tok = dve.now()
    gemm("w_fo", NB, NFF, lambda k: pr[:, k, :], f_tok, lambda nb, ps, t: copy(g.turns(nb), fo[:, nb, :], ps[:, :], t))
    t = g.rstd_of(fo, r, act.now(), dve.now())
    g.add_normed(fo, vec["g_post_ffn"], r, t)
    g.barrier()


def mlp(g, layer):
    act, dve, pool = g.act, g.dve, g.pool
    g.top[0] = g.base
    hf = g.alloc3(NB, S)
    hid = g.alloc3(NMLP, S)
    r = g.alloc(S)
    t = g.rstd_of(g.xT, r)
    gain = g.vec["norm_g"]
    h_tok = g.normed(g.xT, gain[:, 32 * layer + 16:32 * layer + 24], hf, r, t)
    relu = [g.alloc(S) for _ in range(2)]
    relu_free = [None, None]

    def evac(nb, ps, t):
        q = relu[nb % 2]
        a = act.do(lambda e: e.activation(q, ps[:, :], ACT.Relu), t, relu_free[nb % 2])
        relu_free[nb % 2] = dve.do(lambda e: e.tensor_tensor(hid[:, nb, :], q, q, ALU.mult), a)
        return a

    g.gemm(f"w_m1{layer}", NMLP, NB, lambda k: hf[:, k, :], h_tok, evac)
    m_tok = dve.now()
    pe_tok = g.pe.now()
    fo = hf
    g.gemm(f"w_m2{layer}", NB, NMLP, lambda k: hid[:, k, :], m_tok,
           lambda nb, ps, t: g.copy(g.turns(nb), fo[:, nb, :], ps[:, :], t, pe_tok))
    t = g.rstd_of(fo, r, act.now(), dve.now())
    g.add_normed(fo, gain[:, 32 * layer + 24:32 * layer + 32], r, t)


def attention2(g):
    pe, act, dve, pool, vec, I = g.pe, g.act, g.dve, g.pool, g.vec, g.I
    alloc, alloc3, bank, mm, tr, gemm, take, release = g.alloc, g.alloc3, g.bank, g.mm, g.tr, g.gemm, g.take, g.release
    copy, psum, bank_free, xT, ident, top = g.copy, g.psum, g.bank_free, g.xT, g.ident, g.top
    top[0] = g.base
    hT = alloc3(NB, S)
    r = alloc(S)
    oT = alloc3(NB, S)
    qT = alloc3(NB, S)
    kT = alloc(8 * S).rearrange("p (h g s) -> p h g s", h=2, g=4)
    kb = alloc(4 * S).rearrange("p (h g s) -> p h g s", h=2, g=2)
    for q in (kT, kb):
        pool.do(lambda e, q=q: e.memset(q[0:64, 1], 0.0))
        pool.do(lambda e, q=q: e.memset(q[64:128, 0], 0.0))
    VA = alloc3(QT, S)
    VB = alloc3(QT, P)
    sink = alloc(8)
    mark = top[0]
    oh, tab = alloc(1024), alloc(16)
    bv = alloc(1024)
    ld = g.load([(oh[0:32, :], I["onehot"][:, :]), (tab[0:32, :], I["rel_table"][:, :]),
                 (sink, I["sink"][0, :].partition_broadcast(P))])
    for half in range(2):
        i, ps, free = bank()
        t = mm(ps[0:16, :], tab[0:32, :], oh[0:32, half * 512:half * 512 + 512], True, True, True, free, ld)
        bank_free[i] = b_tok = copy(dve, bv[0:16, half * 512:half * 512 + 512], ps[0:16, :], t)
    s_b = g.semaphore("bv")
    pool.dma(I["scratch"][:, :], bv[0:16, :], s_b, 16, b_tok)
    bv_tok = (s_b, 16)

    t = g.rstd_of(xT, r)
    h_tok = g.normed(xT, vec["norm_g"][:, 0:8], hT, r, t)

    def evac(nb, ps, t):
        eng = act if nb % 2 else dve
        if nb < 8:
            return (act.do(lambda e: e.activation(qT[:, nb, :], ps[:, :], ACT.Copy, scale=0.125), t) if nb % 2 else
                    dve.do(lambda e: e.tensor_scalar(qT[:, nb, :], ps[:, :], 0.125, None, ALU.mult), t))
        if nb < 12:
            copy(eng, kT[0:64, 0, nb - 8, :], ps[0:64, :], t)
            return copy(eng, kT[64:128, 1, nb - 8, :], ps[64:128, :], t)
        for gi in range(2):
            for c in range(2):
                t2 = copy(eng, kb[64 * c:64 * c + 64, c, gi, :], ps[64 * gi:64 * gi + 64, :], t)
        return t2

    gemm("w_a2", 13, NB, lambda k: hT[:, k, :], h_tok, evac)
    vbw = [take("w_a2", P) for _ in range(NB)]
    i, ps, free = bank()
    for qt in range(QT):
        for k in range(NB):
            t = mm(ps[:, qt * P:(qt + 1) * P], hT[:, k, qt * P:(qt + 1) * P], vbw[k][0], k == 0, k == NB - 1,
                   k == NB - 1, free, vbw[k][1])
    release(t)
    bank_free[i] = copy(dve, VB, ps[:, :].rearrange("p (a b) -> p a b", b=P), t)
    ws = [take("w_va", 512) for _ in range(NB)]
    for qt in range(QT):
        i, ps, free = bank()
        for k in range(NB):
            t = mm(ps[:, :], hT[:, k, qt * P:(qt + 1) * P], ws[k][0], k == 0, k == NB - 1, k == NB - 1, free, ws[k][1])
        bank_free[i] = copy(g.turns(qt), VA[:, qt, :], ps[:, :], t)
    release(t)
    g.barrier()
    top[0] = mark

    BT = [alloc(896) for _ in range(2)]
    BT_free = [None, None]
    bt_sem = [g.semaphore("bt") for _ in range(2)]
    mA, mB = alloc(896), alloc(896)
    mk = g.load([(mA, I["maskA"][:, :]), (mB, I["maskB"][:, :])], bv_tok)
    Pb = [alloc3(QT, S) for _ in range(2)]
    Pb_free = [None, None]
    PT = [alloc(S) for _ in range(NPT)]
    PT_free = [None] * NPT
    nm = alloc3(2, 8 * QT)
    n_pt = [0]

    def keys(h, qt):
        return (0, S) if h < 8 else (max(0, (qt - 1) * P), min(S, (qt + 2) * P))

    def bias(h):
        b = BT[h % 2]
        sc = I["scratch"]
        src = bass.AP(tensor=sc.tensor, offset=sc.offset + h * 1024, ap=[[1, P], [1, 896]])
        pool.dma(b, src, bt_sem[h % 2], 0, BT_free[h % 2], bv_tok)
        return pool.do(lambda e: e.tensor_tensor(b, b, mA if h < 8 else mB, ALU.add), (bt_sem[h % 2], 16 * (h // 2 + 1)), mk)

    bias_tok = [None] * 18
    bias_tok[0] = bias(0)

    def scores(h, buf):
        K = kT[:, h % 2, h // 2, :] if h < 8 else kb[:, h % 2, (h - 8) // 4, :]
        m = nm[:, buf, :].rearrange("p (c q) -> p c q", q=QT)
        tiles = []
        for qt in range(QT):
            a0, a1 = keys(h, qt)
            i, ps, free = bank()
            t = mm(ps[:, 0:a1 - a0], qT[:, h // 2, qt * P:(qt + 1) * P], K[:, a0:a1], True, True, True, free)
            tiles.append((qt, a1 - a0, 384 - qt * P + a0, i, ps, t, Pb[buf][:, qt, a0:a1]))
        for qt, n, off, i, ps, t, pb in tiles:
            bank_free[i] = a = dve.do(lambda e, ps=ps, n=n, off=off, pb=pb: e.tensor_tensor(
                pb, ps[:, 0:n], BT[h % 2][:, 896 - off - n:896 - off][:, ::-1], ALU.add), t, bias_tok[h], Pb_free[buf])
            a = dve.do(lambda e, pb=pb, qt=qt: e.tensor_reduce(m[:, 0, qt:qt + 1], pb, AX.X, ALU.max), a)
        BT_free[h % 2] = a
        if h >= 8:
            a = dve.do(lambda e: e.tensor_tensor(m[:, 0, :], m[:, 0, :], sink[:, h - 8:h - 7].broadcast_to((P, QT)), ALU.max), a, ld)
        a = dve.do(lambda e: e.tensor_scalar(m[:, 1, :], m[:, 0, :], -1.0, None, ALU.mult), a)
        for qt, n, off, i, ps, t, pb in tiles:
            b = act.do(lambda e, pb=pb, qt=qt: e.activation(pb, pb, ACT.Exp, bias=m[:, 1, qt:qt + 1], accum_out=m[:, 2, qt:qt + 1]), a)
        if h >= 8:
            b = act.do(lambda e: e.activation(m[:, 3, :], m[:, 1, :], ACT.Exp, bias=sink[:, h - 8:h - 7]), a)
        return b

    def weights(h, buf, b):
        m = nm[:, buf, :].rearrange("p (c q) -> p c q", q=QT)
        if h >= 8:
            b = dve.do(lambda e: e.tensor_tensor(m[:, 2, :], m[:, 2, :], m[:, 3, :], ALU.add), b)
        a = dve.do(lambda e: e.reciprocal(m[:, 4, :], m[:, 2, :]), b)
        out = []
        for qt in range(QT):
            pb = Pb[buf][:, qt, slice(*keys(h, qt))]
            out.append(dve.do(lambda e, pb=pb, qt=qt: e.tensor_scalar(pb, pb, m[:, 4, qt:qt + 1], None, ALU.mult), a))
        return out

    def values(h, buf, tok, o, free_o):
        b0 = 64 * (h % 2)
        tiles = []
        for kt in range(QT):
            qs = [qt for qt in range(QT) if keys(h, qt)[0] <= kt * P < keys(h, qt)[1]]
            a0, a1 = qs[0] * P, (qs[-1] + 1) * P
            i, ps, free = bank()
            for qt in qs:
                t = tr(ps[:, qt * P:(qt + 1) * P], Pb[buf][:, qt, kt * P:(kt + 1) * P], ident, qt == qs[-1], free, tok)
            j = n_pt[0] % NPT
            n_pt[0] += 1
            bank_free[i] = c = copy(act, PT[j][:, a0:a1], ps[:, a0:a1], t, PT_free[j])
            tiles.append((kt, j, a0, a1, c))
        Pb_free[buf] = t
        for kt, j, a0, a1, c in tiles:
            V = VA[:, kt, h * 64:h * 64 + 64] if h < 8 else VB[:, kt, (h - 8) // 4 * 64:(h - 8) // 4 * 64 + 64]
            PT_free[j] = last = mm(o[b0:b0 + 64, a0:a1], V, PT[j][:, a0:a1], kt == 0, kt == QT - 1, True, c,
                                   free_o if kt == 0 else None)
        return last

    ready = weights(0, 0, scores(0, 0))
    o_free = [None, None]
    for h in range(NH):
        if h + 1 < NH:
            bias_tok[h + 1] = bias(h + 1)
            nxt = scores(h + 1, (h + 1) % 2)
        o = psum[6 + (h // 2) % 2]
        last = values(h, h % 2, ready, o, o_free[(h // 2) % 2] if h % 2 == 0 else None)
        if h % 2 == 1:
            o_free[(h // 2) % 2] = o_tok = copy(act, oT[:, h // 2, :], o[:, :], last)
        if h + 1 < NH:
            ready = weights(h + 1, (h + 1) % 2, nxt)
    u = hT
    gemm("w_ao", NB, NB, lambda k: oT[:, k, :], o_tok, lambda nb, ps, t: copy(g.turns(nb), u[:, nb, :], ps[:, :], t))
    t = g.rstd_of(u, r, act.now(), dve.now())
    g.add_normed(u, vec["norm_g"][:, 8:16], r, t)
    g.barrier()
    mlp(g, 0)
    g.barrier()


def rwkv(g):
    pe, act, dve, pool, vec, I = g.pe, g.act, g.dve, g.pool, g.vec, g.I
    alloc, alloc3, bank, mm, tr, gemm = g.alloc, g.alloc3, g.bank, g.mm, g.tr, g.gemm
    copy, psum, bank_free, xT, ident, top = g.copy, g.psum, g.bank_free, g.xT, g.ident, g.top
    top[0] = g.base
    rT, kT, vT = alloc3(NB, S), alloc3(NB, S), alloc3(NB, S)
    tw, ta, tg = alloc3(2, S), alloc3(2, S), alloc3(2, S)
    for q in (tw, ta):
        pool.do(lambda e, q=q: e.memset(q[0:64, 1, :], 0.0))
        pool.do(lambda e, q=q: e.memset(q[64:128, 0, :], 0.0))
    z_tok = pool.now()
    mark = top[0]
    hT, dp, dn = alloc3(NB, S), alloc3(NB, S), alloc3(NB, S)
    r = alloc(S)
    mix = alloc3(NB, S)
    t = g.rstd_of(xT, r)
    h_tok = g.normed(xT, vec["norm_g"][:, 32:40], hT, r, t)
    a = pool.do(lambda e: e.tensor_tensor(dp[:, :, 1:S], hT[:, :, 0:S - 1], hT[:, :, 1:S], ALU.subtract), h_tok, z_tok)
    a = pool.do(lambda e: e.tensor_scalar(dp[:, :, 0:1], hT[:, :, 0:1], -1.0, None, ALU.mult), h_tok)
    b = dve.do(lambda e: e.tensor_tensor(dn[:, :, 0:S - 1], hT[:, :, 1:S], hT[:, :, 0:S - 1], ALU.subtract), h_tok)
    b = dve.do(lambda e: e.tensor_scalar(dn[:, :, S - 1:S], hT[:, :, S - 1:S], -1.0, None, ALU.mult), h_tok)
    d_tok = [a, b]
    mp, mn = vec["mu_prev"], vec["mu_next"]

    def mixed(c, free):
        for k in range(NB):
            m = 8 * c + k
            a = dve.do(lambda e, k=k, m=m: e.scalar_tensor_tensor(mix[:, k, :], dp[:, k, :], mp[:, m:m + 1], hT[:, k, :],
                                                                  ALU.mult, ALU.add), d_tok, free)
            a = dve.do(lambda e, k=k, m=m: e.scalar_tensor_tensor(mix[:, k, :], dn[:, k, :], mn[:, m:m + 1], mix[:, k, :],
                                                                  ALU.mult, ALU.add), a)
        return a

    def halves(dst, ps, f, t):
        act.do(lambda e: e.activation(dst[0:64, 0, :], ps[0:64, :], f), t)
        return act.do(lambda e: e.activation(dst[64:128, 1, :], ps[64:128, :], f), t)

    rhs = lambda k: mix[:, k, :]
    m = mixed(1, None)
    gemm("w_rw", 1, NB, rhs, m, lambda nb, ps, t: halves(tw, ps, ACT.Tanh, t))
    m = mixed(4, pe.now())
    gemm("w_ra", 1, NB, rhs, m, lambda nb, ps, t: halves(ta, ps, ACT.Copy, t))
    m = mixed(5, pe.now())
    gemm("w_rg1", 2, NB, rhs, m, lambda nb, ps, t: act.do(lambda e: e.activation(tg[:, nb, :], ps[:, :], ACT.Sigmoid), t))
    for c, name, dst in ((0, "w_rr", rT), (2, "w_rk", kT), (3, "w_rv", vT)):
        m = mixed(c, pe.now())
        g.state["hold"] = c == 3
        gemm(name, NB, NB, rhs, m, lambda nb, ps, t: copy(act, dst[:, nb, :], ps[:, :], t))
    g.barrier()
    top[0] = mark

    lm = alloc(2 * 6 * P).rearrange("p (d l a) -> p d l a", d=2, l=6)
    mM = alloc3(2, P)
    rm = alloc(S)
    w2s = [alloc(4 * P).rearrange("p (a b) -> p a b", a=4) for _ in range(2)]
    omka, nw0, na0 = alloc(NB), alloc(16), alloc(16)
    ld = g.load([(lm, I["levels"].rearrange("p (d l a) -> p d l a", d=2, l=6)),
                 (mM, I["maskM"].rearrange("p (a b) -> p a b", b=P)), (rm, I["starts"][0, :].partition_broadcast(P))])
    kk, sg, cs, aa, kd, e1, e2, t1, t2 = (alloc(S) for _ in range(9))
    BK, BKs = (alloc(2 * S).rearrange("p (c a t) -> p c a t", a=2, t=CH) for _ in range(2))
    LM = BK.rearrange("p c a t -> p c (a t)")
    Y = BKs.rearrange("p c a t -> p c (a t)")
    X = alloc3(NCH, P)
    lent = [g.ring_t[:, j * 1024:(j + 1) * 1024] for j in range(8)]
    LT, MK = (q.rearrange("p (c t) -> p c t", t=P) for q in lent[6:8])
    sets = []
    for j in range(2):
        b = Core()
        b.AR = g.ring_t[:, j * 2048:(j + 1) * 2048].rearrange("p (c a h t) -> p c a h t", a=2, h=2, t=CH)
        b.G1 = lent[4 + j].rearrange("p (c t) -> p c t", t=P)
        b.MR, b.XT, b.BKn, b.SAV = alloc3(NCH, P), alloc3(NCH, P), alloc3(NCH, P), alloc3(NCH, P)
        b.rho = alloc(S)
        b.bon, b.wc = alloc(S), alloc(NCH)
        b.done = None
        sets.append(b)
    U, Sb = alloc(P), alloc(P)
    oS, q1, q2, ysum = alloc(S), alloc(S), alloc(S), alloc(S)
    vec_k = vec["k_a"]
    for q in [Sb, lent[4], lent[5], lent[6], lent[7], g.ring_t[:, 0:4096]]:
        pool.do(lambda e, q=q: e.memset(q, 0.0))
    for b in sets:
        pool.do(lambda e, b=b: e.memset(b.SAV[0:64], 0.0))
    dve.do(lambda e: e.tensor_scalar(nw0, vec["w0"], -1.0, None, ALU.mult))
    dve.do(lambda e: e.tensor_scalar(na0, vec["a0"], -1.0, None, ALU.mult))
    dve.do(lambda e: e.tensor_scalar(omka, vec_k, -1.0, 1.0, ALU.mult, ALU.add))
    w2_sem = [g.semaphore("w2") for _ in range(2)]
    g.barrier()
    for e in (pe, act, dve, pool):
        e.wait(ld)
    prep_done = [None] * 16
    engines = (pe, act, dve, pool)

    def chunks(ap):
        return ap.rearrange("p (c t) -> p c t", t=CH)

    def norm_rows(b):
        a = dve.do(lambda e: e.tensor_scalar(kk, kT[:, b, :], vec["k_k"][:, b:b + 1], None, ALU.mult))
        s = act.do(lambda e: e.activation(t1, kk, ACT.Square), a)
        i, ps, free = bank()
        t = mm(ps[:, :], g.bd, t1, True, True, True, free, s)
        bank_free[i] = s = act.do(lambda e, ps=ps: e.activation(t2, ps[:, :], ACT.Sqrt), t)
        a = dve.do(lambda e: e.tensor_scalar(t2, t2, 1e-12, None, ALU.max), s)
        a = dve.do(lambda e: e.reciprocal(t2, t2), a)
        return dve.do(lambda e: e.tensor_tensor(kk, kk, t2, ALU.mult), a)

    def sigmoid(dst, ps, bias, t):
        s = act.do(lambda e: e.activation(dst, ps[:, :], ACT.Exp, scale=-1.0, bias=bias), t)
        a = dve.do(lambda e: e.tensor_scalar(dst, dst, 1.0, None, ALU.add), s)
        return s, dve.do(lambda e: e.reciprocal(dst, dst), a)

    def prepare(n):
        b, d = n // 2, n % 2
        o = sets[n % 2]
        free_set = o.done
        w2 = w2s[b % 2]
        if n:
            for e in engines:
                e.wait(prep_done[n - 1])
        if d == 0:
            prepare.w2_tok = pool.dma(w2, I["rk2"].rearrange("p (a n) -> p a n", a=4)[:, :, b * P:(b + 1) * P],
                                      w2_sem[b % 2], 16 * (b // 2 + 1), sets[1].done if b >= 2 else None)
            prepare.kk_tok = norm_rows(b)
        kk_tok, w2_tok = prepare.kk_tok, prepare.w2_tok
        yield
        i, ps, free = bank()
        t = mm(ps[:, :], w2[:, 0, :], tw[:, d, :], True, True, True, free, w2_tok)
        bank_free[i], s1 = sigmoid(sg, ps, nw0[:, 8 * d + b:8 * d + b + 1], t)
        yield
        i, ps, free = bank()
        t = mm(ps[:, :], w2[:, 1, :], ta[:, d, :], True, True, True, free)
        bank_free[i], s2 = sigmoid(aa, ps, na0[:, 8 * d + b:8 * d + b + 1], t)
        yield
        st = -1 if d else 1
        a = dve.do(lambda e: e.tensor_tensor_scan(cs[:, ::st], rm, sg[:, ::st], 0.0, ALU.mult, ALU.add), s1)
        last = chunks(cs)[:, :, 0:1] if d else chunks(cs)[:, :, CH - 1:CH]
        s3 = act.do(lambda e: e.activation(e1, cs, ACT.Exp, scale=-DECAY), a)
        s4 = act.do(lambda e: e.activation(e2, cs, ACT.Exp, scale=DECAY), a)
        s5 = act.do(lambda e: e.activation(o.wc.unsqueeze(2), last, ACT.Exp, scale=-DECAY), a, free_set)
        a = dve.do(lambda e: e.tensor_tensor(sg, cs, sg, ALU.subtract), a)
        s6 = act.do(lambda e: e.activation(sg, sg, ACT.Exp, scale=-DECAY), a)
        yield
        for q in range(2):
            i, ps, free = bank()
            for c in range(4):
                ch = 4 * q + c
                t = tr(ps[0:CH, c * P:(c + 1) * P], vT[:, b, ch * CH:(ch + 1) * CH], ident, c == 3, free)
            bank_free[i] = v_tok = copy(act, o.SAV[64:128, 4 * q:4 * q + 4, :], ps[0:CH, :].rearrange("p (a b) -> p a b", b=P), t)
            yield
        a = dve.do(lambda e: e.tensor_scalar(kd, aa, vec_k[:, b:b + 1], omka[:, b:b + 1], ALU.mult, ALU.add), s2)
        kd_tok = dve.do(lambda e: e.tensor_tensor(kd, kd, kT[:, b, :], ALU.mult), a)
        a = pool.do(lambda e: e.tensor_tensor(o.rho, rT[:, b, :], e1, ALU.mult), s3)
        ar = []
        for hh in range(2):
            half = slice(64 * hh, 64 * hh + 64)
            ar.append(act.do(lambda e, half=half, hh=hh: e.activation(o.AR[half, :, 1, hh, :], chunks(o.rho)[half], ACT.Copy), a))
            ar.append(dve.do(lambda e, half=half, hh=hh: e.scalar_tensor_tensor(
                o.AR[half, :, 0, hh, :], chunks(kk)[half], -1.0, chunks(sg)[half], ALU.mult, ALU.mult), s6, kk_tok))
        a = pool.do(lambda e: e.tensor_tensor(t1, kk, aa, ALU.mult), s2, kk_tok)
        a = dve.do(lambda e: e.tensor_tensor(BK[:, :, 0, :], chunks(t1), chunks(e2), ALU.mult), a, s4)
        bk = dve.do(lambda e: e.tensor_tensor(BK[:, :, 1, :], chunks(kd), chunks(e2), ALU.mult), kd_tok)
        bks = pool.do(lambda e: e.tensor_tensor(BKs.rearrange("p c a t -> p c (a t)"), BK.rearrange("p c a t -> p c (a t)"),
                                                o.wc.unsqueeze(2).broadcast_to((P, NCH, P)), ALU.mult), bk, s5)
        yield
        strict, upto = mM[:, d, 0:CH], mM[:, d, CH:P]
        for q in range(4):
            i, ps, free = bank()
            for c in range(2):
                t = mm(ps[:, c * 256:(c + 1) * 256], BK[:, 2 * q + c, :, :], o.AR[:, 2 * q + c, :, :, :], True, True,
                       c == 1, free, bk, ar)
            p1 = t
            prod = ps[:, :].rearrange("p (c k h t) -> p c k h t", c=2, k=2, h=2)
            cs2 = slice(2 * q, 2 * q + 2)
            for hh in range(2):
                half = slice(64 * hh, 64 * hh + 64)
                m_tok = dve.do(lambda e, half=half, prod=prod, hh=hh, cs2=cs2: e.tensor_tensor(
                    LT[half, cs2, half], prod[0:64, :, 0, hh, :], strict[0:64].unsqueeze(1).broadcast_to((64, 2, CH)), ALU.mult), t)
            mk_tok = dve.do(lambda e, prod=prod, cs2=cs2: e.tensor_tensor(
                MK[64:128, cs2, :].rearrange("p c (h t) -> p c h t", h=2), prod[64:128, :, 0, :, :],
                strict[64:128].unsqueeze(1).unsqueeze(1).broadcast_to((64, 2, 2, CH)), ALU.mult), t)
            bank_free[i] = dve.do(lambda e, prod=prod, cs2=cs2: e.tensor_tensor(
                o.MR[:, cs2, :].rearrange("p c (h t) -> p c h t", h=2), prod[:, :, 1, :, :],
                upto.unsqueeze(1).unsqueeze(1).broadcast_to((P, 2, 2, CH)), ALU.mult), t)
            yield
        for q in range(2):
            i, ps, free = bank()
            for c in range(4):
                t = tr(ps[:, c * P:(c + 1) * P], BKs[:, 4 * q + c, :, :], ident, c == 3, free, bks)
            bkt = t
            bank_free[i] = copy(act, o.BKn[:, 4 * q:4 * q + 4, :], ps[:, :].rearrange("p (a b) -> p a b", b=P), t)
            yield
        XT = o.XT

        def masked(level, *tokens):
            return pool.do(lambda e: e.tensor_tensor(LM, LT, lm[:, d, level, :].unsqueeze(1).broadcast_to((P, NCH, P)),
                                                     ALU.mult), m_tok, *tokens)

        a = masked(0, p1, bks)
        a = pool.do(lambda e: e.tensor_tensor(XT, LM, ident.unsqueeze(1).broadcast_to((P, NCH, P)), ALU.add), a)
        xts = [a, a]
        y_used = a
        for level in range(1, 6):
            lt = masked(level, y_used)
            xs, ys = [], []
            for q in range(2):
                i, ps, free = bank()
                for c in range(4):
                    t = tr(ps[:, c * P:(c + 1) * P], XT[:, 4 * q + c, :], ident, c == 3, free, xts[q])
                bank_free[i] = c_tok = copy(act, X[:, 4 * q:4 * q + 4, :], ps[:, :].rearrange("p (a b) -> p a b", b=P), t, y_used)
                xs.append(c_tok)
                yield
            for q in range(2):
                i, ps, free = bank()
                for c in range(4):
                    t = mm(ps[:, c * P:(c + 1) * P], LM[:, 4 * q + c, :], X[:, 4 * q + c, :], True, True, c == 3, free, lt, xs[q])
                y_used = t
                bank_free[i] = c_tok = copy(act, Y[:, 4 * q:4 * q + 4, :], ps[:, :].rearrange("p (a b) -> p a b", b=P), t, bkt)
                ys.append(c_tok)
                yield
            for q in range(2):
                i, ps, free = bank()
                for c in range(4):
                    t = mm(ps[:, c * P:(c + 1) * P], Y[:, 4 * q + c, :], XT[:, 4 * q + c, :], True, True, c == 3, free, ys[q])
                bkt = t
                bank_free[i] = xts[q] = dve.do(lambda e, ps=ps, q=q: e.tensor_tensor(
                    XT[:, 4 * q:4 * q + 4, :], XT[:, 4 * q:4 * q + 4, :],
                    ps[:, :].rearrange("p (a b) -> p a b", b=P), ALU.add), t, xts[q])
                yield
        for q in range(2):
            i, ps, free = bank()
            for c in range(4):
                for hh in range(2):
                    h0 = 64 * hh
                    t = mm(ps[h0:h0 + 64, c * P + h0:c * P + h0 + 64], MK[:, 4 * q + c, h0:h0 + 64], o.SAV[:, 4 * q + c, h0:h0 + 64],
                           True, True, c == 3 and hh == 1, free, v_tok, mk_tok, free_set)
            for hh in range(2):
                half = slice(64 * hh, 64 * hh + 64)
                bank_free[i] = copy(act, o.G1[half, 4 * q:4 * q + 4, half],
                                    ps[half, :].rearrange("p (a b) -> p a b", b=P)[:, :, half], t)
            yield
        c = dve.do(lambda e: e.scalar_tensor_tensor(t1, rT[:, b, :], vec["r_k"][:, b:b + 1], kd, ALU.mult, ALU.mult))
        i, ps, free = bank()
        t = mm(ps[:, :], g.bd, t1, True, True, True, free, c)
        bank_free[i] = dve.do(lambda e, ps=ps: e.tensor_tensor(o.bon, vT[:, b, :], ps[:, :], ALU.mult), t)
        prep_done[n] = [e.now() for e in engines]

    def advance(n):
        b, d = n // 2, n % 2
        o = sets[n % 2]
        w2 = w2s[b % 2]
        for e in engines:
            e.wait(prep_done[n])
        O = psum[6 + n % 2]
        o_free = bank_free[6 + n % 2]
        sb = u_free = sets[1 - n % 2].done
        first = True
        for ch in (range(NCH - 1, -1, -1) if d else range(NCH)):
            if first:
                a = dve.do(lambda e, ch=ch: e.tensor_copy(U, o.G1[:, ch, :]), u_free)
            else:
                i, ps, free = bank()
                t = mm(ps[:, 0:P], o.AR[:, ch, 0, :, :], Sb, True, True, True, free, sb)
                bank_free[i] = a = dve.do(lambda e, ps=ps, ch=ch: e.tensor_tensor(U, ps[:, 0:P], o.G1[:, ch, :], ALU.add), t, u_free)
            yield
            i, ps, free = bank()
            u_free = t = mm(ps[:, 0:P], o.XT[:, ch, :], U, True, True, True, free, a)
            sv = copy(dve, o.SAV[0:64, ch, 0:64], ps[0:64, 0:64], t)
            bank_free[i] = sv = copy(dve, o.SAV[0:64, ch, 64:128], ps[64:128, 64:128], t)
            yield
            i, ps, free = bank()
            for hh in range(2):
                h0 = 64 * hh
                t = mm(ps[h0:h0 + 64, 0:64], o.BKn[:, ch, h0:h0 + 64], o.SAV[:, ch, h0:h0 + 64], True, True, hh == 1, free, sv)
            o_cols = slice(ch * CH, (ch + 1) * CH)
            if not first:
                mm(O[:, o_cols], Sb, o.rho[:, o_cols], True, False, False, o_free)
            for hh in range(2):
                h0 = 64 * hh
                o_last = mm(O[h0:h0 + 64, o_cols], o.SAV[:, ch, h0:h0 + 64], o.MR[:, ch, h0:h0 + 64], first, True, hh == 1, o_free)
            sb = []
            for hh in range(2):
                h0 = 64 * hh
                blk = Sb[h0:h0 + 64, h0:h0 + 64]
                if first:
                    a = dve.do(lambda e, ps=ps, h0=h0, blk=blk: e.tensor_copy(blk, ps[h0:h0 + 64, 0:64]), t, u_free)
                else:
                    a = dve.do(lambda e, ps=ps, h0=h0, blk=blk, ch=ch: e.scalar_tensor_tensor(
                        blk, blk, o.wc[h0:h0 + 64, ch:ch + 1], ps[h0:h0 + 64, 0:64], ALU.mult, ALU.add), t, o_last)
                sb.append(a)
            bank_free[i] = a
            first = False
            yield
        a = copy(dve, oS, O[:, :], o_last)
        bank_free[6 + n % 2] = a
        i, ps, free = bank()
        t = mm(ps[:, :], g.bdm, oS, True, True, True, free, a)
        yield
        bank_free[i] = a = dve.do(lambda e, ps=ps: e.tensor_tensor(oS, oS, ps[:, :], ALU.subtract), t)
        s = act.do(lambda e: e.activation(q1, oS, ACT.Square), a)
        yield
        i, ps, free = bank()
        t = mm(ps[:, :], g.bdm, q1, True, True, True, free, s)
        yield
        bank_free[i] = s = act.do(lambda e, ps=ps: e.activation(q2, ps[:, :], ACT.Sqrt, bias=g.eps[:, 1:2]), t)
        yield
        a = dve.do(lambda e: e.reciprocal(q2, q2), s)
        a = dve.do(lambda e: e.tensor_tensor(oS, oS, q2, ALU.mult), a)
        a = dve.do(lambda e: e.tensor_scalar(oS, oS, vec["gn_w"][:, b:b + 1], vec["gn_b"][:, b:b + 1], ALU.mult, ALU.add), a)
        yield
        a = pool.do(lambda e: e.tensor_tensor(oS, oS, o.bon, ALU.add), a)
        i, ps, free = bank()
        t = mm(ps[:, :], w2[:, 2 + d, :], tg[:, d, :], True, True, True, free)
        yield
        if d == 0:
            bank_free[i] = a = dve.do(lambda e, ps=ps: e.tensor_tensor(ysum, oS, ps[:, :], ALU.mult), a, t)
        else:
            bank_free[i] = a = dve.do(lambda e, ps=ps: e.tensor_tensor(oS, oS, ps[:, :], ALU.mult), a, t)
            a = pool.do(lambda e: e.tensor_tensor(rT[:, b, :], ysum, oS, ALU.add), a)
        o.done = [e.now() for e in engines]

    for _ in prepare(0):
        pass
    for n in range(16):
        ahead = prepare(n + 1) if n < 15 else iter(())
        for k, _ in enumerate(advance(n)):
            for _ in range(2 if k % 2 else 1):
                next(ahead, None)
        for _ in ahead:
            pass
    yT = rT
    g.barrier()
    g.resume()
    g.barrier()
    top[0] = mark
    u, r = kT, alloc(S)
    gemm("w_ro", NB, NB, lambda k: yT[:, k, :], dve.now(), lambda nb, ps, t: copy(g.turns(nb), u[:, nb, :], ps[:, :], t))
    t = g.rstd_of(u, r, act.now(), dve.now())
    g.add_normed(u, vec["norm_g"][:, 40:48], r, t)
    g.barrier()
    mlp(g, 1)


def _fm(w):
    k, n = w.shape
    return np.ascontiguousarray(w.reshape(k // P, P, n // P, P).transpose(1, 2, 0, 3).reshape(P, -1))


def _tm(w):
    k, n = w.shape
    return np.ascontiguousarray(w.reshape(k // P, P, n // 512, 512).transpose(1, 2, 0, 3).reshape(P, -1))


def _vec(v):
    return v.reshape(-1, P).T


def _bucket(rel):
    nb, me = 16, 8
    n = np.abs(rel)
    large = me + (np.log(np.maximum(n, 1) / me) / math.log(1024 / me) * (nb - me)).astype(np.int64)
    return np.where(rel > 0, nb, 0) + np.where(n < me, n, np.minimum(large, nb - 1))


def _constants():
    c = {}
    f = np.float32
    c["ident"] = np.eye(P, dtype=f)
    i = np.arange(P)
    c["tri"] = np.where(i[None, :] <= i[:, None], 0.0, NEG).astype(f)
    c["bd"] = np.kron(np.eye(2), np.ones((64, 64))).astype(f)
    pos = np.arange(S).reshape(QT, P).T[:, :, None]
    end = np.arange(NCMP)[None, None, :] * 16 + 31
    c["cneg"] = np.where(end <= pos, 0.0, NEG).astype(f).reshape(P, -1)
    c["rowvalid"] = (i[:, None] >= 31).astype(f)
    rel = 511 - np.arange(1024)
    c["onehot"] = (_bucket(rel)[None, :] == np.arange(32)[:, None]).astype(f)
    d = 511 - np.arange(896)[None, :] - i[:, None]
    a = np.abs(d)
    count = (a <= 64).astype(int) + ((d % 4 == 0) & (a <= 256)) + (d % 16 == 0)
    c["maskA"] = np.where(count > 0, np.log(np.maximum(count, 1)), NEG).astype(f)
    c["maskB"] = np.where(a <= 128, 0.0, NEG).astype(f)
    s, t = np.arange(CH)[:, None], np.arange(CH)[None, :]
    lv = [(s // n + 1 == t // n) & (s // (2 * n) == t // (2 * n)) for n in (1,) + LEVELS]
    lv = [[np.kron(np.eye(2), m) for m in ms] for ms in (lv, [m.T for m in lv])]
    c["levels"] = np.stack([np.stack(ms, 1) for ms in lv], 1).astype(f).reshape(P, -1)
    fw = np.tile(np.concatenate([s < t, s <= t], 1), (2, 1))
    bw = np.tile(np.concatenate([s > t, s >= t], 1), (2, 1))
    c["maskM"] = np.concatenate([fw, bw], 1).astype(f)
    c["starts"] = (np.arange(S) % CH > 0).astype(f).reshape(1, -1)
    return c


def _layout(x):
    a = {n: np.asarray(v) for n, v in x.items()}
    o = _constants()
    o["xT"] = np.ascontiguousarray(a["x"][0].T)
    w = a["w_in"][0]
    cut = np.cumsum([0, 1024, 1024, 1024, 1536, 48, 1024, 1024, 3072])
    u, v, q, kv, gates, xr, rg, mg = (w[:, cut[j]:cut[j + 1]] for j in range(8))
    o["w_v"], o["w_u"], o["w_q"] = _tm(v), _fm(u), _fm(q)
    o["w_kv"] = _fm(np.concatenate([kv[:, 0:768], kv[:, 1024:1280]], 1))
    o["w_vt"] = _tm(np.concatenate([kv[:, 768:1024], kv[:, 1280:1536]], 1))
    o["w_gate"] = np.ascontiguousarray(gates.reshape(NB, P, 48).transpose(1, 0, 2).reshape(P, -1))
    o["wk1"], o["wv1"] = _fm(a["nsa_wk1"][0]), _fm(a["nsa_wv1"][0])
    o["w_cmp2"] = np.ascontiguousarray(np.concatenate(
        [a[n][0].reshape(2, P, 64).transpose(1, 0, 2).reshape(P, -1) for n in ("nsa_wk2", "nsa_wv2")], 1))
    o["w_xr"], o["w_rg"] = _fm(xr), _fm(rg)
    br = [a[n][0] for n in ("w_br_a", "w_br_b", "w_br_c")]
    for nb in range(NB):
        parts = []
        for c in range(3):
            parts.append(_fm(mg[:, c * D + nb * P:c * D + (nb + 1) * P]))
            parts.append(_fm(br[c][:, nb * P:(nb + 1) * P]))
        o[f"w_mb{nb}"] = np.ascontiguousarray(np.concatenate(parts, 1))
    o["w_o"] = _fm(a["w_o"][0])
    fi = a["w_ffn_in"][0]
    o["w_fi"] = _fm(np.stack([fi[:, :DFF].reshape(D, NFF, P), fi[:, DFF:].reshape(D, NFF, P)], 2).reshape(D, -1))
    o["w_fo"] = _fm(a["w_ffn_out"][0])
    w = a["attn_w_in_2"][0]
    o["w_a2"] = _fm(np.concatenate([w[:, 0:512], w[:, 1536:2048], w[:, 512:1024], w[:, 2048:2176], w[:, 2176:2304]], 1))
    o["w_va"] = _tm(w[:, 1024:1536])
    o["w_ao"] = _fm(a["attn_w_out_2"][0])
    for layer in range(2):
        o[f"w_m1{layer}"] = _fm(a["mlp_w1_2"][layer])
        o[f"w_m2{layer}"] = _fm(a["mlp_w2_2"][layer])
    o["rel_table"] = a["rel_table_2"]
    o["sink"] = a["attn_sink_2"].reshape(1, 8)
    o["w_rw"] = _fm(np.concatenate(list(a["rk_w1_2"][0]), 1))
    o["w_ra"] = _fm(np.concatenate(list(a["rk_a1_2"][0]), 1))
    o["w_rg1"] = _fm(np.concatenate(list(a["rk_g1_2"][0]), 1))
    for n, s in (("w_rr", "rk_w_r_2"), ("w_rk", "rk_w_k_2"), ("w_rv", "rk_w_v_2"), ("w_ro", "rk_w_o_2")):
        o[n] = _fm(a[s][0])
    o["rk2"] = np.ascontiguousarray(np.concatenate(
        [a["rk_w2_2"][0].reshape(P, D), a["rk_a2_2"][0].reshape(P, D), a["rk_g2_2"][0, 0], a["rk_g2_2"][0, 1]], 1))
    o["ln_g"], o["ln_b"] = a["gmlp_ln_g"], a["gmlp_ln_b"]
    o["wsT"] = np.ascontiguousarray(a["gmlp_ws"][0].transpose(2, 0, 1).reshape(P, -1))
    o["bs"] = a["gmlp_bs"].reshape(1, -1)
    o["rnn_wa"], o["rnn_wx"] = a["rnn_wa"][0], a["rnn_wx"][0]
    src = {"g_pre_mix": "g_pre_mix", "g_post_mix": "g_post_mix", "g_pre_ffn": "g_pre_ffn", "g_post_ffn": "g_post_ffn",
           "conv_w": "rnn_conv_w", "conv_b": "rnn_conv_b", "rnn_ba": "rnn_ba", "rnn_bx": "rnn_bx",
           "rnn_lam": "rnn_lam", "pe_k": "nsa_pe_k", "pe_v": "nsa_pe_v", "norm_g": "norm_g_2",
           "mu_prev": "rk_mu_prev_2", "mu_next": "rk_mu_next_2", "k_k": "rk_k_k_2", "k_a": "rk_k_a_2",
           "r_k": "rk_r_k_2", "gn_w": "rk_gn_w_2", "gn_b": "rk_gn_b_2", "w0": "rk_w0_2", "a0": "rk_a0_2"}
    o["vecs"] = np.ascontiguousarray(np.concatenate([_vec(a[src[n]]) for n, _ in VECS], 1))
    return o


def kernel(**inputs):
    import concourse.bacc as bacc
    from concourse.bass_utils import run_bass_kernel_spmd

    nc = bacc.Bacc("TRN2", target_bir_lowering=False, num_devices=1)
    arrays = _layout(inputs)
    I = {n: nc.dram_tensor(f"in_{n}", a.shape, mybir.dt.from_np(a.dtype), kind="ExternalInput").ap()
         for n, a in arrays.items()}
    I["scratch"] = nc.dram_tensor("scratch", (16, 1024), F32, kind="Internal").ap()
    out = nc.dram_tensor("out_0", (D, S), F32, kind="ExternalOutput").ap()
    program(nc, I, out)
    r = run_bass_kernel_spmd(nc, [{f"in_{n}": a for n, a in arrays.items()}], core_ids=[0])
    return np.ascontiguousarray(r.results[0]["out_0"].T)[None]
```

```python
import math
from contextlib import ExitStack

import numpy as np

import concourse.bass as bass
from concourse import mybir

F32 = mybir.dt.float32
F32R = mybir.dt.float32r
ALU = mybir.AluOpType
ACT = mybir.ActivationFunctionType
AX = mybir.AxisListType
P = 128
S = 512
D = 1024
NB = D // P
QT = S // P
PIECE = 2048
ROOM = 53200
RING = 3
NEG = -1e30
EPS = 1e-6
GN_EPS = 64e-5
DFF = 2816
NFF = DFF // P
MLP = 4096
NMLP = MLP // P
NH = 16
NCMP = 31
CH = 64
NCH = S // CH
LEVELS = (2, 4, 8, 16, 32)
DECAY = math.exp(-0.5)
ROT = 6
NPT = 5

STREAM = [("w_v", 8192), ("w_u", 8192), ("w_q", 8192), ("w_kv", 8192), ("w_vt", 4096),
          ("wk1", 4096), ("wv1", 4096), ("w_xr", 8192), ("w_rg", 8192)]
STREAM += [(f"w_mb{c}", 2 * NB * 1024) for c in range(3)]
STREAM += [("w_o", 8192), ("w_fi0", NFF * 1024), ("w_fo0", NFF * 512), ("w_fi1", NFF * 1024), ("w_fo1", NFF * 512)]
STREAM += [("w_a2", 13 * 1024), ("w_vb", 1024), ("w_va", 4096), ("w_ao", 8192)]
STREAM += [(f"w_m{j}0{half}", NMLP * 512) for half in range(2) for j in (1, 2)]
STREAM += [("w_rr", 8192), ("w_rw", 1024), ("w_rk", 8192), ("w_ra", 1024), ("w_rv", 8192), ("w_rg1", 2048),
           ("w_ro", 8192)]
STREAM += [(f"w_m{j}1{half}", NMLP * 512) for half in range(2) for j in (1, 2)]

VECS = [("g_pre_mix", 8), ("g_post_mix", 8), ("g_pre_ffn", 8), ("g_post_ffn", 8), ("conv_w", 32), ("conv_b", 8),
        ("rnn_ba", 8), ("rnn_bx", 8), ("rnn_lam", 8), ("pe_k", 16), ("pe_v", 16), ("norm_g", 64),
        ("mu_prev", 48), ("mu_next", 48), ("k_k", 8), ("k_a", 8), ("r_k", 8), ("gn_w", 8), ("gn_b", 8),
        ("w0", 16), ("a0", 16)]
NVEC = sum(n for _, n in VECS)


class Engine:

    def __init__(self, sem):
        self.sem, self.count, self.queue, self.met = sem, 0, [], {}

    def wait(self, *tokens):
        for t in tokens:
            if t is None:
                continue
            if isinstance(t, list):
                self.wait(*t)
            elif self.met.get(id(t[0]), 0) < t[1]:
                self.met[id(t[0])] = t[1]
                self.queue.append(lambda e, t=t: e.wait_ge(t[0], t[1]))

    def do(self, fn, *tokens):
        self.wait(*tokens)
        self.count += 1
        self.queue.append(lambda e: fn(e).then_inc(self.sem, 1))
        return (self.sem, self.count)

    def quiet(self, fn, *tokens):
        self.wait(*tokens)
        self.queue.append(fn)

    def dma(self, out, in_, sem, value, *tokens):
        self.wait(*tokens)
        self.queue.append(lambda e: e.dma_start(out, in_).then_inc(sem, 16))
        return (sem, value)

    def now(self):
        return (self.sem, self.count)


class Core:
    pass


def program(nc, I, out):
    with ExitStack() as ctx:
        names = iter(range(10 ** 6))

        def semaphore(name):
            return ctx.enter_context(nc.semaphore(f"{name}{next(names)}"))

        psum = [ctx.enter_context(nc.psum_tensor(f"bank{i}", [P, 512], F32)) for i in range(8)]
        pe, act, dve, pool, sp = (Engine(semaphore(n)) for n in ("pe", "act", "dve", "pool", "sp"))
        top = [0]
        levels = []

        def region(level, size, *splits):
            while len(levels) > level:
                levels.pop()[0].close()
            sub = ctx.enter_context(ExitStack())
            pairs, used = [], sum(lv[2] for lv in levels)
            for n in splits:
                pairs.append([sub.enter_context(nc.sbuf_tensor(f"{part}{next(names)}", [P, n], F32R))
                              for part in ("hi", "lo")])
                used += 2 * n
            own = sum(splits) * 2
            if size is None:
                size = ROOM - used
            assert used + size <= ROOM, (used, size)
            levels.append((sub, sub.enter_context(nc.sbuf_tensor(f"arena{next(names)}", [P, size], F32)), own + size, size))
            top[0] = 0
            return pairs

        def alloc(n):
            arena, size = levels[-1][1], levels[-1][3]
            a = arena[:, top[0]:top[0] + n]
            top[0] += n
            assert top[0] <= size, (top[0], size)
            return a

        def alloc3(a, b):
            return alloc(a * b).rearrange("p (a b) -> p a b", b=b)

        def barrier():
            tokens = [e.now() for e in (pe, act, dve, pool)]
            for e in (pe, act, dve, pool):
                e.wait(tokens)

        def load(pairs, *tokens):
            s = semaphore("ld")
            for dst, src in pairs:
                pool.dma(dst, src, s, 0, *tokens)
            return (s, 16 * len(pairs))

        region(0, RING * PIECE + NVEC + 5 * P + 4 + NB * S)
        ring_t = alloc(RING * PIECE)
        slots = [ring_t[:, i * PIECE:(i + 1) * PIECE] for i in range(RING)]
        slot_sem = [semaphore("w") for _ in range(RING)]
        pieces = []
        for name, total in STREAM:
            for a in range(0, total, PIECE):
                pieces.append((name, a, min(PIECE, total - a)))
        state = {"issued": 0, "at": 0, "off": 0, "freed": 0,
                 "limit": [name for name, _, _ in pieces].index("w_ro")}

        def issue(token):
            i = state["issued"]
            if i >= len(pieces):
                return
            name, a, n = pieces[i]
            sp.dma(slots[i % RING][:, 0:n], I[name][:, a:a + n], slot_sem[i % RING], 0, token)
            state["issued"] += 1

        def take(name, n):
            i = state["at"]
            assert pieces[i][0] == name and state["off"] + n <= pieces[i][2], (name, pieces[i])
            assert i < state["issued"], "the ring is too small"
            ap = slots[i % RING][:, state["off"]:state["off"] + n]
            token = (slot_sem[i % RING], 16 * (i // RING + 1))
            state["off"] += n
            if state["off"] == pieces[i][2]:
                state["at"] += 1
                state["off"] = 0
            return ap, token

        def release(token):
            while state["freed"] < state["at"] and state["issued"] < state["limit"]:
                issue(token)
                state["freed"] += 1

        def resume():
            state["limit"] = len(pieces) + RING
            release([e.now() for e in (pe, act, dve, pool)])

        for _ in range(RING):
            issue(None)

        bank_free = [None] * 8
        turn = [0]

        def bank():
            i = turn[0] % ROT
            turn[0] += 1
            return i, psum[i], bank_free[i]

        def mm(out_, lhsT, rhs, start, stop_, last, *tokens):
            if last:
                return pe.do(lambda e: e.matmul(out_, lhsT, rhs, start=start, stop=stop_, skip_group_check=True), *tokens)
            return pe.quiet(lambda e: e.matmul(out_, lhsT, rhs, start=start, stop=stop_, skip_group_check=True), *tokens)

        def tr(out_, in_, ident_, last, *tokens):
            if last:
                return pe.do(lambda e: e.transpose(out_, in_, ident_), *tokens)
            return pe.quiet(lambda e: e.transpose(out_, in_, ident_), *tokens)

        def gemm(name, nblocks, kt, rhs, rhs_token, evac):
            for nb in range(nblocks):
                i, ps, free = bank()
                for k in range(kt):
                    w, wt = take(name, P)
                    t = mm(ps[:, :], w, rhs(k), k == 0, k == kt - 1, k == kt - 1, free, wt, rhs_token)
                release(t)
                bank_free[i] = evac(nb, ps, t)

        halves = {"names": (), "ready": [], "at": 0, "slots": None, "free": [None] * 3, "last": None}

        def split(src, hi, lo, *tokens, low=dve):
            a = act.do(lambda e: e.activation(hi, src, ACT.Copy), *tokens)
            return [a, low.do(lambda e: e.tensor_tensor(lo, src, hi.bitcast(F32), ALU.subtract), a)]

        def split_weights(low=dve):
            i = state["at"]
            if i >= len(pieces) or pieces[i][0] not in halves["names"]:
                return
            j = halves["at"] % 3
            halves["at"] += 1
            raw, wt = take(pieces[i][0], 1024)
            hi, lo = (q[:, j * 1024:(j + 1) * 1024] for q in halves["slots"])
            t = split(raw, hi, lo, wt, halves["free"][j], low=low)
            release([halves["last"], t])
            halves["last"] = t
            halves["ready"].append((pieces[i][0], hi, lo, t, j))

        def splitting(slots, *names_):
            halves.update(names=names_, slots=slots, free=[None] * 3)
            pool.wait(pool.now())
            for _ in range(3):
                split_weights(pool)

        def gemm_split(name, nblocks, kt, parts, rhs_token, evac, each=None):
            n = 0
            for nb in range(nblocks):
                i, ps, free = bank()
                for k in range(kt):
                    if n % 8 == 0:
                        got, hi, lo, wt, j = halves["ready"].pop(0)
                        assert got == name, (got, name)
                    c = slice((n % 8) * P, (n % 8 + 1) * P)
                    xh, xl = parts(k)
                    mm(ps[:, :], hi[:, c], xh, k == 0, False, False, free, wt, rhs_token(k))
                    mm(ps[:, :], hi[:, c], xl, False, False, False)
                    last = k == kt - 1 or n % 8 == 7 or (each is not None and nb == nblocks - 1)
                    t = mm(ps[:, :], lo[:, c], xh, False, k == kt - 1, last)
                    if each is not None and nb == nblocks - 1:
                        each[k] = t
                    if n % 8 == 7:
                        halves["free"][j] = t
                        if k < kt - 1:
                            split_weights()
                    n += 1
                bank_free[i] = evac(nb, ps, t)
                if n % 8 == 0:
                    split_weights()

        def gemm_tokens_split(name, sets, parts, x_token, evac):
            for n in range(sets):
                banks = [bank() for _ in range(QT)]
                toks = []
                for k in range(NB):
                    if k % 2 == 0:
                        got, hi, lo, wt, j = halves["ready"].pop(0)
                        assert got == name, (got, name)
                    c = slice((k % 2) * 512, (k % 2) * 512 + 512)
                    for qt, (i, ps, free) in enumerate(banks):
                        xh, xl = (p[:, qt * P:(qt + 1) * P] for p in parts(k))
                        mm(ps[:, :], xh, hi[:, c], k == 0, False, False, free, wt, x_token(k))
                        mm(ps[:, :], xh, lo[:, c], False, False, False)
                        t = mm(ps[:, :], xl, hi[:, c], False, k == NB - 1, k == NB - 1 or (k % 2 == 1 and qt == QT - 1))
                        if k == NB - 1:
                            toks.append(t)
                    if k % 2 == 1:
                        halves["free"][j] = t
                        if k < NB - 1:
                            split_weights()
                for qt, (i, ps, free) in enumerate(banks):
                    bank_free[i] = evac(n, qt, ps, toks[qt])
                split_weights()

        vec_t = alloc(NVEC)
        vec, at = {}, 0
        for name, n in VECS:
            vec[name] = vec_t[:, at:at + n]
            at += n
        ident = alloc(P)
        tri = alloc(P)
        ones = alloc(P)
        bd = alloc(P)
        bdm = alloc(P)
        eps = alloc(4)
        c_tok = load([(vec_t, I["vecs"][:, :]), (ident, I["ident"][:, :]), (tri, I["tri"][:, :]), (bd, I["bd"][:, :])])
        k1 = pool.do(lambda e: e.memset(ones, 1.0 / D))
        k2 = pool.do(lambda e: e.memset(eps[:, 0:1], EPS))
        k2 = pool.do(lambda e: e.memset(eps[:, 1:2], GN_EPS))
        k3 = dve.do(lambda e: e.tensor_scalar(bdm, bd, 1.0 / CH, None, ALU.mult), c_tok)
        xT = alloc3(NB, S)
        x_tok = load([(xT, I["xT"].rearrange("(k p) t -> p k t", p=P))])
        region(1, None)
        for e in (pe, act, dve, pool):
            e.wait(c_tok, k1, k2, k3, x_tok)

        class Squares:

            def __init__(self):
                self.buf, self.used, self.n, self.last = [alloc(S) for _ in range(2)], [None, None], 0, None

            def add(self, block, *tokens):
                q = self.buf[self.n % 2]
                t = act.do(lambda e: e.activation(q, block, ACT.Square), self.used[self.n % 2], *tokens)
                self.product()
                self.last = (q, self.n, t)
                self.n += 1

            def product(self):
                if self.last:
                    q, n, t = self.last
                    self.used[n % 2] = self.token = mm(psum[6][:, :], ones, q, n == 0, n == NB - 1, True, bank_free[6], t)

            def rstd(self, dst):
                assert self.n == NB
                self.product()
                bank_free[6] = a = act.do(lambda e: e.activation(dst, psum[6][:, :], ACT.Sqrt, bias=eps[:, 0:1]), self.token)
                return dve.do(lambda e: e.reciprocal(dst, dst), a)

        def rstd_of(src, dst, *tokens):
            mark = top[0]
            sums = Squares()
            for k in range(NB):
                sums.add(src[:, k, :], *tokens)
            top[0] = mark
            return sums.rstd(dst)

        def normed(src, gain, dst, r, tok):
            for k in range(NB):
                t = dve.do(lambda e, k=k: e.scalar_tensor_tensor(dst[:, k, :], src[:, k, :], gain[:, k:k + 1], r,
                                                                 ALU.mult, ALU.mult), tok)
            return t

        def normed_split(src, gain, raw, parts, r, tok):
            out_ = []
            for k in range(NB):
                t = dve.do(lambda e, k=k: e.scalar_tensor_tensor(raw[:, k, :], src[:, k, :], gain[:, k:k + 1], r,
                                                                 ALU.mult, ALU.mult), tok)
                out_.append(split(raw[:, k, :], *(p[:, k * S:(k + 1) * S] for p in parts), t, low=pool if k % 2 else dve))
            return out_

        def squared(dst, sums):
            def evac(nb, ps, t):
                a = copy(turns(nb), dst[:, nb, :], ps[:, :], t)
                sums.add(dst[:, nb, :], a)
                return a
            return evac

        def gather(fo, j, sums):
            def evac(nb, ps, t):
                if j == 0:
                    return copy(turns(nb), fo[:, nb, :], ps[:, :], t, act.now(), dve.now())
                a = dve.do(lambda e: e.tensor_tensor(fo[:, nb, :], fo[:, nb, :], ps[:, :], ALU.add), t, act.now())
                sums.add(fo[:, nb, :], a)
                return a
            return evac

        def add_normed(src, gain, r, tok):
            for k in range(NB):
                t = dve.do(lambda e, k=k: e.scalar_tensor_tensor(src[:, k, :], src[:, k, :], gain[:, k:k + 1], r,
                                                                 ALU.mult, ALU.mult), tok)
                adder = dve if k % 3 == 1 or k == NB - 1 else pool
                adder.do(lambda e, k=k: e.tensor_tensor(xT[:, k, :], xT[:, k, :], src[:, k, :], ALU.add), t)

        def copy(eng, dst, src, *tokens):
            if eng is act:
                return act.do(lambda e: e.activation(dst, src, ACT.Copy), *tokens)
            return eng.do(lambda e: e.tensor_copy(dst, src), *tokens)

        def turns(nb):
            return act if nb % 2 else dve

        def emit():
            with nc.Block() as block:
                for e, reg in ((sp, block.sync), (pool, block.gpsimd), (act, block.scalar),
                               (pe, block.tensor), (dve, block.vector)):
                    def body(eng, e=e):
                        for fn in e.queue:
                            fn(eng)
                    reg(body)

        T = Core()
        T.pe = pe
        T.act = act
        T.dve = dve
        T.pool = pool
        T.sp = sp
        T.vec = vec
        T.I = I
        T.alloc = alloc
        T.alloc3 = alloc3
        T.bank = bank
        T.mm = mm
        T.tr = tr
        T.gemm = gemm
        T.take = take
        T.release = release
        T.resume = resume
        T.ring_t = ring_t
        T.copy = copy
        T.psum = psum
        T.bank_free = bank_free
        T.xT = xT
        T.ident = ident
        T.top = top
        T.rstd_of = rstd_of
        T.normed = normed
        T.add_normed = add_normed
        T.load = load
        T.barrier = barrier
        T.state = state
        T.eps = eps
        T.tri = tri
        T.turns = turns
        T.base = 0
        T.region = region
        T.splitting = splitting
        T.gemm_split = gemm_split
        T.split = split
        T.gemm_tokens_split = gemm_tokens_split
        T.normed_split = normed_split
        T.gather = gather
        T.squared = squared
        T.Squares = Squares
        T.semaphore = semaphore
        T.bd = bd
        T.bdm = bdm
        T.ones = ones
        layer1(T)
        attention2(T)
        rwkv(T)
        t = [pe.now(), act.now(), dve.now(), pool.now()]
        s = semaphore("out")
        sp.dma(out.rearrange("(k p) t -> p k t", p=P), xT, s, 16, t)
        sp.wait((s, 16))
        assert state["at"] == len(pieces)
        emit()


def both(*parts):
    parts = list(parts)
    while parts:
        for q in list(parts):
            if next(q, parts) is parts:
                parts.remove(q)


def layer1(g):
    pe, act, dve, pool, vec, I = g.pe, g.act, g.dve, g.pool, g.vec, g.I
    alloc, alloc3, bank, mm, tr, gemm, take, release = g.alloc, g.alloc3, g.bank, g.mm, g.tr, g.gemm, g.take, g.release
    copy, psum, bank_free, xT, ident, top = g.copy, g.psum, g.bank_free, g.xT, g.ident, g.top

    hs, = g.region(1, 3 * NB * S, NB * S)
    yA, yB, yC = alloc3(NB, S), alloc3(NB, S), alloc3(NB, S)

    def part(parts, k):
        return [p[:, k * S:(k + 1) * S] for p in parts]

    slots, = g.region(2, None, 3 * 1024)
    r = alloc(S)
    t = g.rstd_of(xT, r)
    g.splitting(slots, "w_v", "w_u")
    h_tok = g.normed_split(xT, vec["g_pre_mix"], yB, hs, r, t)
    V = alloc3(QT, D)
    lng, lnb = alloc(D), alloc(D)
    wsT = alloc3(4, P)
    bsB = alloc3(4, P)
    row_sums = alloc(QT * 2)
    st = alloc(QT * 4).rearrange("p (a b) -> p a b", b=4)
    sqs = yA[:, 0:2, :].rearrange("p a b -> p (a b)")
    l_tok = g.load([(lng, I["ln_g"][0, :].partition_broadcast(P)), (lnb, I["ln_b"][0, :].partition_broadcast(P)),
                    (wsT, I["wsT"].rearrange("p (a b) -> p a b", b=P)), (bsB, I["bs"][0, :].partition_broadcast(P).rearrange("p (a b) -> p a b", b=P))])
    w_tok = pool.do(lambda e: e.affine_select(out=wsT, in_=wsT, compare_op=ALU.is_ge, fill=0.0, base=0,
                                              pattern=[[0, 4], [1, P]], channel_multiplier=-1), l_tok)
    g.gemm_tokens_split("w_v", 2, lambda k: part(hs, k), lambda k: h_tok[k], lambda half, qt, ps, t: act.do(
        lambda e: e.activation(V[:, qt, half * 512:half * 512 + 512], ps[:, :], ACT.Gelu_apprx_tanh,
                               accum_out=row_sums[:, 2 * qt + half:2 * qt + half + 1]), t))
    v_tok = act.now()

    def ln(qt):
        a = dve.do(lambda e: e.tensor_tensor(st[:, qt, 0:1], row_sums[:, 2 * qt:2 * qt + 1], row_sums[:, 2 * qt + 1:2 * qt + 2], ALU.add), v_tok)
        a = dve.do(lambda e: e.tensor_scalar(st[:, qt, 0:1], st[:, qt, 0:1], 1.0 / D, None, ALU.mult), a)
        a = dve.do(lambda e: e.tensor_scalar(V[:, qt, :], V[:, qt, :], st[:, qt, 0:1], None, ALU.subtract), a)
        b = act.do(lambda e: e.activation(sqs, V[:, qt, :], ACT.Square, accum_out=st[:, qt, 1:2]), a)
        b = act.do(lambda e: e.activation(st[:, qt, 2:3], st[:, qt, 1:2], ACT.Sqrt, scale=1.0 / D, bias=g.eps[:, 0:1]), b)
        b = dve.do(lambda e: e.reciprocal(st[:, qt, 3:4], st[:, qt, 2:3]), b)
        b = dve.do(lambda e: e.scalar_tensor_tensor(V[:, qt, :], V[:, qt, :], st[:, qt, 3:4], lng, ALU.mult, ALU.mult), b, l_tok)
        return dve.do(lambda e: e.tensor_tensor(V[:, qt, :], V[:, qt, :], lnb, ALU.add), b)

    ln_tok = [ln(qt) for qt in range(QT)]
    uT = alloc3(NB, S)
    g.gemm_split("w_u", NB, NB, lambda k: part(hs, k), lambda k: None,
         lambda nb, ps, t: act.do(lambda e: e.activation(uT[:, nb, :], ps[:, :], ACT.Gelu_apprx_tanh), t))
    u_tok = act.now()
    for fb in range(NB):
        i, ps, free = bank()
        for n in range(QT):
            t = mm(ps[:, n * P:(n + 1) * P], V[:, n, fb * P:(fb + 1) * P], wsT[:, fb // 2, :], True, True, n == QT - 1,
                   free, ln_tok, w_tok)
        a = dve.do(lambda e, fb=fb, ps=ps: e.tensor_tensor(
            yA[:, fb, :].rearrange("p (n t) -> p n t", t=P), ps[:, :].rearrange("p (n t) -> p n t", t=P),
            bsB[:, fb // 2, :].unsqueeze(1).broadcast_to((P, QT, P)), ALU.add), t, u_tok)
        bank_free[i] = a
        dve.do(lambda e, fb=fb: e.tensor_tensor(yA[:, fb, :], yA[:, fb, :], uT[:, fb, :], ALU.mult), a)
    g.barrier()

    g.region(2, 3 * NB * S + QT * S + QT * 48)
    qT = alloc3(NB, S)
    ks, kw = (alloc(8 * S).rearrange("p (h g s) -> p h g s", h=2, g=4) for _ in range(2))
    for q in (ks, kw):
        z_tok = pool.do(lambda e, q=q: e.memset(q[0:64, 1], 0.0))
        z_tok = pool.do(lambda e, q=q: e.memset(q[64:128, 0], 0.0))
    kc2, vc2 = yC[:, 0:4, :], yC[:, 4:8, :]
    VV = alloc3(QT, S)
    gat = alloc3(QT, 48)
    slots, gws = g.region(3, None, 3 * 1024, NB * 48)
    gw, gT = yB[:, 0, 0:NB * 48], yB[:, 1, :]
    gw_tok = g.load([(gw, I["w_gate"][:, :])])
    g.splitting(slots, "w_q", "w_kv", "w_vt")
    g.gemm_split("w_q", NB, NB, lambda k: part(hs, k), lambda k: None,
         lambda nb, ps, t: (act.do(lambda e: e.activation(qT[:, nb, :], ps[:, :], ACT.Copy, scale=0.125), t) if nb % 2 else
                            dve.do(lambda e: e.tensor_scalar(qT[:, nb, :], ps[:, :], 0.125, None, ALU.mult), t)))

    def kv_evac(nb, ps, t):
        eng = act if nb % 2 else dve
        what, half = nb // 2, nb % 2
        for gi in range(2):
            grp = 2 * half + gi
            src = ps[64 * gi:64 * gi + 64, :]
            if what < 2:
                dst = (kc2, vc2)[what]
                t2 = copy(eng, dst[0:64, grp, :], src, t)
                t2 = copy(eng, dst[64:128, grp, 0:S - 1], src[:, 1:S], t)
            else:
                dst = (ks, kw)[what - 2]
                t2 = copy(eng, dst[0:64, 0, grp, :], src, t)
                t2 = copy(eng, dst[64:128, 1, grp, :], src, t)
        return t2

    g.gemm_split("w_kv", 8, NB, lambda k: part(hs, k), lambda k: None, kv_evac)
    g.gemm_tokens_split("w_vt", 1, lambda k: part(hs, k), lambda k: None,
                        lambda n, qt, ps, t: copy(g.turns(qt), VV[:, qt, :], ps[:, :], t))
    gw_tok = g.split(gw, gws[0][:, :], gws[1][:, :], gw_tok)
    i, ps, free = bank()
    for k in range(NB):
        xh, xl = part(hs, k)
        gh, gl_ = (q[:, k * 48:(k + 1) * 48] for q in gws)
        mm(ps[0:48, :], gh, xh, k == 0, False, False, free, gw_tok)
        mm(ps[0:48, :], gh, xl, False, False, False)
        t = mm(ps[0:48, :], gl_, xh, False, k == NB - 1, k == NB - 1)
    bank_free[i] = t = copy(dve, gT[0:48, :], ps[0:48, :], t)
    i, ps, free = bank()
    for qt in range(QT):
        t = tr(ps[:, qt * 48:qt * 48 + 48], gT[0:48, qt * P:(qt + 1) * P], ident[0:48, 0:48], qt == QT - 1, free, t)
    bank_free[i] = act.do(lambda e, ps=ps: e.activation(gat, ps[:, 0:192].rearrange("p (a b) -> p a b", b=48), ACT.Sigmoid), t)
    kv_tok = [act.now(), dve.now()]
    g.barrier()
    g.region(3, None)

    hid = alloc3(4, P)
    peb = alloc(4)
    kc = alloc(4 * NCMP)
    vcS = alloc3(4, 64)
    w2 = alloc(4 * 64).rearrange("p (a b c) -> p a b c", a=2, b=2)
    w2_tok = g.load([(w2, I["w_cmp2"].rearrange("p (a b c) -> p a b c", a=2, b=2))])
    for kind in range(2):
        src = (kc2, vc2)[kind]
        for hb in range(2):
            us = [take(("wk1", "wv1")[kind], P) for _ in range(16)]
            i, ps, free = bank()
            for j in range(16):
                mm(ps[:, 0:124].rearrange("p (a b) -> p a b", b=NCMP), us[j][0], src[:, :, 2 * j:2 * j + 481:16], j == 0,
                   j == 15, False, free, us[j][1], kv_tok)
            pv = vec[("pe_k", "pe_v")[kind]]
            for j in range(16):
                t = mm(ps[:, 128:129], us[j][0], pv[:, j:j + 1], j == 0, j == 15, j == 15)
            release(t)
            c = 2 * kind + hb
            a = act.do(lambda e, ps=ps, c=c: e.activation(peb[:, c:c + 1], ps[:, 128:129], ACT.Copy), t)
            bank_free[i] = act.do(lambda e, ps=ps, c=c: e.activation(hid[:, c, 0:124], ps[:, 0:124], ACT.Gelu_apprx_tanh,
                                                                     bias=peb[:, c:c + 1]), a)
    h2 = act.now()
    i, ps, free = bank()
    for hb in range(2):
        t = mm(ps[0:64, 0:124], w2[:, 0, hb, :], hid[:, hb, 0:124], hb == 0, hb == 1, hb == 1, free, h2, w2_tok)
    copy(dve, kc[0:64, :], ps[0:64, 0:124], t)
    bank_free[i] = copy(dve, kc[64:128, :], ps[0:64, 0:124], t)
    i, ps, free = bank()
    for grp in range(4):
        for hb in range(2):
            t = mm(ps[0:NCMP, grp * 64:grp * 64 + 64], hid[:, 2 + hb, grp * NCMP:(grp + 1) * NCMP], w2[:, 1, hb, :],
                   hb == 0, hb == 1, hb == 1, free)
    bank_free[i] = kc_tok = copy(dve, vcS[0:NCMP, :, :], ps[0:NCMP, 0:256].rearrange("p (a b) -> p a b", b=64), t)

    cneg = alloc(QT * NCMP).rearrange("p (a b) -> p a b", b=NCMP)
    rv = alloc(1)
    Pc = yC[:, 0:4, :].rearrange("p a b -> p (a b)")[:, 0:QT * 16 * NCMP].rearrange("p (q h n) -> p q h n", q=QT, n=NCMP)
    sm = alloc(3 * 8).rearrange("p (a b) -> p a b", b=8)
    cn_tok = g.load([(cneg, I["cneg"].rearrange("p (a b) -> p a b", b=NCMP)), (rv, I["rowvalid"][:, :])])
    g.barrier()
    gv = gat.rearrange("p q (h c) -> p q h c", c=3)
    for qt in range(QT):
        for par in range(2):
            i, ps, free = bank()
            for hh in range(8):
                h = 2 * hh + par
                b0 = 64 * par
                t = mm(ps[:, hh * NCMP:(hh + 1) * NCMP], qT[b0:b0 + 64, hh, qt * P:(qt + 1) * P],
                       kc[b0:b0 + 64, (h // 4) * NCMP:(h // 4 + 1) * NCMP], True, True, hh == 7, free, kc_tok)
            pc = Pc[:, qt, par::2, :]
            a = dve.do(lambda e, ps=ps, qt=qt, pc=pc: e.tensor_tensor(
                pc, ps[:, 0:8 * NCMP].rearrange("p (a b) -> p a b", b=NCMP),
                cneg[:, qt, :].unsqueeze(1).broadcast_to((P, 8, NCMP)), ALU.add), t, cn_tok)
            bank_free[i] = a
            a = dve.do(lambda e, pc=pc: e.tensor_reduce(sm[:, 0, :], pc, AX.X, ALU.max), a)
            a = dve.do(lambda e, pc=pc: e.tensor_tensor(pc, pc, sm[:, 0, :].unsqueeze(2).broadcast_to((P, 8, NCMP)), ALU.subtract), a)
            b = act.do(lambda e, pc=pc: e.activation(pc, pc, ACT.Exp), a)
            a = dve.do(lambda e, pc=pc: e.tensor_reduce(sm[:, 1, :], pc, AX.X, ALU.add), b)
            a = dve.do(lambda e: e.reciprocal(sm[:, 2, :], sm[:, 1, :]), a)
            a = dve.do(lambda e, qt=qt, par=par: e.tensor_tensor(sm[:, 2, :], sm[:, 2, :], gv[:, qt, par::2, 0], ALU.mult), a)
            if qt == 0:
                a = dve.do(lambda e: e.tensor_scalar(sm[:, 2, :], sm[:, 2, :], rv, None, ALU.mult), a)
            pc_tok = dve.do(lambda e, pc=pc: e.tensor_tensor(pc, pc, sm[:, 2, :].unsqueeze(2).broadcast_to((P, 8, NCMP)), ALU.mult), a)

    Pb = [alloc3(QT, S), yC[:, 4:8, :], xT[:, 0:4, :]]
    Pb_free = [None] * 3
    PT = [alloc(S) for _ in range(NPT)]
    PT_free = [None] * NPT
    nm = alloc3(3, 4 * QT)
    n_pt = [0]

    def scores(h, br, buf):
        K = (ks, kw)[br][:, h % 2, h // 4, :]
        tiles = []
        for qt in range(QT):
            n = (qt + 1) * P
            i, ps, free = bank()
            t = mm(ps[:, 0:n], qT[:, h // 2, qt * P:(qt + 1) * P], K[:, 0:n], True, True, True, free)
            tiles.append((qt, n, i, ps, t, nm[:, buf, 4 * qt:4 * qt + 4]))
        maxima = []
        for qt, n, i, ps, t, m in tiles:
            dve.do(lambda e, ps=ps, qt=qt: e.tensor_tensor(ps[:, qt * P:(qt + 1) * P], ps[:, qt * P:(qt + 1) * P],
                                                           g.tri, ALU.add), t)
            dve.wait(dve.now(), Pb_free[buf])
            maxima.append(dve.do(lambda e, ps=ps, n=n, m=m: e.tensor_reduce(m[:, 0:1], ps[:, 0:n], AX.X, ALU.max, negate=True)))
        done = []
        for (qt, n, i, ps, t, m), a in zip(tiles, maxima):
            bank_free[i] = b = act.do(lambda e, ps=ps, n=n, m=m, qt=qt: e.activation(
                Pb[buf][:, qt, 0:n], ps[:, 0:n], ACT.Exp, bias=m[:, 0:1], accum_out=m[:, 1:2]), a)
            done.append(b)
        return done

    def weights(h, br, buf, done):
        m = nm[:, buf, :].rearrange("p (q c) -> p q c", c=4)
        a = dve.do(lambda e: e.reciprocal(m[:, :, 2:3], m[:, :, 1:2]), done)
        a = dve.do(lambda e: e.tensor_tensor(m[:, :, 3:4], m[:, :, 2:3], gv[:, :, h, 1 + br:2 + br], ALU.mult), a)
        out = []
        for qt in range(QT):
            n = (qt + 1) * P
            out.append(dve.do(lambda e, n=n, qt=qt: e.tensor_scalar(Pb[buf][:, qt, 0:n], Pb[buf][:, qt, 0:n], m[:, qt, 3:4], None,
                                                                    ALU.mult), a))
        return out

    def values(h, br, buf, tok, o):
        grp, b0 = h // 4, 64 * (h % 2)
        tiles = []
        for kt in range(QT):
            i, ps, free = bank()
            for qt in range(kt, QT):
                t = tr(ps[:, qt * P:(qt + 1) * P], Pb[buf][:, qt, kt * P:(kt + 1) * P], ident, qt == QT - 1, free, tok)
            j = n_pt[0] % NPT
            n_pt[0] += 1
            bank_free[i] = c = copy(act if kt % 2 else dve, PT[j][:, kt * P:S], ps[:, kt * P:S], t, PT_free[j])
            tiles.append((kt, j, c))
        Pb_free[buf] = t
        for kt, j, c in tiles:
            PT_free[j] = last = mm(o[b0:b0 + 64, kt * P:S], VV[:, kt, br * 256 + grp * 64:br * 256 + grp * 64 + 64],
                                   PT[j][:, kt * P:S], False, kt == QT - 1 and br == 1, True, c)
        return last

    def compressed(h, o, free_o):
        b0 = 64 * (h % 2)
        i, ps, free = bank()
        for qt in range(QT):
            t = tr(ps[0:NCMP, qt * P:(qt + 1) * P], Pc[:, qt, h, :], ident, qt == QT - 1, free, pc_tok)
        j = n_pt[0] % NPT
        n_pt[0] += 1
        bank_free[i] = c = copy(dve, PT[j][0:NCMP, :], ps[0:NCMP, :], t, PT_free[j])
        PT_free[j] = mm(o[b0:b0 + 64, :], vcS[0:NCMP, h // 4, :], PT[j][0:NCMP, :], True, False, True, c, free_o)

    jobs = [(h, br) for h in range(NH) for br in range(2)]
    exps = {n: scores(*jobs[n], n % 3) for n in range(2)}
    ready = {0: weights(*jobs[0], 0, exps[0])}
    o_free = [None, None]
    for n, (h, br) in enumerate(jobs):
        if n + 1 < len(jobs):
            ready[n + 1] = weights(*jobs[n + 1], (n + 1) % 3, exps[n + 1])
        if n + 2 < len(jobs):
            exps[n + 2] = scores(*jobs[n + 2], (n + 2) % 3)
        ob = (h // 2) % 2
        o = psum[6 + ob]
        if br == 0:
            compressed(h, o, o_free[ob] if h % 2 == 0 else None)
        last = values(h, br, n % 3, ready[n], o)
        if h % 2 == 1 and br == 1:
            o_free[ob] = copy(act, yB[:, h // 2, :], o[:, :], last)
    g.barrier()

    slots, = g.region(2, None, 3 * 1024)
    g.splitting(slots, "w_xr", "w_rg")
    xc, ii = alloc3(NB, S), alloc3(NB, S)
    rr, gl = xT, yC
    a2 = [alloc(S) for _ in range(2)]
    bda, bdx = alloc3(NB, P), alloc3(NB, P)
    xs = [alloc(S + 3) for _ in range(2)]
    xs_free = [None, None]
    c8 = alloc(NB)
    z = pool.do(lambda e: e.memset(bda, 0.0))
    z = pool.do(lambda e: e.memset(bdx, 0.0), z)
    for q in xs:
        z = pool.do(lambda e, q=q: e.memset(q[:, 0:3], 0.0))
    pairs = []
    for dst, name in ((bda, "rnn_wa"), (bdx, "rnn_wx")):
        for par in range(2):
            pairs.append((dst[64 * par:64 * par + 64, :, 64 * par:64 * par + 64],
                          I[name][par::2, :, :].rearrange("h i o -> i h o")))
    bd_tok = g.load(pairs, z)
    sp_t = alloc3(6, NB)
    ab, ee, zz, z2, ac, mx = (sp_t[:, j, :] for j in range(6))
    lam = vec["rnn_lam"]
    a = dve.do(lambda e: e.tensor_scalar(ab, lam, -1.0, None, ALU.mult))
    a = dve.do(lambda e: e.tensor_tensor(ab, ab, lam, ALU.min), a)
    m0 = dve.do(lambda e: e.tensor_scalar(mx, lam, -1.0, 0.0, ALU.mult, ALU.max), a)
    b = act.do(lambda e: e.activation(ee, ab, ACT.Exp), a)
    a = dve.do(lambda e: e.tensor_scalar(zz, ee, 2.0, None, ALU.add), b)
    a = dve.do(lambda e: e.reciprocal(zz, zz), a)
    a = dve.do(lambda e: e.tensor_tensor(zz, zz, ee, ALU.mult), a)
    a = dve.do(lambda e: e.tensor_tensor(z2, zz, zz, ALU.mult), a)
    a = dve.do(lambda e: e.tensor_scalar(ac, z2, 1.0 / 15, 1.0 / 13, ALU.mult, ALU.add), a)
    for n in (11, 9, 7, 5, 3, 1):
        a = dve.do(lambda e: e.tensor_tensor(ac, ac, z2, ALU.mult), a)
        a = dve.do(lambda e, n=n: e.tensor_scalar(ac, ac, 1.0 / n, None, ALU.add), a)
    a = dve.do(lambda e: e.tensor_tensor(ac, ac, zz, ALU.mult), a)
    a = dve.do(lambda e: e.scalar_tensor_tensor(ac, ac, 2.0, mx, ALU.mult, ALU.add), a, m0)
    c8_tok = dve.do(lambda e: e.tensor_scalar(c8, ac, -8.0, None, ALU.mult), a)

    cw, cb = vec["conv_w"], vec["conv_b"]
    xc_tok = [None] * NB

    def conv(nb, ps, t):
        q = xs[nb % 2]
        a = act.do(lambda e: e.activation(q[:, 3:S + 3], ps[:, :], ACT.Copy), t, xs_free[nb % 2], z)
        b = dve.do(lambda e: e.tensor_scalar(xc[:, nb, :], q[:, 3:S + 3], cw[:, 24 + nb:25 + nb], cb[:, nb:nb + 1], ALU.mult, ALU.add), a)
        for j in (2, 1, 0):
            b = dve.do(lambda e, j=j: e.scalar_tensor_tensor(xc[:, nb, :], q[:, j:j + S], cw[:, 8 * j + nb:8 * j + nb + 1], xc[:, nb, :],
                                                             ALU.mult, ALU.add), b)
        xs_free[nb % 2] = xc_tok[nb] = b
        return a

    g.gemm_split("w_xr", NB, NB, lambda k: part(hs, k), lambda k: None, conv)
    ri_tok = []
    for nb in range(NB):
        for w, dst, bias in ((bda, rr, "rnn_ba"), (bdx, ii, "rnn_bx")):
            i, ps, free = bank()
            t = mm(ps[:, :], w[:, nb, :], xc[:, nb, :], True, True, True, free, bd_tok, xc_tok[nb])
            bank_free[i] = s = act.do(lambda e, ps=ps, dst=dst, bias=bias, nb=nb: e.activation(
                dst[:, nb, :], ps[:, :], ACT.Sigmoid, bias=vec[bias][:, nb:nb + 1]), t)
        ri_tok.append(s)
    tk = [None] * NB

    def decays(blocks):
        for nb in blocks:
            a = dve.do(lambda e, nb=nb: e.tensor_tensor(xc[:, nb, :], xc[:, nb, :], ii[:, nb, :], ALU.mult), ri_tok[nb])
            b = act.do(lambda e, nb=nb: e.activation(ii[:, nb, :], rr[:, nb, :], ACT.Tanh, scale=c8[:, nb:nb + 1]), a, c8_tok)
            b = act.do(lambda e, nb=nb: e.activation(rr[:, nb, :], rr[:, nb, :], ACT.Exp, scale=c8[:, nb:nb + 1]), b)
            sq = a2[nb % 2]
            a = dve.do(lambda e, nb=nb, sq=sq: e.tensor_tensor(sq, rr[:, nb, :], rr[:, nb, :], ALU.mult), b, tk[nb - 2] if nb > 1 else None)
            tk[nb] = dve.do(lambda e, nb=nb, sq=sq: e.scalar_tensor_tensor(ii[:, nb, :], sq, 1.0, ii[:, nb, :], ALU.add, ALU.mult), a)

    scan_tok = [None] * NB

    def scans():
        for nb in range(NB):
            b = act.do(lambda e, nb=nb: e.activation(ii[:, nb, :], ii[:, nb, :], ACT.Sqrt, scale=-1.0), tk[nb])
            a = dve.do(lambda e, nb=nb: e.tensor_tensor(xc[:, nb, :], xc[:, nb, :], ii[:, nb, :], ALU.mult), b)
            scan_tok[nb] = dve.do(lambda e, nb=nb: e.tensor_tensor_scan(ii[:, nb, :], rr[:, nb, :], xc[:, nb, :], 0.0, ALU.mult, ALU.add), a)

    def gated(nb, ps, t):
        b = act.do(lambda e: e.activation(gl[:, nb, :], ps[:, :], ACT.Gelu_apprx_tanh), t)
        if nb == 1:
            decays(range(4, NB))
        if nb == 4:
            scans()
        for m in (range(5) if nb == 4 else [nb] if nb > 4 else ()):
            dve.do(lambda e, m=m: e.tensor_tensor(yC[:, m, :], gl[:, m, :], ii[:, m, :], ALU.mult), b, scan_tok[m])
        return b

    decays(range(4))
    g.gemm_split("w_rg", NB, NB, lambda k: part(hs, k), lambda k: None, gated)
    g.barrier()

    slots, ys = g.region(2, None, 3 * 1024, NB * S)
    x_tok = g.load([(xT, I["xT"].rearrange("(k p) t -> p k t", p=P))])
    mg = alloc3(NB, S)
    r = alloc(S)
    gt = [alloc(S) for _ in range(2)]
    gt_free = [None, None]
    tt = alloc(S)
    g.splitting(slots, "w_mb0", "w_mb1", "w_mb2", "w_o")

    def split_all(src, parts, *tokens):
        return [g.split(src[:, k, :], *(p[:, k * S:(k + 1) * S] for p in parts), *tokens) for k in range(NB)]

    y_tok = split_all(yA, ys)
    m_tok = [None] * NB
    for c in range(3):
        got = {}

        def gate(n, ps, t):
            q = gt[n % 2]
            got["s"] = act.do(lambda e: e.activation(q, ps[:, :], ACT.Sigmoid), t, gt_free[n % 2])
            return got["s"]

        def add(n, ps, t):
            q = gt[n % 2]
            if c == 0:
                m_tok[n] = a = gt_free[n % 2] = dve.do(lambda e: e.tensor_tensor(mg[:, n, :], ps[:, :], q, ALU.mult), t, got["s"])
                return a
            b = gt_free[n % 2] = dve.do(lambda e: e.tensor_tensor(tt, ps[:, :], q, ALU.mult), t, got["s"], dve.now())
            m_tok[n] = dve.do(lambda e: e.tensor_tensor(mg[:, n, :], mg[:, n, :], tt, ALU.add), b, m_tok[n])
            return b

        used = [None] * NB
        for nb in range(NB):
            g.gemm_split(f"w_mb{c}", 1, NB, lambda k: part(hs, k), lambda k: None, lambda _, ps, t: gate(nb, ps, t))
            g.gemm_split(f"w_mb{c}", 1, NB, lambda k: part(ys, k), lambda k: y_tok[k], lambda _, ps, t: add(nb, ps, t),
                         used if nb == NB - 1 else None)
        src = (yB, yC, mg)[c]
        y_tok = [g.split(src[:, k, :], *part(ys, k), used[k], m_tok[k] if c == 2 else None) for k in range(NB)]
    mo = yA
    top[0] = NB * S + S
    act.wait(dve.now())
    sums = g.Squares()
    g.gemm_split("w_o", NB, NB, lambda k: part(ys, k), lambda k: y_tok[k],
                 g.squared(mo, sums))
    pool.wait(x_tok)
    dve.wait(x_tok)
    t = sums.rstd(r)
    x_tok = g.add_normed(mo, vec["g_post_mix"], r, t)
    g.barrier()

    half = NFF // 2
    slots, hs, prs = g.region(1, None, 3 * 1024, NB * S, half * S)
    fo = alloc3(NB, S)
    r = alloc(S)
    sg = [alloc(S) for _ in range(2)]
    px = [alloc(S) for _ in range(2)]
    used = [None, None]
    sums = g.Squares()
    t = g.rstd_of(xT, r)
    g.splitting(slots, "w_fi0", "w_fo0", "w_fi1", "w_fo1")
    h_tok = g.normed_split(xT, vec["g_pre_ffn"], fo, hs, r, t)
    for j in range(2):
        pr_tok = [None] * half
        free = pe.now()
        first = []

        def gate(n, ps, t):
            nb = n // 2
            q, x = sg[nb % 2], px[nb % 2]
            if n % 2 == 0:
                a = act.do(lambda e: e.activation(q, ps[:, :], ACT.Silu), t, used[nb % 2])
                first[:] = [a]
                return a
            a = dve.do(lambda e: e.tensor_tensor(x, ps[:, :], q, ALU.mult), t, first)
            pr_tok[nb] = used[nb % 2] = g.split(x, *(p[:, nb * S:(nb + 1) * S] for p in prs), a, free)
            return a

        g.gemm_split(f"w_fi{j}", 2 * half, NB, lambda k: [p[:, k * S:(k + 1) * S] for p in hs], lambda k: h_tok[k], gate)
        g.gemm_split(f"w_fo{j}", NB, half, lambda k: [p[:, k * S:(k + 1) * S] for p in prs], lambda k: pr_tok[k],
                     g.gather(fo, j, sums))
    t = sums.rstd(r)
    g.add_normed(fo, vec["g_post_ffn"], r, t)
    g.barrier()


def mlp(g, layer):
    act, dve, pe = g.act, g.dve, g.pe
    half = NMLP // 2
    slots, hs, hids = g.region(1, None, 3 * 1024, NB * S, half * S)
    fo = g.alloc3(NB, S)
    r = g.alloc(S)
    relu = [g.alloc(S) for _ in range(2)]
    square = [g.alloc(S) for _ in range(2)]
    used = [None, None]
    sums = g.Squares()
    t = g.rstd_of(g.xT, r)
    g.splitting(slots, *(f"w_m{a}{layer}{b}" for a in (1, 2) for b in range(2)))
    gain = g.vec["norm_g"]
    h_tok = g.normed_split(g.xT, gain[:, 32 * layer + 16:32 * layer + 24], fo, hs, r, t)
    for j in range(2):
        hid_tok = [None] * half
        free = pe.now()

        def evac(nb, ps, t):
            q, x = relu[nb % 2], square[nb % 2]
            a = act.do(lambda e: e.activation(q, ps[:, :], ACT.Relu), t, used[nb % 2])
            b = dve.do(lambda e: e.tensor_tensor(x, q, q, ALU.mult), a)
            hid_tok[nb] = used[nb % 2] = g.split(x, *(p[:, nb * S:(nb + 1) * S] for p in hids), b, free)
            return a

        g.gemm_split(f"w_m1{layer}{j}", half, NB, lambda k: [p[:, k * S:(k + 1) * S] for p in hs], lambda k: h_tok[k], evac)
        g.gemm_split(f"w_m2{layer}{j}", NB, half, lambda k: [p[:, k * S:(k + 1) * S] for p in hids],
                     lambda k: hid_tok[k], g.gather(fo, j, sums))
    t = sums.rstd(r)
    g.add_normed(fo, gain[:, 32 * layer + 24:32 * layer + 32], r, t)


def attention2(g):
    pe, act, dve, pool, vec, I = g.pe, g.act, g.dve, g.pool, g.vec, g.I
    alloc, alloc3, bank, mm, tr, gemm, take, release = g.alloc, g.alloc3, g.bank, g.mm, g.tr, g.gemm, g.take, g.release
    copy, psum, bank_free, xT, ident, top = g.copy, g.psum, g.bank_free, g.xT, g.ident, g.top
    g.region(1, 2 * NB * S + 12 * S + QT * S + QT * P + 8)
    oT = alloc3(NB, S)
    qT = alloc3(NB, S)
    kT = alloc(8 * S).rearrange("p (h g s) -> p h g s", h=2, g=4)
    kb = alloc(4 * S).rearrange("p (h g s) -> p h g s", h=2, g=2)
    VA = alloc3(QT, S)
    VB = alloc3(QT, P)
    sink = alloc(8)
    slots, hs = g.region(2, None, 3 * 1024, NB * S)
    hT = alloc3(NB, S)
    r = alloc(S)
    oh, tab = alloc(1024), alloc(16)
    bv = alloc(1024)
    ld = g.load([(oh[0:32, :], I["onehot"][:, :]), (tab[0:32, :], I["rel_table"][:, :]),
                 (sink, I["sink"][0, :].partition_broadcast(P))])
    t = g.rstd_of(xT, r)
    g.splitting(slots, "w_a2")
    h_tok = g.normed_split(xT, vec["norm_g"][:, 0:8], hT, hs, r, t)
    pool.wait(pool.now())
    for q in (kT, kb):
        pool.do(lambda e, q=q: e.memset(q[0:64, 1], 0.0))
        pool.do(lambda e, q=q: e.memset(q[64:128, 0], 0.0))

    def evac(nb, ps, t):
        eng = act if nb % 2 else dve
        if nb < 8:
            return (act.do(lambda e: e.activation(qT[:, nb, :], ps[:, :], ACT.Copy, scale=0.125), t) if nb % 2 else
                    dve.do(lambda e: e.tensor_scalar(qT[:, nb, :], ps[:, :], 0.125, None, ALU.mult), t))
        if nb < 12:
            copy(eng, kT[0:64, 0, nb - 8, :], ps[0:64, :], t)
            return copy(eng, kT[64:128, 1, nb - 8, :], ps[64:128, :], t)
        for gi in range(2):
            for c in range(2):
                t2 = copy(eng, kb[64 * c:64 * c + 64, c, gi, :], ps[64 * gi:64 * gi + 64, :], t)
        return t2

    g.gemm_split("w_a2", 13, NB, lambda k: [p[:, k * S:(k + 1) * S] for p in hs], lambda k: h_tok[k], evac)
    for half in range(2):
        i, ps, free = bank()
        t = mm(ps[0:16, :], tab[0:32, :], oh[0:32, half * 512:half * 512 + 512], True, True, True, free, ld)
        bank_free[i] = b_tok = copy(dve, bv[0:16, half * 512:half * 512 + 512], ps[0:16, :], t)
    s_b = g.semaphore("bv")
    pool.dma(I["scratch"][:, :], bv[0:16, :], s_b, 16, b_tok)
    bv_tok = (s_b, 16)

    vbw = [take("w_vb", P) for _ in range(NB)]
    i, ps, free = bank()
    for qt in range(QT):
        for k in range(NB):
            t = mm(ps[:, qt * P:(qt + 1) * P], hT[:, k, qt * P:(qt + 1) * P], vbw[k][0], k == 0, k == NB - 1,
                   k == NB - 1, free, vbw[k][1])
    release(t)
    bank_free[i] = copy(dve, VB, ps[:, :].rearrange("p (a b) -> p a b", b=P), t)
    ws = [take("w_va", 512) for _ in range(NB)]
    for qt in range(QT):
        i, ps, free = bank()
        for k in range(NB):
            t = mm(ps[:, :], hT[:, k, qt * P:(qt + 1) * P], ws[k][0], k == 0, k == NB - 1, k == NB - 1, free, ws[k][1])
        bank_free[i] = copy(g.turns(qt), VA[:, qt, :], ps[:, :], t)
    release(t)
    g.barrier()
    g.region(2, None)

    BT = [alloc(896) for _ in range(3)]
    BT_free = [None] * 3
    bt_sem = [g.semaphore("bt") for _ in range(3)]
    mA, mB = alloc(896), alloc(896)
    mk = g.load([(mA, I["maskA"][:, :]), (mB, I["maskB"][:, :])], bv_tok)
    Pb = [alloc3(QT, S) for _ in range(3)]
    Pb_free = [None] * 3
    PT = [alloc(S) for _ in range(NPT)]
    PT_free = [None] * NPT
    nm = alloc3(3, 8 * QT)
    n_pt = [0]

    def keys(h, qt):
        return (0, S) if h < 8 else (max(0, (qt - 1) * P), min(S, (qt + 2) * P))

    def bias(h):
        b = BT[h % 3]
        sc = I["scratch"]
        src = bass.AP(tensor=sc.tensor, offset=sc.offset + h * 1024, ap=[[1, P], [1, 896]])
        pool.dma(b, src, bt_sem[h % 3], 0, BT_free[h % 3], bv_tok)
        return pool.do(lambda e: e.tensor_tensor(b, b, mA if h < 8 else mB, ALU.add), (bt_sem[h % 3], 16 * (h // 3 + 1)), mk)

    bias_tok = [bias(h) for h in range(2)]

    def scores(h, buf):
        K = kT[:, h % 2, h // 2, :] if h < 8 else kb[:, h % 2, (h - 8) // 4, :]
        m = nm[:, buf, :].rearrange("p (c q) -> p c q", q=QT)
        tiles = []
        for qt in range(QT):
            a0, a1 = keys(h, qt)
            i, ps, free = bank()
            t = mm(ps[:, 0:a1 - a0], qT[:, h // 2, qt * P:(qt + 1) * P], K[:, a0:a1], True, True, True, free)
            n, off, pb = a1 - a0, 384 - qt * P + a0, Pb[buf][:, qt, a0:a1]
            tiles.append((qt, pb))
            bank_free[i] = a = dve.do(lambda e, ps=ps, n=n, off=off, pb=pb: e.tensor_tensor(
                pb, ps[:, 0:n], BT[h % 3][:, 896 - off - n:896 - off][:, ::-1], ALU.add), t, bias_tok[h], Pb_free[buf])
            a = dve.do(lambda e, pb=pb, qt=qt: e.tensor_reduce(m[:, 0, qt:qt + 1], pb, AX.X, ALU.max), a)
            yield
        BT_free[h % 3] = a
        if h >= 8:
            a = dve.do(lambda e: e.tensor_tensor(m[:, 0, :], m[:, 0, :], sink[:, h - 8:h - 7].broadcast_to((P, QT)), ALU.max), a, ld)
        a = dve.do(lambda e: e.tensor_scalar(m[:, 1, :], m[:, 0, :], -1.0, None, ALU.mult), a)
        for qt, pb in tiles:
            b = act.do(lambda e, pb=pb, qt=qt: e.activation(pb, pb, ACT.Exp, bias=m[:, 1, qt:qt + 1], accum_out=m[:, 2, qt:qt + 1]), a)
        if h >= 8:
            b = act.do(lambda e: e.activation(m[:, 3, :], m[:, 1, :], ACT.Exp, bias=sink[:, h - 8:h - 7]), a)
        exps[h] = b

    def weights(h, buf, b):
        m = nm[:, buf, :].rearrange("p (c q) -> p c q", q=QT)
        if h >= 8:
            b = dve.do(lambda e: e.tensor_tensor(m[:, 2, :], m[:, 2, :], m[:, 3, :], ALU.add), b)
        a = dve.do(lambda e: e.reciprocal(m[:, 4, :], m[:, 2, :]), b)
        out = []
        for qt in range(QT):
            pb = Pb[buf][:, qt, slice(*keys(h, qt))]
            out.append(dve.do(lambda e, pb=pb, qt=qt: e.tensor_scalar(pb, pb, m[:, 4, qt:qt + 1], None, ALU.mult), a))
        return out

    def values(h, buf, tok, o, free_o):
        b0 = 64 * (h % 2)
        tiles = []

        def take_tile(kt, j, a0, a1, c):
            V = VA[:, kt, h * 64:h * 64 + 64] if h < 8 else VB[:, kt, (h - 8) // 4 * 64:(h - 8) // 4 * 64 + 64]
            PT_free[j] = last[0] = mm(o[b0:b0 + 64, a0:a1], V, PT[j][:, a0:a1], kt == 0, kt == QT - 1, True, c,
                                      free_o if kt == 0 else None)

        for kt in range(QT):
            qs = [qt for qt in range(QT) if keys(h, qt)[0] <= kt * P < keys(h, qt)[1]]
            a0, a1 = qs[0] * P, (qs[-1] + 1) * P
            i, ps, free = bank()
            for qt in qs:
                t = tr(ps[:, qt * P:(qt + 1) * P], Pb[buf][:, qt, kt * P:(kt + 1) * P], ident, qt == qs[-1], free, tok)
            j = n_pt[0] % NPT
            n_pt[0] += 1
            bank_free[i] = c = copy(act, PT[j][:, a0:a1], ps[:, a0:a1], t, PT_free[j])
            tiles.append((kt, j, a0, a1, c))
            if kt == QT - 1:
                Pb_free[buf] = t
            yield
            if kt > 0:
                take_tile(*tiles[kt - 1])
        take_tile(*tiles[QT - 1])

    exps, last = {}, [None]
    for h in range(2):
        both(scores(h, h % 3))
    ready = {0: weights(0, 0, exps[0])}
    bias_tok.append(bias(2))
    o_free = [None, None]
    for h in range(NH):
        if h + 1 < NH:
            ready[h + 1] = weights(h + 1, (h + 1) % 3, exps[h + 1])
        if h + 3 < NH:
            bias_tok.append(bias(h + 3))
        o = psum[6 + (h // 2) % 2]
        both(scores(h + 2, (h + 2) % 3) if h + 2 < NH else iter(()),
             values(h, h % 3, ready[h], o, o_free[(h // 2) % 2] if h % 2 == 0 else None))
        if h % 2 == 1:
            o_free[(h // 2) % 2] = o_tok = copy(act, oT[:, h // 2, :], o[:, :], last[0])
    g.barrier()
    slots, os_ = g.region(2, None, 3 * 1024, NB * S)
    u, r = alloc3(NB, S), alloc(S)
    sums = g.Squares()
    g.splitting(slots, "w_ao")
    o_tok = [g.split(oT[:, k, :], *(p[:, k * S:(k + 1) * S] for p in os_)) for k in range(NB)]
    g.gemm_split("w_ao", NB, NB, lambda k: [p[:, k * S:(k + 1) * S] for p in os_], lambda k: o_tok[k],
                 g.squared(u, sums))
    t = sums.rstd(r)
    g.add_normed(u, vec["norm_g"][:, 8:16], r, t)
    g.barrier()
    mlp(g, 0)
    g.barrier()


def rwkv(g):
    g.region(1, 3 * NB * S + 6 * S)
    pe, act, dve, pool, vec, I = g.pe, g.act, g.dve, g.pool, g.vec, g.I
    alloc, alloc3, bank, mm, tr, gemm = g.alloc, g.alloc3, g.bank, g.mm, g.tr, g.gemm
    copy, psum, bank_free, xT, ident, top = g.copy, g.psum, g.bank_free, g.xT, g.ident, g.top
    top[0] = g.base
    rT, kT, vT = alloc3(NB, S), alloc3(NB, S), alloc3(NB, S)
    tw, ta, tg = alloc3(2, S), alloc3(2, S), alloc3(2, S)
    for q in (tw, ta):
        pool.do(lambda e, q=q: e.memset(q[0:64, 1, :], 0.0))
        pool.do(lambda e, q=q: e.memset(q[64:128, 0, :], 0.0))
    x_sem = g.semaphore("kept")
    x_tok = pool.dma(I["kept_x"].rearrange("(k p) t -> p k t", p=P), xT, x_sem, 16)
    slots, *mixes = g.region(2, None, 3 * 1024, NB * S, NB * S)
    hT = xT
    r, own = alloc(S), alloc(48)
    raw = [alloc(S) for _ in range(2)]
    raw_free = [None, None]
    mp, mn = vec["mu_prev"], vec["mu_next"]
    a = dve.do(lambda e: e.tensor_tensor(own, mp, mn, ALU.add))
    own_tok = dve.do(lambda e: e.tensor_scalar(own, own, -1.0, 1.0, ALU.mult, ALU.add), a)
    t = g.rstd_of(xT, r)
    g.splitting(slots, "w_rw", "w_ra", "w_rg1", "w_rr", "w_rk", "w_rv")
    dve.wait(x_tok)
    h_tok = g.normed(xT, vec["norm_g"][:, 32:40], hT, r, t)
    used = [[None] * NB, [None] * NB]

    def mixed(c, mix, used):
        out = []
        for k in range(NB):
            m, q = 8 * c + k, raw[k % 2]
            a = act.do(lambda e, k=k, m=m, q=q: e.activation(q, hT[:, k, :], ACT.Copy, scale=own[:, m:m + 1]),
                       h_tok, own_tok, raw_free[k % 2])
            a = dve.do(lambda e, k=k, m=m, q=q: e.scalar_tensor_tensor(q[:, 1:S], hT[:, k, 0:S - 1], mp[:, m:m + 1], q[:, 1:S], ALU.mult, ALU.add), a)
            a = dve.do(lambda e, k=k, m=m, q=q: e.scalar_tensor_tensor(q[:, 0:S - 1], hT[:, k, 1:S], mn[:, m:m + 1], q[:, 0:S - 1], ALU.mult, ALU.add), a)
            raw_free[k % 2] = t = g.split(q, *(p[:, k * S:(k + 1) * S] for p in mix), a, used[k])
            out.append(t)
        return out

    def halves(dst, ps, f, t):
        act.do(lambda e: e.activation(dst[0:64, 0, :], ps[0:64, :], f), t)
        return act.do(lambda e: e.activation(dst[64:128, 1, :], ps[64:128, :], f), t)

    jobs = ((0, "w_rr", NB, lambda nb, ps, t: copy(act, rT[:, nb, :], ps[:, :], t)),
            (1, "w_rw", 1, lambda nb, ps, t: halves(tw, ps, ACT.Tanh, t)),
            (2, "w_rk", NB, lambda nb, ps, t: copy(act, kT[:, nb, :], ps[:, :], t)),
            (4, "w_ra", 1, lambda nb, ps, t: halves(ta, ps, ACT.Copy, t)),
            (3, "w_rv", NB, lambda nb, ps, t: copy(act, vT[:, nb, :], ps[:, :], t)),
            (5, "w_rg1", 2, lambda nb, ps, t: act.do(lambda e: e.activation(tg[:, nb, :], ps[:, :], ACT.Sigmoid), t)))
    following = mixed(0, mixes[0], used[0])
    for j, (c, name, nblocks, evac) in enumerate(jobs):
        m_tok, mix = following, mixes[j % 2]
        if j + 1 < len(jobs):
            following = mixed(jobs[j + 1][0], mixes[(j + 1) % 2], used[(j + 1) % 2])
        used[j % 2] = [None] * NB
        g.gemm_split(name, nblocks, NB, lambda k: [p[:, k * S:(k + 1) * S] for p in mix], lambda k: m_tok[k], evac, used[j % 2])
    g.barrier()
    g.region(2, None)

    lm = alloc(2 * 6 * P).rearrange("p (d l a) -> p d l a", d=2, l=6)
    mM = alloc3(2, P)
    rm = alloc(S)
    w2s = [alloc(4 * P).rearrange("p (a b) -> p a b", a=4) for _ in range(3)]
    omka = alloc(NB)
    ld = g.load([(lm, I["levels"].rearrange("p (d l a) -> p d l a", d=2, l=6)),
                 (mM, I["maskM"].rearrange("p (a b) -> p a b", b=P)), (rm, I["starts"][0, :].partition_broadcast(P))])
    kk, sg, cs, aa, kd, e1, e2, t1, t2 = (alloc(S) for _ in range(9))
    BK, BKs = (alloc(2 * S).rearrange("p (c a t) -> p c a t", a=2, t=CH) for _ in range(2))
    Y, X, LT, MK = (alloc3(NCH, P) for _ in range(4))
    LMs = [alloc3(NCH, P) for _ in range(2)]
    lent = [g.ring_t[:, j * 1024:(j + 1) * 1024].rearrange("p (c t) -> p c t", t=P) for j in range(6)]
    lent += [xT[:, 2 * j:2 * j + 2, :].rearrange("p a b -> p (a b)").rearrange("p (c t) -> p c t", t=P) for j in range(4)]
    A = [q.rearrange("p c (h t) -> p c h t", h=2) for q in lent[0:3]]
    R = lent[3].rearrange("p c (h t) -> p c h t", h=2)
    rhos, wcs, bons = [alloc(S) for _ in range(3)], [alloc(NCH) for _ in range(3)], [alloc(S) for _ in range(4)]
    sets = []
    for j in range(2):
        b = Core()
        b.G1, b.MR, b.XT = lent[4 + j], lent[6 + j], lent[8 + j]
        b.BKn, b.SAV = alloc3(NCH, P), alloc3(NCH, P)
        sets.append(b)
    U, Sb = alloc(P), alloc(P)
    oS, q1, ysum = alloc(S), alloc(S), alloc(S)
    q2 = q1
    vec_k = vec["k_a"]
    for q in (pe, act, dve, pool):
        q.wait(x_tok)
    for q in [Sb, LT, MK, g.ring_t]:
        pool.do(lambda e, q=q: e.memset(q, 0.0))
    for b in sets:
        pool.do(lambda e, b=b: e.memset(b.SAV[0:64], 0.0))
    dve.do(lambda e: e.tensor_scalar(omka, vec_k, -1.0, 1.0, ALU.mult, ALU.add))
    w2_sem = [g.semaphore("w2") for _ in range(3)]
    g.barrier()
    for e in (pe, act, dve, pool):
        e.wait(ld)
    engines = (pe, act, dve, pool)

    def chunks(ap):
        return ap.rearrange("p (c t) -> p c t", t=CH)

    def norm_rows(b):
        a = dve.do(lambda e: e.tensor_scalar(kk, kT[:, b, :], vec["k_k"][:, b:b + 1], None, ALU.mult))
        s = act.do(lambda e: e.activation(t1, kk, ACT.Square), a)
        i, ps, free = bank()
        t = mm(ps[:, :], g.bd, t1, True, True, True, free, s)
        bank_free[i] = s = act.do(lambda e, ps=ps: e.activation(t2, ps[:, :], ACT.Sqrt), t)
        a = dve.do(lambda e: e.tensor_scalar(t2, t2, 1e-12, None, ALU.max), s)
        yield
        for q in range(4):
            cols = slice(q * P, (q + 1) * P)
            r = dve.do(lambda e, cols=cols: e.reciprocal(t2[:, cols], t2[:, cols]), a)
            yield
        kept["kk"] = dve.do(lambda e: e.tensor_tensor(kk, kk, t2, ALU.mult), r)

    done = {}

    def begin(*stages):
        for e in engines:
            e.wait(*(done.get(q) for q in stages))

    def end(stage):
        done[stage] = [e.now() for e in engines]

    def w2_of(b):
        return w2s[b % 3]

    kept = {"w2": None, "kk": None}

    def head(n):
        b, d = n // 2, n % 2
        begin(("head", n - 1), ("advance", n - 3), ("tail", n - 4))
        rho, wc = rhos[n % 3], wcs[n % 3]
        w2 = w2_of(b)
        if d == 0:
            kept["w2"] = pool.dma(w2, I["rk2"].rearrange("p (a n) -> p a n", a=4)[:, :, b * P:(b + 1) * P],
                                  w2_sem[b % 3], 16 * (b // 3 + 1))
            yield from norm_rows(b)
        kk_tok, w2_tok = kept["kk"], kept["w2"]
        yield
        i, ps, free = bank()
        t = mm(ps[:, :], w2[:, 0, :], tw[:, d, :], True, True, True, free, w2_tok)
        bank_free[i] = s1 = act.do(lambda e, ps=ps: e.activation(sg, ps[:, :], ACT.Sigmoid, bias=vec["w0"][:, 8 * d + b:8 * d + b + 1]), t)
        i, ps, free = bank()
        t = mm(ps[:, :], w2[:, 1, :], ta[:, d, :], True, True, True, free)
        bank_free[i] = s2 = act.do(lambda e, ps=ps: e.activation(aa, ps[:, :], ACT.Sigmoid, bias=vec["a0"][:, 8 * d + b:8 * d + b + 1]), t)
        yield
        st = -1 if d else 1
        a = dve.do(lambda e: e.tensor_tensor_scan(cs[:, ::st], rm, sg[:, ::st], 0.0, ALU.mult, ALU.add), s1)
        last = chunks(cs)[:, :, 0:1] if d else chunks(cs)[:, :, CH - 1:CH]
        s3 = act.do(lambda e: e.activation(e1, cs, ACT.Exp, scale=-DECAY), a)
        s4 = act.do(lambda e: e.activation(e2, cs, ACT.Exp, scale=DECAY), a)
        s5 = act.do(lambda e: e.activation(wc.unsqueeze(2), last, ACT.Exp, scale=-DECAY), a)
        a = dve.do(lambda e: e.tensor_tensor(sg, cs, sg, ALU.subtract), a)
        s6 = act.do(lambda e: e.activation(sg, sg, ACT.Exp, scale=-DECAY), a)
        yield
        a = dve.do(lambda e: e.tensor_scalar(kd, aa, vec_k[:, b:b + 1], omka[:, b:b + 1], ALU.mult, ALU.add), s2)
        kd_tok = dve.do(lambda e: e.tensor_tensor(kd, kd, kT[:, b, :], ALU.mult), a)
        yield
        rho_tok = pool.do(lambda e: e.tensor_tensor(rho, rT[:, b, :], e1, ALU.mult), s3)
        for hh in range(2):
            half = slice(64 * hh, 64 * hh + 64)
            dve.do(lambda e, half=half, hh=hh: e.scalar_tensor_tensor(
                A[n % 3][half, :, hh, :], chunks(kk)[half], -1.0, chunks(sg)[half], ALU.mult, ALU.mult), s6, kk_tok)
        yield
        bk_in = pool.do(lambda e: e.tensor_tensor(t1, kk, aa, ALU.mult), s2, kk_tok)
        read = done.get(("products", n - 1))
        assert n == 0 or read
        for hh in range(2):
            half = slice(64 * hh, 64 * hh + 64)
            act.do(lambda e, half=half, hh=hh: e.activation(R[half, :, hh, :], chunks(rho)[half], ACT.Copy), rho_tok, read)
        yield
        a = dve.do(lambda e: e.tensor_tensor(BK[:, :, 0, :], chunks(t1), chunks(e2), ALU.mult), bk_in, s4, read)
        bk = dve.do(lambda e: e.tensor_tensor(BK[:, :, 1, :], chunks(kd), chunks(e2), ALU.mult), kd_tok)
        yield
        pool.do(lambda e: e.tensor_tensor(BKs.rearrange("p c a t -> p c (a t)"), BK.rearrange("p c a t -> p c (a t)"),
                                          wc.unsqueeze(2).broadcast_to((P, NCH, P)), ALU.mult), bk, s5, read)
        c = dve.do(lambda e: e.scalar_tensor_tensor(t2, rT[:, b, :], vec["r_k"][:, b:b + 1], kd, ALU.mult, ALU.mult))
        yield
        i, ps, free = bank()
        t = mm(ps[:, :], g.bd, t2, True, True, True, free, c)
        bank_free[i] = dve.do(lambda e, ps=ps: e.tensor_tensor(bons[n % 4], vT[:, b, :], ps[:, :], ALU.mult), t)
        end(("head", n))

    def middle(n):
        b, d = n // 2, n % 2
        o = sets[n % 2]
        begin(("head", n), ("middle", n - 1), ("advance", n - 2))
        strict, upto = mM[:, d, 0:CH], mM[:, d, CH:P]
        for q in range(4):
            i, ps, free = bank()
            for c in range(2):
                ch = 2 * q + c
                mm(ps[:, c * 256:c * 256 + 128], BK[:, ch, :, :], A[n % 3][:, ch, :, :], True, True, False, free)
                t = mm(ps[:, c * 256 + 128:c * 256 + 256], BK[:, ch, :, :], R[:, ch, :, :], True, True, c == 1)
            prod = ps[:, :].rearrange("p (c k h t) -> p c k h t", c=2, k=2, h=2)
            cs2 = slice(2 * q, 2 * q + 2)
            for hh in range(2):
                half = slice(64 * hh, 64 * hh + 64)
                m_tok = dve.do(lambda e, half=half, prod=prod, hh=hh, cs2=cs2: e.tensor_tensor(
                    LT[half, cs2, half], prod[0:64, :, 0, hh, :], strict[0:64].unsqueeze(1).broadcast_to((64, 2, CH)), ALU.mult), t)
            mk_tok = dve.do(lambda e, prod=prod, cs2=cs2: e.tensor_tensor(
                MK[64:128, cs2, :].rearrange("p c (h t) -> p c h t", h=2), prod[64:128, :, 0, :, :],
                strict[64:128].unsqueeze(1).unsqueeze(1).broadcast_to((64, 2, 2, CH)), ALU.mult), t)
            bank_free[i] = dve.do(lambda e, prod=prod, cs2=cs2: e.tensor_tensor(
                o.MR[:, cs2, :].rearrange("p c (h t) -> p c h t", h=2), prod[:, :, 1, :, :],
                upto.unsqueeze(1).unsqueeze(1).broadcast_to((P, 2, 2, CH)), ALU.mult), t)
            yield
        for q in range(2):
            i, ps, free = bank()
            for c in range(4):
                t = tr(ps[:, c * P:(c + 1) * P], BKs[:, 4 * q + c, :, :], ident, c == 3, free)
            bank_free[i] = copy(act, o.BKn[:, 4 * q:4 * q + 4, :], ps[:, :].rearrange("p (a b) -> p a b", b=P), t)
            yield
        done[("products", n)] = t
        for q in range(2):
            i, ps, free = bank()
            for c in range(4):
                ch = 4 * q + c
                t = tr(ps[0:CH, c * P:(c + 1) * P], vT[:, b, ch * CH:(ch + 1) * CH], ident, c == 3, free)
            bank_free[i] = v_tok = copy(act, o.SAV[64:128, 4 * q:4 * q + 4, :], ps[0:CH, :].rearrange("p (a b) -> p a b", b=P), t)
            yield
        XT = o.XT

        def masked(level, *tokens):
            return pool.do(lambda e: e.tensor_tensor(LMs[level % 2], LT, lm[:, d, level, :].unsqueeze(1).broadcast_to((P, NCH, P)),
                                                     ALU.mult), m_tok, *tokens)

        a = masked(0)
        a = pool.do(lambda e: e.tensor_tensor(XT, LMs[0], ident.unsqueeze(1).broadcast_to((P, NCH, P)), ALU.add), a)
        xts = [a, a]
        y_used = y_read = a
        lts = [masked(1)] + [None] * 5
        for level in range(1, 6):
            lt = lts[level - 1]
            LM = LMs[level % 2]
            if level < 5:
                lts[level] = masked(level + 1, y_used)
            xs, ys = [], []
            for q in range(2):
                i, ps, free = bank()
                for c in range(4):
                    t = tr(ps[:, c * P:(c + 1) * P], XT[:, 4 * q + c, :], ident, c == 3, free, xts[q])
                bank_free[i] = c_tok = copy(act, X[:, 4 * q:4 * q + 4, :], ps[:, :].rearrange("p (a b) -> p a b", b=P), t, y_used)
                xs.append(c_tok)
                yield
            for q in range(2):
                i, ps, free = bank()
                for c in range(4):
                    t = mm(ps[:, c * P:(c + 1) * P], LM[:, 4 * q + c, :], X[:, 4 * q + c, :], True, True, c == 3, free, lt, xs[q])
                y_used = t
                bank_free[i] = c_tok = copy(act, Y[:, 4 * q:4 * q + 4, :], ps[:, :].rearrange("p (a b) -> p a b", b=P), t, y_read)
                ys.append(c_tok)
                yield
            for q in range(2):
                i, ps, free = bank()
                for c in range(4):
                    t = mm(ps[:, c * P:(c + 1) * P], Y[:, 4 * q + c, :], XT[:, 4 * q + c, :], True, True, c == 3, free, ys[q])
                y_read = t
                bank_free[i] = xts[q] = dve.do(lambda e, ps=ps, q=q: e.tensor_tensor(
                    XT[:, 4 * q:4 * q + 4, :], XT[:, 4 * q:4 * q + 4, :],
                    ps[:, :].rearrange("p (a b) -> p a b", b=P), ALU.add), t, xts[q])
                yield
        for q in range(2):
            i, ps, free = bank()
            for c in range(4):
                for hh in range(2):
                    h0 = 64 * hh
                    t = mm(ps[h0:h0 + 64, c * P + h0:c * P + h0 + 64], MK[:, 4 * q + c, h0:h0 + 64], o.SAV[:, 4 * q + c, h0:h0 + 64],
                           True, True, c == 3 and hh == 1, free, v_tok, mk_tok)
            for hh in range(2):
                half = slice(64 * hh, 64 * hh + 64)
                bank_free[i] = copy(act, o.G1[half, 4 * q:4 * q + 4, half],
                                    ps[half, :].rearrange("p (a b) -> p a b", b=P)[:, :, half], t)
            yield
        end(("middle", n))

    def advance(n):
        b, d = n // 2, n % 2
        o = sets[n % 2]
        rho, wc = rhos[n % 3], wcs[n % 3]
        begin(("middle", n), ("head", n), ("tail", n - 2), ("advance", n - 1))
        O = psum[6 + n % 2]
        o_free = bank_free[6 + n % 2]
        sb = u_free = None
        first = True
        for ch in (range(NCH - 1, -1, -1) if d else range(NCH)):
            if first:
                a = dve.do(lambda e, ch=ch: e.tensor_copy(U, o.G1[:, ch, :]), u_free)
            else:
                i, ps, free = bank()
                t = mm(ps[:, 0:P], A[n % 3][:, ch, :, :], Sb, True, True, True, free, sb)
                bank_free[i] = a = dve.do(lambda e, ps=ps, ch=ch: e.tensor_tensor(U, ps[:, 0:P], o.G1[:, ch, :], ALU.add), t, u_free)
            yield
            i, ps, free = bank()
            u_free = t = mm(ps[:, 0:P], o.XT[:, ch, :], U, True, True, True, free, a)
            sv = copy(dve, o.SAV[0:64, ch, 0:64], ps[0:64, 0:64], t)
            bank_free[i] = sv = copy(dve, o.SAV[0:64, ch, 64:128], ps[64:128, 64:128], t)
            yield
            i, ps, free = bank()
            for hh in range(2):
                h0 = 64 * hh
                t = mm(ps[h0:h0 + 64, 0:64], o.BKn[:, ch, h0:h0 + 64], o.SAV[:, ch, h0:h0 + 64], True, True, hh == 1, free, sv)
            o_cols = slice(ch * CH, (ch + 1) * CH)
            if not first:
                mm(O[:, o_cols], Sb, rho[:, o_cols], True, False, False, o_free)
            for hh in range(2):
                h0 = 64 * hh
                o_last = mm(O[h0:h0 + 64, o_cols], o.SAV[:, ch, h0:h0 + 64], o.MR[:, ch, h0:h0 + 64], first, True, hh == 1, o_free)
            sb = []
            for hh in range(2):
                h0 = 64 * hh
                blk = Sb[h0:h0 + 64, h0:h0 + 64]
                if first:
                    a = dve.do(lambda e, ps=ps, h0=h0, blk=blk: e.tensor_copy(blk, ps[h0:h0 + 64, 0:64]), t, u_free)
                else:
                    a = dve.do(lambda e, ps=ps, h0=h0, blk=blk, ch=ch: e.scalar_tensor_tensor(
                        blk, blk, wc[h0:h0 + 64, ch:ch + 1], ps[h0:h0 + 64, 0:64], ALU.mult, ALU.add), t, o_last)
                sb.append(a)
            bank_free[i] = a
            first = False
            yield
        end(("advance", n))

    def tail(n):
        b, d = n // 2, n % 2
        O, w2 = psum[6 + n % 2], w2_of(b)
        begin(("advance", n), ("tail", n - 1), ("head", n))
        a = copy(dve, oS, O[:, :])
        t = mm(O[:, :], g.bdm, oS, True, True, True, a)
        yield
        a = dve.do(lambda e: e.tensor_tensor(oS, oS, O[:, :], ALU.subtract), t)
        s = act.do(lambda e: e.activation(q1, oS, ACT.Square), a)
        yield
        t = mm(O[:, :], g.bdm, q1, True, True, True, s)
        yield
        s = act.do(lambda e: e.activation(q2, O[:, :], ACT.Sqrt, bias=g.eps[:, 1:2]), t)
        yield
        for q in range(4):
            cols = slice(q * P, (q + 1) * P)
            r = dve.do(lambda e, cols=cols: e.reciprocal(q2[:, cols], q2[:, cols]), s)
            yield
        a = dve.do(lambda e: e.tensor_tensor(oS, oS, q2, ALU.mult), r)
        a = dve.do(lambda e: e.tensor_scalar(oS, oS, vec["gn_w"][:, b:b + 1], vec["gn_b"][:, b:b + 1], ALU.mult, ALU.add), a)
        t = mm(O[:, :], w2[:, 2 + d, :], tg[:, d, :], True, True, True, s)
        yield
        a = pool.do(lambda e: e.tensor_tensor(oS, oS, bons[n % 4], ALU.add), a)
        yield
        if d == 0:
            dve.do(lambda e: e.tensor_tensor(ysum, oS, O[:, :], ALU.mult), a, t)
        else:
            a = dve.do(lambda e: e.tensor_tensor(oS, oS, O[:, :], ALU.mult), a, t)
            pool.do(lambda e: e.tensor_tensor(rT[:, b, :], ysum, oS, ALU.add), a)
        end(("tail", n))

    stages = ((advance, 0, 24), (tail, -1, 20), (head, 2, 14), (middle, 1, 36))
    for n in range(-2, 17):
        running = [[stage(n + ahead), 0, steps] for stage, ahead, steps in stages if 0 <= n + ahead < 16]
        for k in range(24):
            for q in running:
                while q[1] * 24 < (k + 1) * q[2]:
                    next(q[0], None)
                    q[1] += 1
        for q in running:
            for _ in q[0]:
                pass
    yT = rT
    g.barrier()
    g.resume()
    g.barrier()
    slots, ys = g.region(2, None, 3 * 1024, NB * S)
    x_tok = g.load([(xT, I["kept_x"].rearrange("(k p) t -> p k t", p=P))])
    u, r = kT, alloc(S)
    sums = g.Squares()
    g.splitting(slots, "w_ro")
    y_tok = [g.split(yT[:, k, :], *(p[:, k * S:(k + 1) * S] for p in ys)) for k in range(NB)]
    g.gemm_split("w_ro", NB, NB, lambda k: [p[:, k * S:(k + 1) * S] for p in ys], lambda k: y_tok[k],
                 g.squared(u, sums))
    t = sums.rstd(r)
    pool.wait(x_tok)
    dve.wait(x_tok)
    g.add_normed(u, vec["norm_g"][:, 40:48], r, t)
    g.barrier()
    mlp(g, 1)


def _fm(w):
    k, n = w.shape
    return np.ascontiguousarray(w.reshape(k // P, P, n // P, P).transpose(1, 2, 0, 3).reshape(P, -1))


def _tm(w):
    k, n = w.shape
    return np.ascontiguousarray(w.reshape(k // P, P, n // 512, 512).transpose(1, 2, 0, 3).reshape(P, -1))


def _vec(v):
    return v.reshape(-1, P).T


def _bucket(rel):
    nb, me = 16, 8
    n = np.abs(rel)
    large = me + (np.log(np.maximum(n, 1) / me) / math.log(1024 / me) * (nb - me)).astype(np.int64)
    return np.where(rel > 0, nb, 0) + np.where(n < me, n, np.minimum(large, nb - 1))


def _constants():
    c = {}
    f = np.float32
    c["ident"] = np.eye(P, dtype=f)
    i = np.arange(P)
    c["tri"] = np.where(i[None, :] <= i[:, None], 0.0, NEG).astype(f)
    c["bd"] = np.kron(np.eye(2), np.ones((64, 64))).astype(f)
    pos = np.arange(S).reshape(QT, P).T[:, :, None]
    end = np.arange(NCMP)[None, None, :] * 16 + 31
    c["cneg"] = np.where(end <= pos, 0.0, NEG).astype(f).reshape(P, -1)
    c["rowvalid"] = (i[:, None] >= 31).astype(f)
    rel = 511 - np.arange(1024)
    c["onehot"] = (_bucket(rel)[None, :] == np.arange(32)[:, None]).astype(f)
    d = 511 - np.arange(896)[None, :] - i[:, None]
    a = np.abs(d)
    count = (a <= 64).astype(int) + ((d % 4 == 0) & (a <= 256)) + (d % 16 == 0)
    c["maskA"] = np.where(count > 0, np.log(np.maximum(count, 1)), NEG).astype(f)
    c["maskB"] = np.where(a <= 128, 0.0, NEG).astype(f)
    s, t = np.arange(CH)[:, None], np.arange(CH)[None, :]
    lv = [(s // n + 1 == t // n) & (s // (2 * n) == t // (2 * n)) for n in (1,) + LEVELS]
    lv = [[np.kron(np.eye(2), m) for m in ms] for ms in (lv, [m.T for m in lv])]
    c["levels"] = np.stack([np.stack(ms, 1) for ms in lv], 1).astype(f).reshape(P, -1)
    fw = np.tile(np.concatenate([s < t, s <= t], 1), (2, 1))
    bw = np.tile(np.concatenate([s > t, s >= t], 1), (2, 1))
    c["maskM"] = np.concatenate([fw, bw], 1).astype(f)
    c["starts"] = (np.arange(S) % CH > 0).astype(f).reshape(1, -1)
    return c


def _layout(x):
    a = {n: np.asarray(v) for n, v in x.items()}
    o = _constants()
    o["xT"] = np.ascontiguousarray(a["x"][0].T)
    w = a["w_in"][0]
    cut = np.cumsum([0, 1024, 1024, 1024, 1536, 48, 1024, 1024, 3072])
    u, v, q, kv, gates, xr, rg, mg = (w[:, cut[j]:cut[j + 1]] for j in range(8))
    o["w_v"], o["w_u"], o["w_q"] = _tm(v), _fm(u), _fm(q)
    o["w_kv"] = _fm(np.concatenate([kv[:, 0:768], kv[:, 1024:1280]], 1))
    o["w_vt"] = _tm(np.concatenate([kv[:, 768:1024], kv[:, 1280:1536]], 1))
    o["w_gate"] = np.ascontiguousarray(gates.reshape(NB, P, 48).transpose(1, 0, 2).reshape(P, -1))
    o["wk1"], o["wv1"] = _fm(a["nsa_wk1"][0]), _fm(a["nsa_wv1"][0])
    o["w_cmp2"] = np.ascontiguousarray(np.concatenate(
        [a[n][0].reshape(2, P, 64).transpose(1, 0, 2).reshape(P, -1) for n in ("nsa_wk2", "nsa_wv2")], 1))
    o["w_xr"], o["w_rg"] = _fm(xr), _fm(rg)
    br = [a[n][0] for n in ("w_br_a", "w_br_b", "w_br_c")]
    for c in range(3):
        parts = [_fm(mg[:, c * D:(c + 1) * D]).reshape(P, NB, 1024), _fm(br[c]).reshape(P, NB, 1024)]
        o[f"w_mb{c}"] = np.ascontiguousarray(np.stack(parts, 2).reshape(P, -1))
    o["w_o"] = _fm(a["w_o"][0])
    fi = a["w_ffn_in"][0]
    fi = _fm(np.stack([fi[:, :DFF].reshape(D, NFF, P), fi[:, DFF:].reshape(D, NFF, P)], 2).reshape(D, -1))
    for j in range(2):
        o[f"w_fi{j}"] = np.ascontiguousarray(fi[:, j * NFF * 1024:(j + 1) * NFF * 1024])
        o[f"w_fo{j}"] = _fm(a["w_ffn_out"][0][j * DFF // 2:(j + 1) * DFF // 2])
    w = a["attn_w_in_2"][0]
    o["w_a2"] = _fm(np.concatenate([w[:, 0:512], w[:, 1536:2048], w[:, 512:1024], w[:, 2048:2176]], 1))
    o["w_vb"] = _fm(w[:, 2176:2304])
    o["w_va"] = _tm(w[:, 1024:1536])
    o["w_ao"] = _fm(a["attn_w_out_2"][0])
    for layer in range(2):
        for j in range(2):
            half = slice(j * MLP // 2, (j + 1) * MLP // 2)
            o[f"w_m1{layer}{j}"] = _fm(a["mlp_w1_2"][layer][:, half])
            o[f"w_m2{layer}{j}"] = _fm(a["mlp_w2_2"][layer][half])
    o["rel_table"] = a["rel_table_2"]
    o["sink"] = a["attn_sink_2"].reshape(1, 8)
    o["w_rw"] = _fm(np.concatenate(list(a["rk_w1_2"][0]), 1))
    o["w_ra"] = _fm(np.concatenate(list(a["rk_a1_2"][0]), 1))
    o["w_rg1"] = _fm(np.concatenate(list(a["rk_g1_2"][0]), 1))
    for n, s in (("w_rr", "rk_w_r_2"), ("w_rk", "rk_w_k_2"), ("w_rv", "rk_w_v_2"), ("w_ro", "rk_w_o_2")):
        o[n] = _fm(a[s][0])
    o["rk2"] = np.ascontiguousarray(np.concatenate(
        [a["rk_w2_2"][0].reshape(P, D), a["rk_a2_2"][0].reshape(P, D), a["rk_g2_2"][0, 0], a["rk_g2_2"][0, 1]], 1))
    o["ln_g"], o["ln_b"] = a["gmlp_ln_g"], a["gmlp_ln_b"]
    o["wsT"] = np.ascontiguousarray(a["gmlp_ws"][0].transpose(2, 0, 1).reshape(P, -1))
    o["bs"] = a["gmlp_bs"].reshape(1, -1)
    o["rnn_wa"], o["rnn_wx"] = a["rnn_wa"][0], a["rnn_wx"][0]
    src = {"g_pre_mix": "g_pre_mix", "g_post_mix": "g_post_mix", "g_pre_ffn": "g_pre_ffn", "g_post_ffn": "g_post_ffn",
           "conv_w": "rnn_conv_w", "conv_b": "rnn_conv_b", "rnn_ba": "rnn_ba", "rnn_bx": "rnn_bx",
           "rnn_lam": "rnn_lam", "pe_k": "nsa_pe_k", "pe_v": "nsa_pe_v", "norm_g": "norm_g_2",
           "mu_prev": "rk_mu_prev_2", "mu_next": "rk_mu_next_2", "k_k": "rk_k_k_2", "k_a": "rk_k_a_2",
           "r_k": "rk_r_k_2", "gn_w": "rk_gn_w_2", "gn_b": "rk_gn_b_2", "w0": "rk_w0_2", "a0": "rk_a0_2"}
    o["vecs"] = np.ascontiguousarray(np.concatenate([_vec(a[src[n]]) for n, _ in VECS], 1))
    return o


def kernel(**inputs):
    import concourse.bacc as bacc
    from concourse.bass_utils import run_bass_kernel_spmd

    nc = bacc.Bacc("TRN2", target_bir_lowering=False, num_devices=1)
    arrays = _layout(inputs)
    I = {n: nc.dram_tensor(f"in_{n}", a.shape, mybir.dt.from_np(a.dtype), kind="ExternalInput").ap()
         for n, a in arrays.items()}
    I["kept_x"] = nc.dram_tensor("kept_x", (D, S), F32, kind="Internal").ap()
    I["scratch"] = nc.dram_tensor("scratch", (16, 1024), F32, kind="Internal").ap()
    out = nc.dram_tensor("out_0", (D, S), F32, kind="ExternalOutput").ap()
    program(nc, I, out)
    r = run_bass_kernel_spmd(nc, [{f"in_{n}": a for n, a in arrays.items()}], core_ids=[0])
    return np.ascontiguousarray(r.results[0]["out_0"].T)[None]
```
